# Optimizing a Trainium2 kernel written in Bass

```python
import math
import jax, jax.numpy as jnp
from jax import lax
import numpy as np

D_MODEL = 1024
BATCH = 1
SEQ = 256
DEPTH = 2

GRID_W = 64
CTX_LEN = 256
HEAD_DIM = 64
N_HEADS_A = 8
N_KV_A = 2
N_HEADS_B = 8
N_HEADS_C = 8
N_KV_C = 2
MIX_WIDTH = HEAD_DIM * (N_HEADS_A + N_HEADS_B + N_HEADS_C)
Q_BLOCK = 128
NB_ROWS = 8
NB_COLS = 16
WINDOW = 128
ROPE_THETA = 10000.0
EPS = 1e-6
IN_SIZES = (
    N_HEADS_A * HEAD_DIM, N_KV_A * HEAD_DIM, N_KV_A * HEAD_DIM,
    N_HEADS_B * HEAD_DIM, N_HEADS_B * HEAD_DIM, N_HEADS_B * HEAD_DIM,
    N_HEADS_C * HEAD_DIM, N_KV_C * HEAD_DIM, N_KV_C * HEAD_DIM,
    MIX_WIDTH,
)
IN_WIDTH = sum(IN_SIZES)


def rmsnorm(x, w):
    xf = x.astype(jnp.float32)
    y = xf * lax.rsqrt(jnp.mean(xf * xf, axis=-1, keepdims=True) + EPS)
    return y.astype(x.dtype) * w

def softmax_f32(s, dtype):
    return jax.nn.softmax(s.astype(jnp.float32), axis=-1).astype(dtype)

def heads(z, h):
    return z.reshape(z.shape[:-1] + (h, HEAD_DIM))

def split_cols(z):
    outs, off = [], 0
    for sz in IN_SIZES:
        outs.append(z[..., off:off + sz])
        off += sz
    return outs

def axial_rope(n, dtype):
    t = jnp.arange(n, dtype=jnp.int32)
    rows = (t // GRID_W).astype(jnp.float32)
    cols = (t % GRID_W).astype(jnp.float32)
    n_freq = HEAD_DIM // 4
    freq = ROPE_THETA ** (-jnp.arange(n_freq, dtype=jnp.float32) / n_freq)
    ang = jnp.concatenate([rows[:, None] * freq, cols[:, None] * freq], axis=-1)
    return jnp.cos(ang).astype(dtype), jnp.sin(ang).astype(dtype)

def apply_rope(x, cos, sin):
    x1, x2 = jnp.split(x, 2, axis=-1)
    c = cos[None, :, None, :]
    s = sin[None, :, None, :]
    return jnp.concatenate([x1 * c - x2 * s, x1 * s + x2 * c], axis=-1)

def global_gqa(q, k, v, qc, kc, vc, cos, sin, qn, kn, need_ctx):
    B, N = q.shape[0], q.shape[1]
    C = qc.shape[1]
    G = N_HEADS_A // N_KV_A
    scale = HEAD_DIM ** -0.5
    q = apply_rope(rmsnorm(heads(q, N_HEADS_A), qn), cos, sin) * scale
    k = apply_rope(rmsnorm(heads(k, N_KV_A), kn), cos, sin)
    v = heads(v, N_KV_A)
    qc = rmsnorm(heads(qc, N_HEADS_A), qn) * scale
    kc = rmsnorm(heads(kc, N_KV_A), kn)
    vc = heads(vc, N_KV_A)
    k_all = jnp.concatenate([k, kc], axis=1)
    v_all = jnp.concatenate([v, vc], axis=1)
    nblk = N // Q_BLOCK
    qb = q.reshape(B, nblk, Q_BLOCK, N_KV_A, G, HEAD_DIM).transpose(1, 0, 2, 3, 4, 5)

    def block(qi):
        s = jnp.einsum('bqhgd,bkhd->bhgqk', qi, k_all)
        p = softmax_f32(s, v_all.dtype)
        return jnp.einsum('bhgqk,bkhd->bqhgd', p, v_all)

    y = lax.map(block, qb).transpose(1, 0, 2, 3, 4, 5).reshape(B, N, N_HEADS_A * HEAD_DIM)
    yc = None
    if need_ctx:
        qcg = qc.reshape(B, C, N_KV_A, G, HEAD_DIM)
        p = softmax_f32(jnp.einsum('bqhgd,bkhd->bhgqk', qcg, kc), vc.dtype)
        yc = jnp.einsum('bhgqk,bkhd->bqhgd', p, vc).reshape(B, C, N_HEADS_A * HEAD_DIM)
    return y, yc

def neighbourhood_attn(q, k, v, qc, kc, vc, rpb, need_ctx):
    B, N = q.shape[0], q.shape[1]
    C = qc.shape[1]
    H = N_HEADS_B
    scale = HEAD_DIM ** -0.5
    rows = N // GRID_W
    kh = min(NB_ROWS, rows)
    kw = NB_COLS
    t = jnp.arange(N, dtype=jnp.int32)
    r = t // GRID_W
    col = t % GRID_W
    rs = jnp.clip(r - kh // 2, 0, rows - kh)
    cs = jnp.clip(col - kw // 2, 0, GRID_W - kw)
    key_r = rs[:, None, None] + jnp.arange(kh, dtype=jnp.int32)[None, :, None]
    key_c = cs[:, None, None] + jnp.arange(kw, dtype=jnp.int32)[None, None, :]
    idx = (key_r * GRID_W + key_c).reshape(N, kh * kw)
    rel = ((key_r - r[:, None, None] + NB_ROWS - 1) * (2 * NB_COLS - 1)
           + (key_c - col[:, None, None] + NB_COLS - 1)).reshape(N, kh * kw)
    rpb_flat = rpb.reshape(H, -1)
    q = heads(q, H) * scale
    k = heads(k, H)
    v = heads(v, H)
    qc = heads(qc, H) * scale
    kc = heads(kc, H)
    vc = heads(vc, H)
    nblk = N // Q_BLOCK
    kn = kh * kw
    xs = (q.reshape(B, nblk, Q_BLOCK, H, HEAD_DIM).transpose(1, 0, 2, 3, 4),
          idx.reshape(nblk, Q_BLOCK, kn), rel.reshape(nblk, Q_BLOCK, kn))

    def block(args):
        qi, ii, ri = args
        kg = jnp.take(k, ii, axis=1)
        vg = jnp.take(v, ii, axis=1)
        s_nb = jnp.einsum('bqhd,bqkhd->bhqk', qi, kg) + jnp.take(rpb_flat, ri, axis=1)[None]
        s_ctx = jnp.einsum('bqhd,bchd->bhqc', qi, kc)
        p = softmax_f32(jnp.concatenate([s_nb, s_ctx], axis=-1), v.dtype)
        return (jnp.einsum('bhqk,bqkhd->bqhd', p[..., :kn], vg)
                + jnp.einsum('bhqc,bchd->bqhd', p[..., kn:], vc))

    y = lax.map(block, xs).transpose(1, 0, 2, 3, 4).reshape(B, N, H * HEAD_DIM)
    yc = None
    if need_ctx:
        p = softmax_f32(jnp.einsum('bqhd,bchd->bhqc', qc, kc), vc.dtype)
        yc = jnp.einsum('bhqc,bchd->bqhd', p, vc).reshape(B, C, H * HEAD_DIM)
    return y, yc

def window_gqa(q, k, v, qc, kc, vc, cos, sin, sink, need_ctx):
    B, N = q.shape[0], q.shape[1]
    C = qc.shape[1]
    G = N_HEADS_C // N_KV_C
    scale = HEAD_DIM ** -0.5
    q = (apply_rope(heads(q, N_HEADS_C), cos, sin) * scale).reshape(B, N, N_KV_C, G, HEAD_DIM)
    k = apply_rope(heads(k, N_KV_C), cos, sin)
    v = heads(v, N_KV_C)
    qc = (heads(qc, N_HEADS_C) * scale).reshape(B, C, N_KV_C, G, HEAD_DIM)
    kc = heads(kc, N_KV_C)
    vc = heads(vc, N_KV_C)
    pad = ((0, 0), (WINDOW, WINDOW), (0, 0), (0, 0))
    kp = jnp.pad(k, pad)
    vp = jnp.pad(v, pad)
    span = Q_BLOCK + 2 * WINDOW
    sink_l = sink.astype(jnp.float32).reshape(N_KV_C, G)
    neg = jnp.finfo(jnp.float32).min
    nblk = N // Q_BLOCK
    qs = q.reshape(B, nblk, Q_BLOCK, N_KV_C, G, HEAD_DIM).transpose(1, 0, 2, 3, 4, 5)

    def block(args):
        i, qi = args
        start = i * Q_BLOCK
        kb = lax.dynamic_slice_in_dim(kp, start, span, axis=1)
        vb = lax.dynamic_slice_in_dim(vp, start, span, axis=1)
        qpos = start + jnp.arange(Q_BLOCK, dtype=jnp.int32)
        kpos = start - WINDOW + jnp.arange(span, dtype=jnp.int32)
        valid = (jnp.abs(qpos[:, None] - kpos[None, :]) <= WINDOW) & (kpos >= 0)[None, :] & (kpos < N)[None, :]
        s = jnp.where(valid, jnp.einsum('bqhgd,bkhd->bhgqk', qi, kb).astype(jnp.float32), neg)
        s_ctx = jnp.einsum('bqhgd,bkhd->bhgqk', qi, kc).astype(jnp.float32)
        s_sink = jnp.broadcast_to(sink_l[None, :, :, None, None], s.shape[:-1] + (1,))
        p = softmax_f32(jnp.concatenate([s, s_ctx, s_sink], axis=-1), v.dtype)
        return (jnp.einsum('bhgqk,bkhd->bqhgd', p[..., :span], vb)
                + jnp.einsum('bhgqk,bkhd->bqhgd', p[..., span:span + C], vc))

    y = lax.map(block, (jnp.arange(nblk, dtype=jnp.int32), qs))
    y = y.transpose(1, 0, 2, 3, 4, 5).reshape(B, N, N_HEADS_C * HEAD_DIM)
    yc = None
    if need_ctx:
        s = jnp.einsum('bqhgd,bkhd->bhgqk', qc, kc).astype(jnp.float32)
        s_sink = jnp.broadcast_to(sink_l[None, :, :, None, None], s.shape[:-1] + (1,))
        p = softmax_f32(jnp.concatenate([s, s_sink], axis=-1), vc.dtype)
        yc = jnp.einsum('bhgqk,bkhd->bqhgd', p[..., :C], vc).reshape(B, C, N_HEADS_C * HEAD_DIM)
    return y, yc

def layer(x, cx, c_silu, cctx_silu, norm_w, ada_w, ada_b, w_in, w_out, qn, kn, rpb, sink, cos, sin, need_ctx):
    mod = c_silu @ ada_w + ada_b
    mod_c = cctx_silu @ ada_w + ada_b
    shift, scale, gate = jnp.split(mod, 3, axis=-1)
    shift_c, scale_c, gate_c = jnp.split(mod_c, 3, axis=-1)
    hx = rmsnorm(x, norm_w) * (1 + scale[:, None, :]) + shift[:, None, :]
    hc = rmsnorm(cx, norm_w) * (1 + scale_c) + shift_c
    px = split_cols(hx @ w_in)
    pc = split_cols(hc @ w_in)
    ya, yca = global_gqa(px[0], px[1], px[2], pc[0], pc[1], pc[2], cos, sin, qn, kn, need_ctx)
    yb, ycb = neighbourhood_attn(px[3], px[4], px[5], pc[3], pc[4], pc[5], rpb, need_ctx)
    yc_, ycc = window_gqa(px[6], px[7], px[8], pc[6], pc[7], pc[8], cos, sin, sink, need_ctx)
    ux = jnp.concatenate([ya, yb, yc_], axis=-1) * jax.nn.silu(px[9])
    x = x + gate[:, None, :] * (ux @ w_out)
    if need_ctx:
        uc = jnp.concatenate([yca, ycb, ycc], axis=-1) * jax.nn.silu(pc[9])
        cx = cx + gate_c * (uc @ w_out)
    return x, cx

def first_inputs(seed: int = 0) -> dict:
    key = jax.random.key(seed)
    ks = jax.random.split(key, 14)
    f32 = jnp.float32
    n_rel = (2 * NB_ROWS - 1, 2 * NB_COLS - 1)
    return {
        "x": jax.random.normal(ks[0], (BATCH, SEQ, D_MODEL), f32),
        "c": jax.random.normal(ks[1], (BATCH, D_MODEL), f32),
        "ctx": jax.random.normal(ks[2], (BATCH, CTX_LEN, D_MODEL), f32),
        "c_ctx": jax.random.normal(ks[3], (D_MODEL,), f32),
        "norm_w": 1.0 + 0.05 * jax.random.normal(ks[4], (DEPTH, D_MODEL), f32),
        "ada_w": jax.random.normal(ks[5], (DEPTH, D_MODEL, 3 * D_MODEL), f32) * D_MODEL ** -0.5,
        "ada_b": 0.02 * jax.random.normal(ks[6], (DEPTH, 3 * D_MODEL), f32),
        "w_in": jax.random.normal(ks[7], (DEPTH, D_MODEL, IN_WIDTH), f32) * D_MODEL ** -0.5,
        "w_out": jax.random.normal(ks[8], (DEPTH, MIX_WIDTH, D_MODEL), f32) * MIX_WIDTH ** -0.5,
        "q_norm_a": 1.0 + 0.05 * jax.random.normal(ks[9], (DEPTH, HEAD_DIM), f32),
        "k_norm_a": 1.0 + 0.05 * jax.random.normal(ks[10], (DEPTH, HEAD_DIM), f32),
        "rpb_b": 0.1 * jax.random.normal(ks[11], (DEPTH, N_HEADS_B) + n_rel, f32),
        "sink_c": 0.5 * jax.random.normal(ks[12], (DEPTH, N_HEADS_C), f32),
        "final_norm_w": 1.0 + 0.05 * jax.random.normal(ks[13], (D_MODEL,), f32),
    }

def first_block(x, c, ctx, c_ctx, norm_w, ada_w, ada_b, w_in, w_out, q_norm_a, k_norm_a, rpb_b, sink_c, final_norm_w):
    n_tok = x.shape[1]
    cos, sin = axial_rope(n_tok, x.dtype)
    c_silu = jax.nn.silu(c)
    cctx_silu = jax.nn.silu(c_ctx)
    cx = ctx
    for l in range(DEPTH):
        x, cx = layer(x, cx, c_silu, cctx_silu, norm_w[l], ada_w[l], ada_b[l], w_in[l], w_out[l],
                      q_norm_a[l], k_norm_a[l], rpb_b[l], sink_c[l], cos, sin, l < DEPTH - 1)
    return rmsnorm(x, final_norm_w)


NSA_HEADS = 8
NSA_KV_GROUPS = 2
NSA_REP = NSA_HEADS // NSA_KV_GROUPS
CMP_LEN = 32
CMP_STRIDE = 16
CMP_HIDDEN = 128
SEL_BLOCK = 64
SEL_TOPK = 16
WINDOW_2 = 512
MOBA_HEADS = 8
MOBA_BLOCK = 256
MOBA_TOPK = 3
D_FF = 2816
NEG = -1e30
TINY = 1e-30
FORCE_BONUS = 1e4
NSA_WIDTH = NSA_HEADS * HEAD_DIM
NSA_KV_WIDTH = NSA_KV_GROUPS * HEAD_DIM
MOBA_WIDTH = MOBA_HEADS * HEAD_DIM
SPLIT_SIZES = (NSA_WIDTH, 3 * NSA_HEADS, NSA_KV_WIDTH, NSA_KV_WIDTH, NSA_KV_WIDTH, NSA_KV_WIDTH, NSA_KV_WIDTH, NSA_KV_WIDTH, MOBA_WIDTH, MOBA_WIDTH, MOBA_WIDTH, D_MODEL, D_MODEL)
IN_COLS = NSA_WIDTH + 3 * NSA_HEADS + 6 * NSA_KV_WIDTH + 3 * MOBA_WIDTH + 2 * D_MODEL


def _rms(x, g):
    xf = x.astype(jnp.float32)
    y = xf * lax.rsqrt(jnp.mean(xf * xf, axis=-1, keepdims=True) + EPS)
    return (y * g.astype(jnp.float32)).astype(x.dtype)

def _swiglu(h, wg, wu, wd):
    return (jax.nn.silu(h @ wg) * (h @ wu)) @ wd

def _rope_tables(pos):
    inv = ROPE_THETA ** (-jnp.arange(0, HEAD_DIM, 2, dtype=jnp.float32) / HEAD_DIM)
    ang = pos.astype(jnp.float32)[:, None] * inv[None, :]
    return jnp.cos(ang), jnp.sin(ang)

def _rope(x, cos, sin):
    x1, x2 = jnp.split(x.astype(jnp.float32), 2, axis=-1)
    return jnp.concatenate([x1 * cos - x2 * sin, x2 * cos + x1 * sin], axis=-1).astype(x.dtype)

def _masked_softmax(s, mask, axis):
    s = jnp.where(mask, s.astype(jnp.float32), NEG)
    m = jnp.max(s, axis=axis, keepdims=True)
    p = jnp.exp(s - m) * mask
    return p / jnp.maximum(jnp.sum(p, axis=axis, keepdims=True), TINY)

def _heads(z, n):
    b, s, _ = z.shape
    return z.reshape(b, s, n, HEAD_DIM).transpose(0, 2, 1, 3)

def _split_cols(z):
    idx = []
    acc = 0
    for w in SPLIT_SIZES[:-1]:
        acc += w
        idx.append(acc)
    return jnp.split(z, idx, axis=-1)

def _chunk_queries(a):
    b = a.shape[0]
    s = a.shape[-2]
    nq = s // Q_BLOCK
    mid = a.shape[1:-2]
    a = a.reshape((b,) + mid + (nq, Q_BLOCK, a.shape[-1]))
    nd = a.ndim
    perm = (0, nd - 3) + tuple(range(1, nd - 3)) + (nd - 2, nd - 1)
    return a.transpose(perm).reshape((b * nq,) + mid + (Q_BLOCK, a.shape[-1]))

def _unchunk_queries(a, b):
    nq = a.shape[0] // b
    mid = a.shape[1:-2]
    a = a.reshape((b, nq) + mid + a.shape[-2:])
    nd = a.ndim
    perm = (0,) + tuple(range(2, nd - 2)) + (1, nd - 2, nd - 1)
    return a.transpose(perm).reshape((b,) + mid + (nq * Q_BLOCK, a.shape[-1]))

def _compress(k, pos_emb, w1, w2):
    b, g, s, d = k.shape
    ch = k.reshape(b, g, s // CMP_STRIDE, CMP_STRIDE, d)
    blocks = jnp.concatenate([ch[:, :, :-1], ch[:, :, 1:]], axis=3) + pos_emb
    flat = blocks.reshape(b, g, blocks.shape[2], CMP_LEN * d)
    return jax.nn.gelu(flat @ w1) @ w2

def _nsa(q, g, kc, vc, ks, vs, kw, vw, ck_pos, ck_w1, ck_w2, cv_pos, cv_w1, cv_w2):
    B, S, _ = q.shape
    G, R, D = NSA_KV_GROUPS, NSA_REP, HEAD_DIM
    scale = HEAD_DIM ** -0.5
    t = jnp.arange(S)
    cos, sin = _rope_tables(t)
    qh = _rope(_heads(q, NSA_HEADS), cos, sin).reshape(B, G, R, S, D)

    kcb = _compress(_heads(kc, G), ck_pos, ck_w1, ck_w2)
    vcb = _compress(_heads(vc, G), cv_pos, cv_w1, cv_w2)
    nc = kcb.shape[2]
    end_pos = jnp.arange(nc) * CMP_STRIDE + (CMP_LEN - 1)
    cc, sc = _rope_tables(end_pos)
    kcb = _rope(kcb, cc, sc)
    s_cmp = jnp.einsum('bgrtd,bgcd->bgrtc', qh, kcb) * scale
    p_cmp = _masked_softmax(s_cmp, end_pos[None, :] <= t[:, None], -1)
    o_cmp = jnp.einsum('bgrtc,bgcd->bgrtd', p_cmp.astype(vcb.dtype), vcb)

    ns = S // SEL_BLOCK
    ci = jnp.arange(nc)[:, None] * CMP_STRIDE
    sj = jnp.arange(ns)[None, :] * SEL_BLOCK
    overlap = ((ci < sj + SEL_BLOCK) & (ci + CMP_LEN > sj)).astype(jnp.float32)
    imp = jnp.einsum('bgrtc,cj->bgtj', p_cmp, overlap)
    tblk = (t // SEL_BLOCK)[:, None]
    jj = jnp.arange(ns)[None, :]
    forced = (jj == 0) | (jj == tblk) | (jj == tblk - 1)
    imp = jnp.where(jj <= tblk, imp + jnp.where(forced, FORCE_BONUS, 0.0), NEG)
    k_sel = min(SEL_TOPK, ns)
    _, sel_idx = lax.top_k(imp, k_sel)

    ksb = _rope(_heads(ks, G), cos, sin).reshape(B, G, ns, SEL_BLOCK, D)
    vsb = _heads(vs, G).reshape(B, G, ns, SEL_BLOCK, D)
    nq = S // Q_BLOCK
    q_ch = _chunk_queries(qh)
    idx_ch = _chunk_queries(sel_idx)
    b_ids = jnp.repeat(jnp.arange(B), nq)
    n_ids = jnp.tile(jnp.arange(nq), B)

    def sel_body(args):
        qc, ic, bi, ni = args
        kg = jax.vmap(lambda kk, ii: kk[ii])(ksb[bi], ic)
        vg = jax.vmap(lambda vv, ii: vv[ii])(vsb[bi], ic)
        s = jnp.einsum('grqd,gqnkd->grqnk', qc, kg) * scale
        tq = ni * Q_BLOCK + jnp.arange(Q_BLOCK)
        kpos = ic[..., None] * SEL_BLOCK + jnp.arange(SEL_BLOCK)
        mask = (kpos <= tq[None, :, None, None])[:, None]
        p = _masked_softmax(s, mask, (-2, -1))
        return jnp.einsum('grqnk,gqnkd->grqd', p.astype(vg.dtype), vg)

    o_sel = _unchunk_queries(lax.map(sel_body, (q_ch, idx_ch, b_ids, n_ids)), B)

    kwh = _rope(_heads(kw, G), cos, sin)
    vwh = _heads(vw, G)
    pad = ((0, 0), (0, 0), (WINDOW_2, 0), (0, 0))
    band = jnp.arange(nq)[:, None] * Q_BLOCK + jnp.arange(WINDOW_2 + Q_BLOCK)[None, :]
    kband = jnp.take(jnp.pad(kwh, pad), band, axis=2)
    vband = jnp.take(jnp.pad(vwh, pad), band, axis=2)
    qb = qh.reshape(B, G, R, nq, Q_BLOCK, D)
    s_win = jnp.einsum('bgrnqd,bgnkd->bgrnqk', qb, kband) * scale
    kpos = (band - WINDOW_2)[:, None, :]
    tq = (jnp.arange(nq)[:, None] * Q_BLOCK + jnp.arange(Q_BLOCK)[None, :])[:, :, None]
    m_win = (kpos >= 0) & (kpos <= tq) & (tq - kpos < WINDOW_2)
    p_win = _masked_softmax(s_win, m_win, -1)
    o_win = jnp.einsum('bgrnqk,bgnkd->bgrnqd', p_win.astype(vband.dtype), vband).reshape(B, G, R, S, D)

    gate = jax.nn.sigmoid(g).reshape(B, S, G, R, 3).transpose(0, 2, 3, 1, 4)
    o = gate[..., 0:1] * o_cmp + gate[..., 1:2] * o_sel + gate[..., 2:3] * o_win
    return o.transpose(0, 3, 1, 2, 4).reshape(B, S, NSA_WIDTH)

def _moba(q, k, v):
    B, S, _ = q.shape
    H, D = MOBA_HEADS, HEAD_DIM
    scale = HEAD_DIM ** -0.5
    t = jnp.arange(S)
    cos, sin = _rope_tables(t)
    qh = _rope(_heads(q, H), cos, sin)
    kh = _rope(_heads(k, H), cos, sin)
    vh = _heads(v, H)
    nb = -(-S // MOBA_BLOCK)
    sp = nb * MOBA_BLOCK
    kp = jnp.pad(kh, ((0, 0), (0, 0), (0, sp - S), (0, 0)))
    vp = jnp.pad(vh, ((0, 0), (0, 0), (0, sp - S), (0, 0)))
    kblk = kp.reshape(B, H, nb, MOBA_BLOCK, D)
    vblk = vp.reshape(B, H, nb, MOBA_BLOCK, D)
    n_top = min(MOBA_TOPK, nb - 1)
    nq = S // Q_BLOCK
    if n_top > 0:
        kmean = jnp.mean(kblk.astype(jnp.float32), axis=3).astype(kh.dtype)
        gsc = jnp.einsum('bhtd,bhjd->bhtj', qh, kmean)
        past = jnp.arange(nb)[None, :] < (t // MOBA_BLOCK)[:, None]
        gsc = jnp.where(past, gsc.astype(jnp.float32), NEG)
        _, gidx = lax.top_k(gsc, n_top)
        idx_ch = _chunk_queries(gidx)
    else:
        idx_ch = jnp.zeros((B * nq, H, Q_BLOCK, 1), jnp.int32)
    q_ch = _chunk_queries(qh)
    b_ids = jnp.repeat(jnp.arange(B), nq)
    n_ids = jnp.tile(jnp.arange(nq), B)

    def body(args):
        qc, ic, bi, ni = args
        tq = ni * Q_BLOCK + jnp.arange(Q_BLOCK)
        c = (ni * Q_BLOCK) // MOBA_BLOCK
        kown = lax.dynamic_slice_in_dim(kp[bi], c * MOBA_BLOCK, MOBA_BLOCK, axis=1)
        vown = lax.dynamic_slice_in_dim(vp[bi], c * MOBA_BLOCK, MOBA_BLOCK, axis=1)
        s_own = jnp.einsum('hqd,hkd->hqk', qc, kown) * scale
        own_pos = c * MOBA_BLOCK + jnp.arange(MOBA_BLOCK)
        m_own = jnp.broadcast_to((own_pos[None, :] <= tq[:, None])[None], s_own.shape)
        if n_top > 0:
            kg = jax.vmap(lambda kk, ii: kk[ii])(kblk[bi], ic)
            vg = jax.vmap(lambda vv, ii: vv[ii])(vblk[bi], ic)
            s_sel = jnp.einsum('hqd,hqnkd->hqnk', qc, kg) * scale
            m_sel = jnp.broadcast_to((ic < c)[..., None], s_sel.shape)
            s_all = jnp.concatenate([s_sel.reshape(H, Q_BLOCK, -1), s_own], axis=-1)
            m_all = jnp.concatenate([m_sel.reshape(H, Q_BLOCK, -1), m_own], axis=-1)
            p = _masked_softmax(s_all, m_all, -1)
            p_sel = p[..., :n_top * MOBA_BLOCK].reshape(H, Q_BLOCK, n_top, MOBA_BLOCK)
            p_own = p[..., n_top * MOBA_BLOCK:]
            return (jnp.einsum('hqnk,hqnkd->hqd', p_sel.astype(vg.dtype), vg)
                    + jnp.einsum('hqk,hkd->hqd', p_own.astype(vown.dtype), vown))
        p_own = _masked_softmax(s_own, m_own, -1)
        return jnp.einsum('hqk,hkd->hqd', p_own.astype(vown.dtype), vown)

    o = _unchunk_queries(lax.map(body, (q_ch, idx_ch, b_ids, n_ids)), B)
    return o.transpose(0, 2, 1, 3).reshape(B, S, MOBA_WIDTH)

def second_inputs(seed: int = 0) -> dict:
    key = jax.random.key(seed)
    ks = jax.random.split(key, 24)

    def w(k, shape, fan_in):
        return jax.random.normal(k, shape, jnp.float32) * (fan_in ** -0.5)

    def gain(k, shape):
        return 1.0 + 0.01 * jax.random.normal(k, shape, jnp.float32)

    L, Dm, F = DEPTH, D_MODEL, D_FF
    return {
        "x": jax.random.normal(ks[0], (BATCH, SEQ, Dm), jnp.float32),
        "ffn1_norm": gain(ks[1], (L, Dm)),
        "ffn1_wg": w(ks[2], (L, Dm, F), Dm),
        "ffn1_wu": w(ks[3], (L, Dm, F), Dm),
        "ffn1_wd": w(ks[4], (L, F, Dm), F),
        "mix_norm": gain(ks[5], (L, Dm)),
        "w_in": w(ks[6], (L, Dm, IN_COLS), Dm),
        "cmpk_pos": 0.1 * jax.random.normal(ks[7], (L, CMP_LEN, HEAD_DIM), jnp.float32),
        "cmpk_w1": w(ks[8], (L, CMP_LEN * HEAD_DIM, CMP_HIDDEN), CMP_LEN * HEAD_DIM),
        "cmpk_w2": w(ks[9], (L, CMP_HIDDEN, HEAD_DIM), CMP_HIDDEN),
        "cmpv_pos": 0.1 * jax.random.normal(ks[10], (L, CMP_LEN, HEAD_DIM), jnp.float32),
        "cmpv_w1": w(ks[11], (L, CMP_LEN * HEAD_DIM, CMP_HIDDEN), CMP_LEN * HEAD_DIM),
        "cmpv_w2": w(ks[12], (L, CMP_HIDDEN, HEAD_DIM), CMP_HIDDEN),
        "w_branch_nsa": w(ks[13], (L, NSA_WIDTH, Dm), NSA_WIDTH),
        "w_branch_moba": w(ks[14], (L, MOBA_WIDTH, Dm), MOBA_WIDTH),
        "w_out": w(ks[15], (L, Dm, Dm), Dm),
        "ffn2_norm": gain(ks[16], (L, Dm)),
        "ffn2_wg": w(ks[17], (L, Dm, F), Dm),
        "ffn2_wu": w(ks[18], (L, Dm, F), Dm),
        "ffn2_wd": w(ks[19], (L, F, Dm), F),
        "final_norm": gain(ks[20], (Dm,)),
    }

def second_block(x, ffn1_norm, ffn1_wg, ffn1_wu, ffn1_wd, mix_norm, w_in, cmpk_pos, cmpk_w1, cmpk_w2, cmpv_pos, cmpv_w1, cmpv_w2, w_branch_nsa, w_branch_moba, w_out, ffn2_norm, ffn2_wg, ffn2_wu, ffn2_wd, final_norm):
    for l in range(DEPTH):
        x = x + 0.5 * _swiglu(_rms(x, ffn1_norm[l]), ffn1_wg[l], ffn1_wu[l], ffn1_wd[l])
        h = _rms(x, mix_norm[l])
        (q_a, g_a, kc, vc, ks_, vs_, kw, vw, q_b, k_b, v_b, gate_a, gate_b) = _split_cols(h @ w_in[l])
        y_a = _nsa(q_a, g_a, kc, vc, ks_, vs_, kw, vw, cmpk_pos[l], cmpk_w1[l], cmpk_w2[l], cmpv_pos[l], cmpv_w1[l], cmpv_w2[l]) @ w_branch_nsa[l]
        y_b = _moba(q_b, k_b, v_b) @ w_branch_moba[l]
        merged = jax.nn.sigmoid(gate_a) * y_a + jax.nn.sigmoid(gate_b) * y_b
        x = x + merged @ w_out[l]
        x = x + 0.5 * _swiglu(_rms(x, ffn2_norm[l]), ffn2_wg[l], ffn2_wu[l], ffn2_wd[l])
    return _rms(x, final_norm)


def setup_inputs(seed=0):
    out = dict(first_inputs(seed))
    for name, value in second_inputs(seed + 1).items():
        if name != "x":
            out[name + "_2"] = value
    return out


def reference(
    x, c, ctx, c_ctx, norm_w, ada_w, ada_b, w_in, w_out, q_norm_a, k_norm_a, rpb_b, sink_c,
    final_norm_w, ffn1_norm_2, ffn1_wg_2, ffn1_wu_2, ffn1_wd_2, mix_norm_2, w_in_2, cmpk_pos_2,
    cmpk_w1_2, cmpk_w2_2, cmpv_pos_2, cmpv_w1_2, cmpv_w2_2, w_branch_nsa_2, w_branch_moba_2,
    w_out_2, ffn2_norm_2, ffn2_wg_2, ffn2_wu_2, ffn2_wd_2, final_norm_2,
):
    x = first_block(
        x, c, ctx, c_ctx, norm_w, ada_w, ada_b, w_in, w_out, q_norm_a, k_norm_a, rpb_b, sink_c,
        final_norm_w,
    )
    return second_block(
        x, ffn1_norm_2, ffn1_wg_2, ffn1_wu_2, ffn1_wd_2, mix_norm_2, w_in_2, cmpk_pos_2,
        cmpk_w1_2, cmpk_w2_2, cmpv_pos_2, cmpv_w1_2, cmpv_w2_2, w_branch_nsa_2, w_branch_moba_2,
        w_out_2, ffn2_norm_2, ffn2_wg_2, ffn2_wu_2, ffn2_wd_2, final_norm_2,
    )


_drawn_inputs = setup_inputs


def setup_inputs(seed=0):
    import zlib

    import numpy as np

    out = dict(_drawn_inputs(seed))
    spreads = {}
    factors = {'q_norm_a': 8.0,
     'k_norm_a': 8.0,
     'rpb_b': 8.0,
     'sink_c': 8.0,
     'ffn1_norm_2': 8.0,
     'mix_norm_2': 8.0,
     'cmpk_pos_2': 8.0,
     'cmpv_pos_2': 12.953,
     'ffn2_norm_2': 8.0,
     'final_norm_2': 31.999}
    for name, (base, spread) in spreads.items():
        noise = np.random.default_rng([zlib.crc32(name.encode()), seed]).standard_normal(out[name].shape)
        drawn = base * np.exp(spread * noise) if base else spread * noise
        out[name] = __import__('jax').numpy.asarray(drawn.astype(out[name].dtype))
    for name, factor in factors.items():
        out[name] = (out[name] * factor).astype(out[name].dtype)
    return out
```

```python
from contextlib import ExitStack
from dataclasses import asdict, dataclass

import numpy as np

import concourse.bass as bass
from concourse import mybir

F32 = mybir.dt.float32
F32R = mybir.dt.float32r
ACT = mybir.ActivationFunctionType
ALU = mybir.AluOpType
AX = mybir.AxisListType

P = 128
D = 1024
KT = D // P
T = 256
TT = T // P
HD = 64
HALF = HD // 2
NH = 8
NPAIR = NH // 2
GRID_W = 64
ROWS = T // GRID_W
NB_ROWS, NB_COLS = 8, 16
LAYERS = 2
FF = 2816
FT = FF // P
NCMP = 16
PAN = 2048
PW = 256
NB = PAN // PW
EPS = 1e-6
TINY = 1e-30
NEG = -1e30

MIX1 = ("A", "B", "C")
QKV_PANELS = {"A": 3, "B": 6, "C": 3}
DOWN_PANELS = FT * D // PW * PW // PAN
DOWN_STEP_ENDS = [(m + 1) * FT for m in range(D // PW)]


@dataclass
class Stage:
    name: str
    layer: int
    panels: int = 0
    steps: int = 0
    ticks: int = 0
    units: int = 0
    groups: int = 0
    pairs: int = 0
    turns: int = 0
    norms: int = 0
    xtiles: int = 0
    merges: int = 0
    cmps: int = 0
    at: dict = None


COUNTED = ("panels", "steps", "ticks", "units", "groups", "pairs", "turns", "norms", "xtiles", "merges", "cmps")


def block1_stages(l):
    ctx = l == 0
    nq = 4 if ctx else 2

    def qkv(m):
        n = QKV_PANELS[m]
        return Stage("qkv" + m, l, panels=n, steps=n, ticks=n)

    def gate(m):
        return Stage("gate" + m, l, panels=2, steps=2, ticks=2)

    def wout(m):
        return Stage("wout" + m, l, panels=2, steps=4, ticks=4)

    def turn(m):
        return Stage("turn" + m, l, turns=nq + (4 if m == "B" else 2))

    def attn(m):
        return Stage("attn" + m, l, units=24 if ctx else 16, groups=12 if ctx else 8, pairs=8 if ctx else 4)

    return [Stage("ada", l, panels=12, steps=12, ticks=12), Stage("norm", l, norms=1, xtiles=8),
            qkv("A"), gate("A"), turn("A"), attn("A"),
            qkv("B"), wout("A"), gate("B"), turn("B"), attn("B"),
            qkv("C"), wout("B"), gate("C"), turn("C"), attn("C"), wout("C")]


def block2_stages():
    down = Stage("down1", 0, panels=DOWN_PANELS, steps=4, ticks=DOWN_PANELS + 3)
    return [Stage("norm1", 0, norms=1, xtiles=8), Stage("up1", 0, panels=FT, steps=FT, ticks=FT), down,
            Stage("norm2", 0, norms=1, xtiles=8),
            Stage("cmp_kv", 0, panels=1, steps=1, ticks=1, turns=2),
            Stage("nsa_g", 0, panels=1, steps=1, ticks=1), Stage("nsa_q", 0, panels=2, steps=2, ticks=2),
            Stage("nsa_kv", 0, panels=2, steps=2, ticks=2), Stage("cmp_w1", 0, panels=2, steps=2, ticks=2),
            Stage("moba_qkv", 0, panels=6, steps=6, ticks=6),
            Stage("turn_nsa", 0, turns=4), Stage("cmp_attn", 0, cmps=1),
            Stage("turn_moba", 0, turns=4),
            Stage("attn", 0, units=24, groups=12, pairs=8),
            Stage("merge", 0, panels=12, steps=12, ticks=12, merges=4),
            Stage("out", 0, panels=4, steps=4, ticks=4),
            Stage("norm3", 0, norms=1, xtiles=8), Stage("up2", 0, panels=FT, steps=FT, ticks=FT),
            Stage("down2", 0, panels=DOWN_PANELS, steps=4, ticks=DOWN_PANELS + 3)]


def plan():
    one = {}
    at = dict.fromkeys(COUNTED, 0)
    for l in range(LAYERS):
        for s in block1_stages(l):
            s.at = dict(at)
            one[s.name, l] = s
            uses = asdict(s)
            for c in COUNTED:
                at[c] += uses[c]
    at["norms"] += 1
    two = {}
    start = dict(at)
    for s in block2_stages():
        s.at = dict(at)
        two[s.name] = s
        uses = asdict(s)
        for c in COUNTED:
            at[c] += uses[c]
    per_layer = {c: at[c] - start[c] for c in COUNTED}
    return one, two, start, per_layer


ONE, TWO, START2, PER_LAYER = plan()


def tick_tables():
    of_panel, of_step = {}, {}
    for s in [*ONE.values(), *TWO.values()]:
        p, q, t = s.at["panels"], s.at["steps"], s.at["ticks"]
        if s.name.startswith("down"):
            ends = sorted({*DOWN_STEP_ENDS, *((i + 1) * NB for i in range(DOWN_PANELS))})
            for i in range(DOWN_PANELS):
                of_panel[p + i] = t + ends.index((i + 1) * NB) + 1
            for i, e in enumerate(DOWN_STEP_ENDS):
                of_step[q + i] = t + ends.index(e) + 1
            assert len(ends) == s.ticks
            continue
        for i in range(s.panels):
            of_panel[p + i] = t + (i + 1) * s.ticks // s.panels
        for i in range(s.steps):
            of_step[q + i] = t + i + 1
    return of_panel, of_step


PANEL_TICK, STEP_TICK = tick_tables()



def k_x(k):
    return k if k < LAYERS else k - 1


def qkv_places(mixer, j):
    if mixer == "B":
        return [((Q1, K1, V1)[j // 2], (j % 2) * PW, 0, PW)]
    return [(Q1, j * PW, 0, PW)] if j < 2 else [(K1, 0, 0, P), (V1, 0, P, P)]


def bcast(ap, axis, n):
    dims = [list(d) for d in ap.ap]
    return bass.AP(ap.tensor, ap.offset, dims[:axis] + [[0, n]] + dims[axis:])


ROPED2 = 2 * LAYERS
X_DONE2 = LAYERS + 1
OUT_DONE = X_DONE2 + 3 * LAYERS + 1
DVE_START2, DVE_LAYER = 352, 92
PANELS = START2["panels"] + LAYERS * PER_LAYER["panels"]
SPARE = 2
assert START2["panels"] % 2 == 0 and PER_LAYER["panels"] % 2 == 0
assert START2["steps"] % 2 == 0 and PER_LAYER["steps"] % 2 == 0

CONST = {}
_at = 0
for _name, _n in (("ident", P), ("ones", P), ("tri_le", P), ("tri_ge", P), ("near", 2 * T),
                  ("cos1", TT * HALF), ("sin1", TT * HALF), ("nsin1", TT * HALF),
                  ("cos2", TT * HALF), ("sin2", TT * HALF), ("nsin2", TT * HALF),
                  ("cosc", HALF), ("sinc", HALF), ("nsinc", HALF),
                  ("cmp_add", TT * NCMP), ("cmp_keep", TT * NCMP), ("head_of", NH), ("sel", 2), ("eps", 1)):
    CONST[_name] = (_at, _at + _n)
    _at += _n
NCONST = _at
SMALL1 = {"norm_w": (0, 8), "ada_b": (8, 32), "qn": (32, 96), "kn": (96, 160), "sink": (160, 168)}
NSMALL1 = 168
SMALL2 = {"n1": (0, 8), "n2": (8, 16), "n3": (16, 24), "pos": (24, 56), "w2k": (56, 120), "w2v": (120, 184)}
NSMALL2 = 184
NSMALLG = 16 + 2 * KT

Q1, K1, V1 = 0, 2048, 4096
Q2, KC2, KS2, VS2, M2 = 0, 1024, 1536, 2048, 2560
PT0 = 0


def program(nc, ctx, xin, smallg, small1, small2, consts, rpb, weights, out):
    def sb(name, cols, dt=F32):
        return ctx.enter_context(nc.sbuf_tensor(name, [P, cols], dt))

    def sem(name):
        return ctx.enter_context(nc.semaphore(name))

    raw = sb("raw_panels", 2 * PAN)
    whi = sb("panels_hi", 2 * PAN, F32R)
    wlo = sb("panels_lo", 2 * PAN, F32R)
    xT = sb("xT", KT * 2 * T)
    NACT = 2048 + FT * T
    ahi = sb("acts_hi", NACT, F32R)
    alo = sb("acts_lo", NACT, F32R)
    tok = sb("token_major", 3 * 2048)
    work = sb("work", 2048)
    qT = sb("qT", 2048)
    kP = sb("kT_padded", 4096)
    gates = sb("gates", 2048)
    bias = sb("near_bias", 2 * 512)
    cst = sb("consts_sb", NCONST)
    sm1 = sb("small1_sb", LAYERS * NSMALL1)
    sm2all = sb("small2_layers", LAYERS * NSMALL2)
    sm2 = sb("small2_sb", NSMALL2)
    smg = sb("smallg_sb", NSMALLG)
    mod = sb("modulation", 48)
    moda = sb("modulation_scale", 16)
    rs = sb("token_scale", T)
    rcol = sb("token_scale_columns", 2)
    warm = sb("table_scratch", 1)
    stats = sb("softmax_stats", 3 * 8)
    hstat = sb("head_stats", 40)
    gT = sb("branch_gates", 48)
    cmpw = sb("cmp_work", 256)
    cstat = sb("cmp_stats", 16)
    pcT = gates[:, 1280:1280 + T]
    vblk = gates[:, 1536:1536 + 4 * P]
    kcp = sb("cmp_keys", 4 * NCMP)
    glu = sb("cmp_hidden", 32 + P)
    kct = sb("cmp_keys_tok", 2 * P)
    banks = [ctx.enter_context(nc.psum_tensor(f"bank{i}", [P, 512], F32)) for i in range(8)]

    def const(name, rows=slice(0, P)):
        a, b = CONST[name]
        return cst[rows, a:b]

    ident, ones, eps = const("ident"), const("ones"), const("eps")

    loaded = [sem(f"panel_loaded{i}") for i in range(2)]
    hi_ready, lo_ready = sem("panel_hi_ready"), sem("panel_lo_ready")
    tick = sem("pe_panel_or_step_done")
    freed = sem("projection_banks_freed")
    inputs_in, consts_in, small2_in, bias_in = sem("inputs_in"), sem("consts_in"), sem("layer_weights_ready"), sem("bias_in")
    pads_zero = sem("pads_zero")
    sq_ready, sq_used = sem("squares_ready"), sem("squares_summed")
    std_ready, tile_ready = sem("std_ready"), sem("tile_ready_to_round")
    rs_ready, rcol_turned, rcol_ready = sem("token_scale_ready"), sem("token_scale_turned"), sem("token_scale_columns_ready")
    table_in, hid_gated = sem("silu_table_loaded"), sem("hidden_gated")
    xhi_ready, x_split = sem("x_hi_ready"), sem("x_split_ready")
    c_silu, c_hi, c_split = sem("c_silu"), sem("c_hi"), sem("c_split_ready")
    mod_cols, mod_ready = sem("mod_columns"), sem("mod_ready")
    hs_sum, hs_std = sem("head_squares_summed"), sem("head_std_ready")
    roped = sem("queries_keys_ready")
    turned, turn_out = sem("turned"), sem("turned_out")
    scores, negmax, exped, normed = sem("scores"), sem("negmax"), sem("exped"), sem("probs_normed")
    probT, probT_out, pv = sem("probs_turned"), sem("probs_turned_out"), sem("values_added")
    omul, uhi, usplit = sem("heads_gated"), sem("u_hi_ready"), sem("u_split_ready")
    biased = sem("near_bias_masked")
    bias_used = sem("near_bias_used")
    silu_ready, hhi_ready, hid_split = sem("silu_ready"), sem("hid_hi"), sem("hidden_split")
    merge_gate = sem("merge_gate_ready")
    merged, mhi_ready, m_split = sem("merged"), sem("merged_hi"), sem("merged_split")
    cm_pe, cm_act, cm_dve = sem("cmp_pe"), sem("cmp_act"), sem("cmp_dve")
    x_done = sem("residual_done")
    dve_chain, act_chain = sem("dve_chain"), sem("act_chain")
    stored = sem("stored")

    L = PER_LAYER
    grows = {
        loaded[0]: (16 * L["panels"] // 2, 16), loaded[1]: (16 * L["panels"] // 2, 16),
        hi_ready: (2 * L["panels"], 4), lo_ready: (2 * L["panels"], 4),
        tick: (L["ticks"], 2), freed: (L["steps"], 2),
        sq_ready: (8 * L["norms"], 0), sq_used: (8 * L["norms"], 0), std_ready: (L["norms"], 0),
        rs_ready: (3, 0), rcol_turned: (1, 0), rcol_ready: (1, 0),
        table_in: (FT, 1), hid_gated: (2 * FT, 2), xhi_ready: (8 * L["norms"], 0), x_split: (8 * L["norms"], 0),
        small2_in: (1, 0), turned: (L["turns"], 0), turn_out: (L["turns"], 0),
        scores: (L["units"], 0), negmax: (L["units"], 0), exped: (L["units"], 0), normed: (L["units"], 0),
        probT: (L["units"], 0), probT_out: (L["units"], 0), pv: (L["groups"], 0),
        omul: (L["pairs"], 0), uhi: (L["pairs"], 0), usplit: (L["pairs"], 0), roped: (3, 0),
        silu_ready: (2 * FT, 2), hhi_ready: (2 * FT, 2), hid_split: (2 * FT, 2),
        merge_gate: (8, 0), merged: (L["merges"], 0), mhi_ready: (L["merges"], 0), m_split: (L["merges"], 0),
        cm_pe: (5, 0), cm_act: (5, 0), cm_dve: (5, 0), x_done: (3, 0), dve_chain: (DVE_LAYER, 0),
    }

    class Place:
        layer = None
        turn = None

    def now(s, n):
        if Place.layer is not None:
            n = n + Place.layer * grows[s][0]
        if Place.turn is not None and grows[s][1]:
            n = n + Place.turn * grows[s][1]
        return n

    class Chain:

        def __init__(self, s):
            self.s, self.n = s, 0

        def next(self):
            self.n += 1
            return now(self.s, self.n)

    def slot_hi(n, a, b):
        return whi[:, (n % 2) * PAN + a:(n % 2) * PAN + b]

    def slot_lo(n, a, b):
        return wlo[:, (n % 2) * PAN + a:(n % 2) * PAN + b]

    def step_banks(s):
        return banks[2 * (s % 2)], banks[2 * (s % 2) + 1]

    def tile4(ap, n):
        return ap.rearrange("p (a b) -> p a b", a=n)

    def x_of(kt, t0=0, t1=T):
        return xT[:, kt * 2 * T + t0:kt * 2 * T + t1]

    XW = {1: 2 * T, 2: T}

    def act_x(part, blk, kt, t0, t1):
        return part[:, kt * XW[blk] + t0:kt * XW[blk] + t1]

    CP = 6144
    U1 = 8 * 2 * T
    H2 = 8 * T

    @dataclass
    class Unit:
        q: object
        keys: list
        segs: list
        masks: list
        blocks: list
        qt: int
        group: int

    @dataclass
    class Group:
        adds: list
        pair: int
        last: bool
        cmp: bool = False
        head: object = None

    def attention_plan(blk, mixer, with_ctx):
        units, groups, pairs = [], [], []
        qv = qT[:, :].rearrange("p (a t) -> p a t", a=4)

        def val(tt, col, width):
            base = V1 + tt * 512 + col
            return tok[:, base:base + HD]

        if blk == 1:
            kv = kP[:, :].rearrange("p (i t) -> p i t", i=8)
            gqa = mixer != "B"
            for h in range(NH):
                idx = 2 * (h // 4) + h % 2 if gqa else h
                vcol = (h // 4 if gqa else h) * HD
                for qt in range(TT):
                    masks = []
                    if mixer == "C":
                        masks = [(P, P, 1, const("tri_le"))] if qt == 0 else [(0, P, 1, const("tri_ge"))]
                    if mixer == "B":
                        masks = [(0, T, 1, ("bias", h, qt))]
                    units.append(Unit(qv[:, h // 2, qt * P:(qt + 1) * P], [(kv[:, idx, :], 0, 512)],
                                      [(0, 512, h if mixer == "C" else None, None)], masks,
                                      [(b * P, b) for b in range(4)], qt, len(groups)))
                groups.append(Group([(h % 2, val(b, vcol, 1), b, 0, b == 0) for b in range(4)], len(pairs), h % 2 == 1, head=h))
                if h % 2:
                    pairs.append((h // 2, 0))
            if with_ctx:
                for p in range(NPAIR):
                    for qt in range(TT):
                        keys, segs, blocks = [], [], []
                        for e in range(2):
                            h = 2 * p + e
                            idx = 2 * (h // 4) + h % 2 if gqa else h
                            keys.append((kv[:, idx, T:2 * T], e * T, T))
                            segs.append((e * T, T, h if mixer == "C" else None, None))
                            blocks += [(e * T + b * P, 2 * e + b) for b in range(2)]
                        units.append(Unit(qv[:, p, T + qt * P:T + (qt + 1) * P], keys, segs, [], blocks, qt, len(groups)))
                    adds = []
                    for e in range(2):
                        h = 2 * p + e
                        vcol = (h // 4 if gqa else h) * HD
                        adds += [(e, val(2 + b, vcol, 1), 2 * e + b, 0, b == 0) for b in range(2)]
                    groups.append(Group(adds, len(pairs), True))
                    pairs.append((p, 1))
            return units, groups, pairs
        kv = kP[:, :].rearrange("p (i t) -> p i t", i=16)

        def causal_adds(e, vals, kind, started):
            return [(e, vals[b], 2 * kind + b, b * P, b == 0 and kind == 0 and not started) for b in range(2)]

        for h in range(NH):
            g = h // 4
            for qt in range(TT):
                w = (qt + 1) * P
                units.append(Unit(qv[:, h // 2, 0 + qt * P:(qt + 1) * P],
                                  [(kv[:, 4 * k + 2 * g + h % 2, 0:w], k * T, w) for k in range(2)],
                                  [(k * T, w, None, (qt, 3 * h + 1 + k)) for k in range(2)],
                                  [(qt * P, P, 2, const("tri_le"))],
                                  [(k * T + b * P, 2 * k + b) for k in range(2) for b in range(qt + 1)], qt, len(groups)))
            adds = []
            for k in range(2):
                vals = [tok[:, VS2 + b * 256 + k * P + g * HD:VS2 + b * 256 + k * P + (g + 1) * HD] for b in range(2)]
                adds += causal_adds(h % 2, vals, k, True)
            groups.append(Group(adds, len(pairs), h % 2 == 1, cmp=h % 2 == 0))
            if h % 2:
                pairs.append((h // 2, 0))
        for p in range(NPAIR):
            for qt in range(TT):
                w = (qt + 1) * P
                units.append(Unit(qv[:, p, T + qt * P:T + (qt + 1) * P],
                                  [(kv[:, 8 + 2 * p + e, 0:w], e * T, w) for e in range(2)],
                                  [(e * T, w, None, None) for e in range(2)],
                                  [(qt * P, P, 2, const("tri_le"))],
                                  [(e * T + b * P, 2 * e + b) for e in range(2) for b in range(qt + 1)], qt, len(groups)))
            adds = []
            for e in range(2):
                c = M2 + 1024 + (2 * p + e) * HD
                vals = [tok[:, c + b * 1536:c + b * 1536 + HD] for b in range(2)]
                adds += [(e, vals[b], 2 * e + b, b * P, b == 0) for b in range(2)]
            groups.append(Group(adds, len(pairs), True))
            pairs.append((p, 1))
        return units, groups, pairs

    def last_unit_of(units, g):
        return max(i for i, u in enumerate(units) if u.group == g)

    def score_bank(u):
        return banks[u % 3]

    def prob_bank(u):
        return banks[3 + u % 2]

    def out_bank(p):
        return banks[5 + p % 2]

    def turn_bank(b):
        return banks[5 + b % 2]

    def probs(u):
        return work[:, (u % 3) * 512:(u % 3) * 512 + 512]

    def probsT(g):
        return tok[:, PT0 + (g % 2) * 1024:PT0 + (g % 2) * 1024 + 1024].rearrange("p (b q) -> p b q", b=4)

    def gated(p):
        return work[:, 1536 + (p % 2) * T:1536 + (p % 2) * T + T]

    def gate_of(blk, pair):
        i, c = pair
        return gates[:, i * 512 + c * T:i * 512 + c * T + T]

    def u_of(part, blk, pair):
        i, c = pair
        if blk == 1:
            return part[:, U1 + i * 512 + c * T:U1 + i * 512 + c * T + T]
        return part[:, H2 + c * 1024 + i * T:H2 + c * 1024 + (i + 1) * T]

    block = ctx.enter_context(nc.Block())

    @block.sync
    def _(sp):
        sp.dma_start(xT[:, :], xin).then_inc(inputs_in, 16)
        for n in range(2):
            sp.dma_start(raw[:, n * PAN:(n + 1) * PAN], weights[n]).then_inc(loaded[n], 16)
        with sp.Fori(1, (PANELS + SPARE) // 2) as i:
            for j in range(2):
                sp.wait_ge(lo_ready, 4 * i + 2 * j - 2)
                sp.dma_start(raw[:, j * PAN:(j + 1) * PAN], weights[2 * i + j]).then_inc(loaded[j], 16)
        sp.wait_ge(x_done, OUT_DONE)
        sp.dma_start(out.rearrange("(k p) t -> p k t", p=P),
                     xT[:, :].rearrange("p (k t) -> p k t", k=KT)[:, :, 0:T]).then_inc(stored, 16)
        sp.wait_ge(stored, 16)

    @block.gpsimd
    def _(pool):
        pool.dma_start(cst[:, :], consts).then_inc(consts_in, 16)
        pool.dma_start(smg[:, :], smallg).then_inc(consts_in, 16)
        pool.dma_start(sm1[:, :], small1).then_inc(consts_in, 16)
        pool.dma_start(sm2all[:, :], small2).then_inc(consts_in, 16)
        pool.memset(kP[:, :], 0.0).then_inc(pads_zero, 1)
        pool.memset(kct[:, :], 0.0)
        pool.memset(kcp[:, :], 0.0).then_inc(pads_zero, 1)
        pool.wait_ge(consts_in, 64)
        for l in range(LAYERS):
            for h in range(NH):
                n = l * NH + h
                if n >= 2:
                    pool.wait_ge(bias_used, 2 * (n - 1))
                buf = bias[:, (n % 2) * 512:(n % 2) * 512 + 512]
                pool.dma_start(buf, rpb[n]).then_inc(bias_in, 16)
                pool.wait_ge(bias_in, 16 * (n + 1))
                pool.tensor_tensor(buf, buf, const("near"), ALU.add).then_inc(biased, 1)
        pool.wait_ge(x_done, LAYERS)
        kv = kP[:, :].rearrange("p (i t) -> p i t", i=16)
        pool.memset(kv[HD:P, 0:16:2, :], 0.0).then_inc(pads_zero, 1)
        pool.memset(kv[0:HD, 1:16:2, :], 0.0).then_inc(pads_zero, 1)

    @block.scalar
    def _(act):
        chain = Chain(act_chain)
        Place.layer = Place.turn = None

        def round_half(n, h):
            if h == 0:
                act.wait_ge(loaded[n % 2], now(loaded[n % 2], 16 * (n // 2 + 1)))
                if n >= 2:
                    act.wait_ge(tick, now(tick, PANEL_TICK[n - 2]))
            a, b = h * PAN // 2, (h + 1) * PAN // 2
            act.activation(slot_hi(n, a, b), raw[:, (n % 2) * PAN + a:(n % 2) * PAN + b], ACT.Copy).then_inc(hi_ready, 1)

        def round_panel(n):
            round_half(n, 0)
            round_half(n, 1)

        def begin(s):
            act.wait_ge(tick, now(tick, STEP_TICK[s]))
            if s >= 1:
                act.wait_ge(freed, now(freed, s))

        def norm(k, blk, modulate, x_ready=None):
            w = XW[blk]
            if x_ready:
                act.wait_ge(x_done, now(x_done, x_ready))
            for kt in range(KT):
                if kt >= 2:
                    act.wait_ge(sq_used, now(sq_used, 8 * k + kt - 1))
                act.activation(work[:, (kt % 2) * 512:(kt % 2) * 512 + w], x_of(kt, 0, w),
                               ACT.Square).then_inc(sq_ready, 1)
            act.wait_ge(sq_used, now(sq_used, 8 * k + 8))
            act.activation(work[:, 1024:1024 + w], banks[7][:, 0:w], ACT.Sqrt, bias=eps).then_inc(std_ready, 1)
            if modulate is None:
                return
            for kt in range(KT):
                buf = work[:, (kt % 2) * 512:(kt % 2) * 512 + w]
                act.wait_ge(tile_ready, now(tile_ready, 8 * k_x(k) + kt + 1))
                if modulate and kt == 0:
                    act.wait_ge(mod_ready, modulate)
                if modulate:
                    for c in range(2):
                        m = act.activation(buf[:, c * T:(c + 1) * T], buf[:, c * T:(c + 1) * T], ACT.Identity,
                                           scale=moda[:, kt * 2 + c:kt * 2 + c + 1], bias=mod[:, kt * 2 + c:kt * 2 + c + 1])
                    m.then_inc(act_chain, 1)
                    act.wait_ge(act_chain, chain.next())
                act.activation(act_x(ahi, blk, kt, 0, w), buf, ACT.Copy).then_inc(xhi_ready, 1)

        def norm_hi(weight, tiles):
            for kt in tiles:
                act.activation(act_x(ahi, 2, kt, 0, T), x_of(kt), ACT.Identity,
                               scale=weight[:, kt:kt + 1]).then_inc(xhi_ready, 1)

        def norm_root(k):
            act.wait_ge(sq_used, now(sq_used, 8 * k + 8))
            act.activation(rs[:, :], banks[7][:, 0:T], ACT.Sqrt, bias=eps).then_inc(std_ready, 1)

        def attention(blk, mixer, with_ctx, st):
            units, groups, pairs = attention_plan(blk, mixer, with_ctx)
            u0, g0, p0 = st.at["units"], st.at["groups"], st.at["pairs"]
            for i in range(len(units) + 6):
                if i < len(units):
                    un, u = units[i], u0 + i
                    act.wait_ge(negmax, now(negmax, u + 1))
                    if u - 2 >= 1:
                        act.wait_ge(probT, now(probT, u - 2))
                    sbase = (u % 3) * 8
                    for k, (c, w, sink, _) in enumerate(un.segs):
                        if sink is not None:
                            a = SMALL1["sink"][0] + st.layer * NSMALL1 + sink
                            act.activation(stats[:, sbase + 6 + k:sbase + 7 + k], sm1[:, a:a + 1], ACT.Exp,
                                           bias=stats[:, sbase + k:sbase + k + 1])
                        e = act.activation(probs(u)[:, c:c + w], score_bank(u)[:, c:c + w], ACT.Exp,
                                           bias=stats[:, sbase + k:sbase + k + 1],
                                           accum_out=stats[:, sbase + 2 + k:sbase + 3 + k])
                        if k == len(un.segs) - 1:
                            e.then_inc(exped, 1)
                j = i - 2
                if 0 <= j < len(units):
                    un, u = units[j], u0 + j
                    act.wait_ge(probT, now(probT, u + 1))
                    if g0 + un.group - 1 >= 1:
                        act.wait_ge(pv, now(pv, g0 + un.group - 1))
                    w = len(un.blocks) * P
                    dst = probsT(g0 + un.group)[:, :, un.qt * P:(un.qt + 1) * P]
                    src = prob_bank(u)[:, :].rearrange("p (b q) -> p b q", b=4)
                    if len(un.blocks) < 4:
                        dst, src = dst[:, 0:4:2, :], src[:, 0:4:2, :]
                    act.activation(dst, src, ACT.Copy).then_inc(probT_out, 1)
                j = i - 5
                if 0 <= j < len(units) and last_unit_of(units, units[j].group) == j and groups[units[j].group].last:
                    pr = groups[units[j].group].pair
                    act.wait_ge(omul, now(omul, p0 + pr + 1))
                    act.activation(u_of(ahi, blk, pairs[pr]), gated(p0 + pr), ACT.Copy).then_inc(uhi, 1)

        def turns(st, b, top, bottom, scale=1.0):
            act.wait_ge(turned, now(turned, b + 1))
            for k, (dst, src) in enumerate([x for x in (top, bottom) if x is not None]):
                m = act.activation(dst, src, ACT.Copy, scale=scale)
            m.then_inc(turn_out, 1)

        act.wait_ge(inputs_in, 16)
        act.wait_ge(consts_in, 64)
        round_panel(0)
        cc = smg[:, 16:16 + 2 * KT]
        cs = cmpw[:, 0:2 * KT]
        act.activation(cs, cc, ACT.Silu).then_inc(act_chain, 1)
        act.wait_ge(act_chain, chain.next())
        cpad = ahi[:, CP:CP + KT * P].rearrange("p (k m) -> p k m", k=KT)
        act.wait_ge(c_split, 1)
        act.activation(cpad[:, :, 0:2], tile4(cs, KT), ACT.Copy).then_inc(c_hi, 1)
        round_panel(1)

        for l in range(LAYERS):
            wctx = l == 0
            nq = 4 if wctx else 2
            st = ONE["ada", l]
            for j in range(12):
                n, s = st.at["panels"] + j, st.at["steps"] + j
                round_panel(n + 2)
                begin(s)
                act.activation(tok[0:4, j * PW:(j + 1) * PW], step_banks(s)[0][0:4, 0:PW], ACT.Copy).then_inc(freed, 1)
            st = ONE["norm", l]
            norm(st.at["norms"], 1, l + 1, l)
            for m in MIX1:
                def qkv(m):
                    st = ONE["qkv" + m, l]
                    for j in range(st.panels):
                        n, s = st.at["panels"] + j, st.at["steps"] + j
                        round_panel(n + 2)
                        begin(s)
                        kinds = qkv_places(m, j)
                        full = kinds[0][0] != Q1 or wctx
                        for c in range(2 if full else 1):
                            bk = step_banks(s)[c][:, :].rearrange("p (t w) -> p t w", t=2)
                            for a, w, (sec, col) in [(x[2], x[3], (x[0], x[1])) for x in kinds]:
                                dst = tok[:, sec:sec + 2048].rearrange("p (t w) -> p t w", t=4)[:, 2 * c:2 * c + 2, col:col + w]
                                e = act.activation(dst, bk[:, :, a:a + w], ACT.Copy)
                        e.then_inc(freed, 1)

                def wout(m):
                    st = ONE["wout" + m, l]
                    for j in range(2):
                        round_panel(st.at["panels"] + j + 2)

                def gate(m):
                    st = ONE["gate" + m, l]
                    for j in range(2):
                        n, s = st.at["panels"] + j, st.at["steps"] + j
                        round_panel(n + 2)
                        begin(s)
                        w = 2 * T if wctx else T
                        for c in range(2):
                            i = 2 * j + c
                            e = act.activation(gates[:, i * 512:i * 512 + w], step_banks(s)[c][:, 0:w], ACT.Silu)
                        e.then_inc(freed, 1)

                if m == "A":
                    qkv("A")
                gate(m)
                if m == "A":
                    act.wait_ge(hs_sum, l + 1)
                    w = 10 * 4
                    act.activation(hstat[:, 0:w], hstat[:, 0:w], ACT.Sqrt, scale=1.0 / HD, bias=eps).then_inc(hs_std, 1)
                st = ONE["turn" + m, l]
                b = st.at["turns"]
                qv = qT[:, :].rearrange("p (a t) -> p a t", a=4)
                kv = kP[:, :].rearrange("p (i t) -> p i t", i=8)
                for tt in range(nq):
                    turns(st, b, (qv[:, :, tt * P:(tt + 1) * P], tile4(turn_bank(b)[:, :], 4)), None, HD ** -0.5)
                    b += 1
                if m == "B":
                    for tt in range(4):
                        src = tile4(turn_bank(b)[:, :], 4)
                        turns(st, b, (kv[0:HD, 0:8:2, tt * P:(tt + 1) * P], src[0:HD]),
                              (kv[HD:P, 1:8:2, tt * P:(tt + 1) * P], src[HD:P]))
                        b += 1
                else:
                    for c in range(2):
                        src = turn_bank(b)[:, :].rearrange("p (g t) -> p g t", g=2)
                        turns(st, b, (kv[0:HD, 0:4:2, 2 * c * P:2 * (c + 1) * P], src[0:HD]),
                              (kv[HD:P, 1:4:2, 2 * c * P:2 * (c + 1) * P], src[HD:P]))
                        b += 1
                attention(1, m, wctx, ONE["attn" + m, l])
                if m == "A":
                    qkv("B")
                    wout("A")
                if m == "B":
                    qkv("C")
                    wout("B")
                if m == "C":
                    wout("C")

        norm(START2["norms"] - 1, 2, None, LAYERS)

        with act.Fori(0, LAYERS) as layer:
            Place.layer = layer
            def small(name):
                a, b = SMALL2[name]
                return sm2[:, a:b]

            def up(st, first_hidden):
                s0, n0 = st.at["steps"], st.at["panels"]
                with act.Fori(0, FT // 2) as turn:
                    Place.turn = turn
                    act.activation(warm[:, :], eps, ACT.Silu).then_inc(table_in, 1)
                    act.wait_ge(table_in, now(table_in, first_hidden // 2 + 1))
                    for j in range(2):
                        n, s, a = n0 + j, s0 + j, first_hidden + j
                        gu = work[:, (j % 2) * 512:(j % 2) * 512 + 512]
                        round_half(n + 2, 0)
                        act.wait_ge(freed, now(freed, s + 1))
                        act.activation(gu[:, 0:T], gu[:, 0:T], ACT.Silu).then_inc(silu_ready, 1)
                        round_half(n + 2, 1)
                        act.wait_ge(hid_gated, now(hid_gated, a + 1))
                        dst = ahi[:, H2:H2 + FT * T].rearrange("p (f t) -> p f t", f=FT)[:, 2 * turn + j, :]
                        act.activation(dst, gu[:, T:2 * T], ACT.Copy).then_inc(hhi_ready, 1)
                    Place.turn = None

            def down(st, next_weight=None):
                for n in range(DOWN_PANELS):
                    round_panel(st.at["panels"] + n + 2)
                    for j, e in enumerate(DOWN_STEP_ENDS):
                        if next_weight is not None and (e - 1) // NB == n:
                            act.wait_ge(freed, now(freed, st.at["steps"] + j + 1))
                            norm_hi(next_weight, (2 * j, 2 * j + 1))

            act.wait_ge(x_done, now(x_done, X_DONE2))
            act.wait_ge(small2_in, now(small2_in, 1))
            norm_hi(small("n1"), range(KT))
            norm_root(TWO["norm1"].at["norms"])
            up(TWO["up1"], 0)
            down(TWO["down1"], small("n2"))
            norm_root(TWO["norm2"].at["norms"])

            st = TWO["cmp_kv"]
            n, s = st.at["panels"], st.at["steps"]
            round_panel(n + 2)
            begin(s)
            act.wait_ge(rcol_turned, now(rcol_turned, 1))
            act.activation(rcol[:, :], banks[7][:, T:T + 4:2], ACT.Copy).then_inc(rcol_ready, 1)
            act.wait_ge(rcol_ready, now(rcol_ready, 1))
            for tt in range(TT):
                e = act.activation(tok[:, KC2 + tt * PW:KC2 + (tt + 1) * PW], step_banks(s)[0][:, tt * PW:(tt + 1) * PW],
                                   ACT.Identity, scale=rcol[:, tt:tt + 1])
            e.then_inc(freed, 1)
            def tokens(name, j):
                st = TWO[name]
                n, s = st.at["panels"] + j, st.at["steps"] + j
                round_panel(n + 2)
                begin(s)
                bk = step_banks(s)[0][:, :].rearrange("p (t w) -> p t w", t=2)
                for tt in range(TT):
                    scale = rcol[:, tt:tt + 1]
                    if name == "nsa_g":
                        e = act.activation(gT[:, tt * 24:(tt + 1) * 24], bk[:, tt, 0:24], ACT.Sigmoid, scale=scale)
                    elif name == "nsa_q":
                        a = Q2 + tt * 512 + j * PW
                        e = act.activation(tok[:, a:a + PW], bk[:, tt, :], ACT.Identity, scale=scale)
                    elif name == "nsa_kv":
                        dst = tok[:, KS2:KS2 + 1024].rearrange("p (c t w) -> p c t w", c=2, t=2)
                        e = act.activation(dst[:, :, tt, j * P:(j + 1) * P], tile4(bk[:, tt, :], 2), ACT.Identity,
                                           scale=scale)
                    else:
                        a = M2 + tt * 1536 + j * PW
                        e = act.activation(tok[:, a:a + PW], bk[:, tt, :], ACT.Identity, scale=scale)
                e.then_inc(freed, 1)

            tokens("nsa_g", 0)
            b = st.at["turns"]
            x2 = gates[:, 0:4 * 272].rearrange("p (k t) -> p k t", k=4)
            for tt in range(TT):
                src = tile4(turn_bank(b)[:, :], 4)
                o = 1 - tt
                turns(st, b, (x2[0:HD, :, tt * P:(tt + 1) * P], src[0:HD]),
                      (x2[HD:P, :, tt * P - tt:tt * P + P - 1], src[HD:P, :, o:P]))
                b += 1
            tokens("nsa_q", 0)
            act.wait_ge(cm_dve, now(cm_dve, 1))
            act.activation(ahi[:, H2:H2 + 1024], work[:, 0:1024], ACT.Copy).then_inc(cm_act, 1)
            tokens("nsa_q", 1)
            tokens("nsa_kv", 0)
            tokens("nsa_kv", 1)
            st = TWO["cmp_w1"]
            for j in range(2):
                n, s = st.at["panels"] + j, st.at["steps"] + j
                round_panel(n + 2)
                begin(s)
                dst, src = glu[:, 0:32], step_banks(s)[0][:, 0:32]
                if j == 1:
                    dst = glu[:, 32:32 + P].rearrange("p (g r c) -> p g r c", g=2, r=4)
                    src = bcast(src.rearrange("p (g c) -> p g c", g=2), 2, 4)
                act.activation(dst, src, ACT.Gelu_apprx_tanh).then_inc(freed, 1)
            qv = qT[:, :].rearrange("p (a t) -> p a t", a=4)
            kv = kP[:, :].rearrange("p (i t) -> p i t", i=16)
            b = TWO["turn_nsa"].at["turns"]
            tokens("moba_qkv", 0)
            act.wait_ge(cm_pe, now(cm_pe, 1))
            act.activation(kct[0:32, 0:HD], banks[7][0:32, 0:HD], ACT.Copy).then_inc(cm_act, 1)
            tokens("moba_qkv", 1)
            for tt in range(TT):
                turns(st, b, (qv[:, :, tt * P:(tt + 1) * P], tile4(turn_bank(b)[:, :], 4)), None, HD ** -0.5)
                b += 1
            tokens("moba_qkv", 2)
            for tt in range(TT):
                src = tile4(turn_bank(b)[:, :], 4)
                turns(st, b, (kv[0:HD, 0:8:2, tt * P:(tt + 1) * P], src[0:HD]),
                      (kv[HD:P, 1:8:2, tt * P:(tt + 1) * P], src[HD:P]))
                b += 1
            act.wait_ge(cm_pe, now(cm_pe, 2))
            act.activation(kcp[0:HD, :].rearrange("p (g e c) -> p g e c", g=2, e=2)[:, :, 0, :],
                           banks[7][0:HD, 0:32].rearrange("p (g c) -> p g c", g=2), ACT.Copy)
            act.activation(kcp[HD:P, :].rearrange("p (g e c) -> p g e c", g=2, e=2)[:, :, 1, :],
                           banks[7][HD:P, 0:32].rearrange("p (g c) -> p g c", g=2), ACT.Copy).then_inc(cm_act, 1)
            tokens("moba_qkv", 3)
            tokens("moba_qkv", 4)
            act.wait_ge(cm_dve, now(cm_dve, 4))
            act.activation(cmpw[:, :], cmpw[:, :], ACT.Exp).then_inc(cm_act, 1)
            tokens("moba_qkv", 5)
            act.wait_ge(cm_pe, now(cm_pe, 5))
            act.activation(pcT, banks[7][:, 0:T], ACT.Copy).then_inc(cm_act, 1)
            st = TWO["turn_moba"]
            b = st.at["turns"]
            for tt in range(TT):
                turns(st, b, (qv[:, :, T + tt * P:T + (tt + 1) * P], tile4(turn_bank(b)[:, :], 4)), None, HD ** -0.5)
                b += 1
            for tt in range(TT):
                src = tile4(turn_bank(b)[:, :], 4)
                turns(st, b, (kv[0:HD, 8:16:2, tt * P:(tt + 1) * P], src[0:HD]),
                      (kv[HD:P, 9:16:2, tt * P:(tt + 1) * P], src[HD:P]))
                b += 1
            attention(2, None, False, TWO["attn"])
            st = TWO["merge"]
            for j in range(4):
                for c in range(3):
                    n, s = st.at["panels"] + 3 * j + c, st.at["steps"] + 3 * j + c
                    round_panel(n + 2)
                    if c < 2:
                        act.wait_ge(freed, now(freed, s + 1))
                        g = gates[:, (j % 2) * 1024 + c * 512:(j % 2) * 1024 + (c + 1) * 512]
                        act.activation(g, g, ACT.Sigmoid).then_inc(merge_gate, 1)
                act.wait_ge(merged, now(merged, st.at["merges"] + j + 1))
                act.activation(ahi[:, H2 + 2048 + j * 512:H2 + 2048 + (j + 1) * 512],
                               work[:, (j % 2) * 1024 + 512:(j % 2) * 1024 + 1024], ACT.Copy).then_inc(mhi_ready, 1)
            st = TWO["out"]
            for j in range(4):
                round_panel(st.at["panels"] + j + 2)
                act.wait_ge(freed, now(freed, st.at["steps"] + j + 1))
                norm_hi(small("n3"), (2 * j, 2 * j + 1))
            norm_root(TWO["norm3"].at["norms"])
            up(TWO["up2"], FT)
            down(TWO["down2"])
            Place.layer = None
        norm(START2["norms"] + LAYERS * PER_LAYER["norms"], 2, None, OUT_DONE - 1)

    @block.vector
    def _(dve):
        chain = Chain(dve_chain)
        Place.layer = Place.turn = None

        def split_half(n, h):
            dve.wait_ge(hi_ready, now(hi_ready, 2 * n + h + 1))
            a, b = h * PAN // 2, (h + 1) * PAN // 2
            dve.tensor_tensor(slot_lo(n, a, b), raw[:, (n % 2) * PAN + a:(n % 2) * PAN + b],
                              slot_hi(n, a, b).bitcast(F32), ALU.subtract).then_inc(lo_ready, 1)

        def split_panel(n):
            split_half(n, 0)
            split_half(n, 1)

        def begin(s):
            dve.wait_ge(tick, now(tick, STEP_TICK[s]))
            dve.wait_ge(freed, now(freed, s))

        def norm(k, blk, weight, last=None):
            w = XW[blk]
            rs = work[:, 1024:1024 + w]
            dve.wait_ge(std_ready, now(std_ready, k + 1))
            dve.reciprocal(rs, rs).then_inc(dve_chain, 1)
            dve.wait_ge(dve_chain, chain.next())
            if last:
                for kt in range(KT):
                    m = dve.scalar_tensor_tensor(x_of(kt, 0, w), x_of(kt, 0, w), weight[:, kt:kt + 1], rs,
                                                 ALU.mult, ALU.mult)
                    if kt < KT - 1:
                        m.then_inc(dve_chain, 1)
                        chain.n += 1
                m.then_inc(x_done, 1)
                return

            def scaled(kt):
                buf = work[:, (kt % 2) * 512:(kt % 2) * 512 + w]
                if weight is None:
                    m = dve.tensor_tensor(buf, x_of(kt, 0, w), rs, ALU.mult)
                else:
                    m = dve.scalar_tensor_tensor(buf, x_of(kt, 0, w), weight[:, kt:kt + 1], rs, ALU.mult, ALU.mult)
                m.then_inc(tile_ready, 1)

            def lo(kt):
                dve.wait_ge(xhi_ready, now(xhi_ready, 8 * k_x(k) + kt + 1))
                dve.tensor_tensor(act_x(alo, blk, kt, 0, w), work[:, (kt % 2) * 512:(kt % 2) * 512 + w],
                                  act_x(ahi, blk, kt, 0, w).bitcast(F32), ALU.subtract).then_inc(x_split, 1)
                if kt < KT - 1:
                    dve.wait_ge(x_split, now(x_split, 8 * k_x(k) + kt + 1))

            scaled(0)
            scaled(1)
            for kt in range(KT):
                lo(kt)
                if kt + 2 < KT:
                    scaled(kt + 2)

        def attention(blk, mixer, with_ctx, st):
            units, groups, pairs = attention_plan(blk, mixer, with_ctx)
            u0, g0, p0 = st.at["units"], st.at["groups"], st.at["pairs"]
            for i in range(len(units) + 7):
                if i < len(units):
                    un, u = units[i], u0 + i
                    sbase = (u % 3) * 8
                    dve.wait_ge(scores, now(scores, u + 1))
                    bank = score_bank(u)
                    for c, w, segs, mask in un.masks:
                        if isinstance(mask, tuple):
                            nb = st.layer * NH + mask[1]
                            dve.wait_ge(biased, nb + 1)
                            mk = bias[:, (nb % 2) * 512 + mask[2] * T:(nb % 2) * 512 + (mask[2] + 1) * T]
                            dve.tensor_tensor(bank[:, c:c + w], bank[:, c:c + w], mk, ALU.add).then_inc(bias_used, 1)
                            dve.wait_ge(bias_used, 2 * nb + mask[2] + 1)
                        elif segs == 1:
                            dve.tensor_tensor(bank[:, c:c + w], bank[:, c:c + w], mask, ALU.add).then_inc(dve_chain, 1)
                            dve.wait_ge(dve_chain, chain.next())
                        else:
                            dst = tile4(bank[:, :], 2)[:, :, c:c + w]
                            dve.tensor_tensor(dst, dst, bcast(mask, 1, 2), ALU.add).then_inc(dve_chain, 1)
                            dve.wait_ge(dve_chain, chain.next())
                    ns = len(un.segs)
                    nm = stats[:, sbase:sbase + ns]
                    w = un.segs[0][1]
                    src = bank[:, 0:w] if ns == 1 else tile4(bank[:, :], 2)[:, :, 0:w]
                    m = dve.reduce_max(nm, src, AX.X, negate=True)
                    if un.segs[0][2] is not None:
                        m.then_inc(dve_chain, 1)
                        dve.wait_ge(dve_chain, chain.next())
                        a = SMALL1["sink"][0] + st.layer * NSMALL1 + un.segs[0][2]
                        m = dve.scalar_tensor_tensor(nm, sm1[:, a:a + ns], -1.0, nm, ALU.mult, ALU.min)
                    m.then_inc(negmax, 1)
                j = i - 1
                if 0 <= j < len(units):
                    un, u = units[j], u0 + j
                    sbase = (u % 3) * 8
                    ns = len(un.segs)
                    dve.wait_ge(exped, now(exped, u + 1))
                    total = stats[:, sbase + 2:sbase + 2 + ns]
                    if un.segs[0][2] is not None:
                        dve.tensor_tensor(total, total, stats[:, sbase + 6:sbase + 6 + ns], ALU.add).then_inc(dve_chain, 1)
                        dve.wait_ge(dve_chain, chain.next())
                    inv = stats[:, sbase + 4:sbase + 4 + ns]
                    dve.reciprocal(inv, total).then_inc(dve_chain, 1)
                    dve.wait_ge(dve_chain, chain.next())
                    if un.segs[0][3] is not None:
                        qt, col = un.segs[0][3]
                        dve.tensor_tensor(inv, inv, gT[:, qt * 24 + col:qt * 24 + col + 2], ALU.mult).then_inc(dve_chain, 1)
                        dve.wait_ge(dve_chain, chain.next())
                    for k, (c, w, _, _) in enumerate(un.segs):
                        m = dve.tensor_scalar(probs(u)[:, c:c + w], probs(u)[:, c:c + w], inv[:, k:k + 1], None, ALU.mult)
                    m.then_inc(normed, 1)
                j = i - 4
                if 0 <= j < len(units) and last_unit_of(units, units[j].group) == j and groups[units[j].group].last:
                    g = units[j].group
                    pr = groups[g].pair
                    dve.wait_ge(pv, now(pv, g0 + g + 1))
                    if p0 + pr - 1 >= 1:
                        dve.wait_ge(usplit, now(usplit, p0 + pr - 1))
                    if blk == 1:
                        m = dve.tensor_tensor(gated(p0 + pr), out_bank(p0 + pr)[:, 0:T], gate_of(1, pairs[pr]), ALU.mult)
                    else:
                        m = dve.tensor_copy(gated(p0 + pr), out_bank(p0 + pr)[:, 0:T])
                    m.then_inc(omul, 1)
                j = i - 6
                if 0 <= j < len(units) and last_unit_of(units, units[j].group) == j and groups[units[j].group].last:
                    pr = groups[units[j].group].pair
                    dve.wait_ge(uhi, now(uhi, p0 + pr + 1))
                    dve.tensor_tensor(u_of(alo, blk, pairs[pr]), gated(p0 + pr), u_of(ahi, blk, pairs[pr]).bitcast(F32),
                                      ALU.subtract).then_inc(usplit, 1)

        def norm_squares(j):
            x = xT[:, :].rearrange("p (k t) -> p k t", k=KT)[:, 2 * j:2 * j + 2, 0:T]
            dve.tensor_tensor(tile4(work[:, j * 512:(j + 1) * 512], 2), x, x, ALU.mult).then_inc(sq_ready, 2)

        def norm_lo(k, weight, j):
            for kt in (2 * j, 2 * j + 1):
                dve.wait_ge(xhi_ready, now(xhi_ready, 8 * k_x(k) + kt + 1))
                dve.scalar_tensor_tensor(act_x(alo, 2, kt, 0, T), x_of(kt), weight[:, kt:kt + 1],
                                         act_x(ahi, 2, kt, 0, T).bitcast(F32), ALU.mult, ALU.subtract).then_inc(x_split, 1)

        def norm_scale(k):
            dve.wait_ge(std_ready, now(std_ready, k + 1))
            dve.reciprocal(rs[:, :], rs[:, :]).then_inc(rs_ready, 1)

        def rope(src, dst, heads, cos, sin, nsin, rows=P, dup=False):
            x = src.rearrange("p (h e f) -> p h e f", h=heads, e=2)
            t1 = work[0:rows, 0:heads * HD].rearrange("p (h e f) -> p h e f", h=heads, e=2)
            t2 = work[0:rows, 512:512 + heads * HD].rearrange("p (h e f) -> p h e f", h=heads, e=2)
            b1 = bcast(bcast(cos, 1, 2), 1, heads)
            dve.tensor_tensor(t1, x, b1, ALU.mult)
            dve.tensor_tensor(t2[:, :, 0, :], x[:, :, 1, :], bcast(nsin, 1, heads), ALU.mult)
            dve.tensor_tensor(t2[:, :, 1, :], x[:, :, 0, :], bcast(sin, 1, heads), ALU.mult).then_inc(dve_chain, 1)
            dve.wait_ge(dve_chain, chain.next())
            a, b = work[0:rows, 0:heads * HD], work[0:rows, 512:512 + heads * HD]
            if not dup:
                dve.tensor_tensor(dst, a, b, ALU.add).then_inc(dve_chain, 1)
                dve.wait_ge(dve_chain, chain.next())
            else:
                d = dst.rearrange("p (h e f) -> p h e f", h=heads, e=2)
                a, b = (v.rearrange("p (h f) -> p h f", h=heads) for v in (a, b))
                dve.tensor_tensor(d[:, :, 0, :], a, b, ALU.add).then_inc(dve_chain, 1)
                dve.wait_ge(dve_chain, chain.next())
                dve.tensor_tensor(d[:, :, 1, :], a, b, ALU.add).then_inc(dve_chain, 1)
                dve.wait_ge(dve_chain, chain.next())

        dve.memset(ahi[:, CP:CP + KT * P].bitcast(mybir.dt.uint32), 0).then_inc(c_split, 1)
        split_panel(0)
        dve.wait_ge(c_hi, 1)
        cpad = ahi[:, CP:CP + KT * P].rearrange("p (k m) -> p k m", k=KT)
        dve.tensor_tensor(cpad[:, :, 2:4], tile4(cmpw[:, 0:2 * KT], KT), cpad[:, :, 0:2].bitcast(F32),
                          ALU.subtract).then_inc(c_split, 1)
        split_panel(1)

        for l in range(LAYERS):
            wctx = l == 0
            nt = 4 if wctx else 2
            st = ONE["ada", l]
            for j in range(12):
                split_panel(st.at["panels"] + j + 2)
            s1 = l * NSMALL1

            def small(name):
                a, b = SMALL1[name]
                return sm1[:, s1 + a:s1 + b]

            dve.wait_ge(consts_in, 64)
            dve.wait_ge(mod_cols, l + 1)
            dve.tensor_tensor(mod[:, :].rearrange("p (t c) -> p t c", c=2),
                                         banks[7][:, 0:48].rearrange("p (t c) -> p t c", c=2),
                                         bcast(small("ada_b"), 2, 2), ALU.add).then_inc(dve_chain, 1)
            dve.wait_ge(dve_chain, chain.next())
            dve.scalar_tensor_tensor(moda[:, :].rearrange("p (t c) -> p t c", c=2),
                                     mod[:, 16:32].rearrange("p (t c) -> p t c", c=2), 1.0,
                                     bcast(small("norm_w"), 2, 2), ALU.add, ALU.mult).then_inc(mod_ready, 1)
            norm(ONE["norm", l].at["norms"], 1, None)

            def qkv(m):
                st = ONE["qkv" + m, l]
                for j in range(st.panels):
                    split_panel(st.at["panels"] + j + 2)
                return st.at["steps"] + st.panels

            def head_norm(evacuated):
                dve.wait_ge(freed, now(freed, evacuated))
                for tt in range(4):
                    for sec, heads, col in ((Q1, 8, 0), (K1, 2, 8)):
                        if sec == Q1 and tt >= nt:
                            continue
                        x = tok[:, sec + tt * 512:sec + tt * 512 + heads * HD]
                        dve.tensor_tensor(work[:, 0:heads * HD], x, x, ALU.mult).then_inc(dve_chain, 1)
                        dve.wait_ge(dve_chain, chain.next())
                        m = dve.reduce_sum(hstat[:, tt * 10 + col:tt * 10 + col + heads],
                                           work[:, 0:heads * HD].rearrange("p (h f) -> p h f", h=heads), AX.X)
                        m.then_inc(dve_chain, 1)
                        dve.wait_ge(dve_chain, chain.next())
                if nt == 2:
                    dve.memset(hstat[:, 20:28], 1.0).then_inc(dve_chain, 1)
                    dve.wait_ge(dve_chain, chain.next())
                    dve.memset(hstat[:, 30:38], 1.0).then_inc(dve_chain, 1)
                    dve.wait_ge(dve_chain, chain.next())
                dve.sem_inc(hs_sum, 1)

            def head_scale():
                dve.wait_ge(hs_std, l + 1)
                dve.reciprocal(hstat[:, :], hstat[:, :]).then_inc(dve_chain, 1)
                dve.wait_ge(dve_chain, chain.next())
                for tt in range(4):
                    for sec, heads, col, w in ((Q1, 8, 0, "qn"), (K1, 2, 8, "kn")):
                        if sec == Q1 and tt >= nt:
                            continue
                        x = tok[:, sec + tt * 512:sec + tt * 512 + heads * HD].rearrange("p (h f) -> p h f", h=heads)
                        dve.tensor_tensor(x, x, bcast(hstat[:, tt * 10 + col:tt * 10 + col + heads], 2, HD), ALU.mult).then_inc(dve_chain, 1)
                        dve.wait_ge(dve_chain, chain.next())
                        dve.tensor_tensor(x, x, bcast(small(w), 1, heads), ALU.mult).then_inc(dve_chain, 1)
                        dve.wait_ge(dve_chain, chain.next())

            def rope_all(m):
                for tt in range(4):
                    tabs = [const(x)[:, tt * HALF:(tt + 1) * HALF] for x in ("cos1", "sin1", "nsin1")] if tt < 2 else None
                    if tt < 2:
                        q = tok[:, Q1 + tt * 512:Q1 + (tt + 1) * 512]
                        rope(q, q, 8, *tabs)
                    k = tok[:, K1 + tt * 512:K1 + tt * 512 + P]
                    kd = work[:, 1024 + tt * 256:1024 + (tt + 1) * 256]
                    if tt < 2:
                        rope(k, kd, 2, *tabs, dup=True)
                    else:
                        dve.tensor_copy(kd.rearrange("p (h e f) -> p h e f", h=2, e=2),
                                                   bcast(k.rearrange("p (h f) -> p h f", h=2), 2, 2)).then_inc(dve_chain, 1)
                        dve.wait_ge(dve_chain, chain.next())
                dve.sem_inc(roped, 1)

            def gate(m):
                for j in range(2):
                    split_panel(ONE["gate" + m, l].at["panels"] + j + 2)

            def wout(m):
                st = ONE["wout" + m, l]
                for j in range(2):
                    for c in range(2):
                        s = st.at["steps"] + 2 * j + c
                        if c == 1:
                            split_panel(st.at["panels"] + j + 2)
                        begin(s)
                        for e in range(2):
                            kt = 4 * j + 2 * c + e
                            bank = step_banks(s)[e]
                            for part in range(2 if wctx else 1):
                                o = dve.scalar_tensor_tensor(x_of(kt, part * T, (part + 1) * T), bank[:, part * T:(part + 1) * T],
                                                             mod[:, 32 + kt * 2 + part:33 + kt * 2 + part],
                                                             x_of(kt, part * T, (part + 1) * T), ALU.mult, ALU.add)
                        o.then_inc(freed, 1)

            for m in MIX1:
                if m == "A":
                    done = qkv("A")
                    head_norm(done)
                    gate("A")
                    head_scale()
                    rope_all("A")
                else:
                    gate(m)
                    if m == "C":
                        dve.wait_ge(freed, now(freed, ONE["qkvC", l].at["steps"] + 3))
                        rope_all("C")
                attention(1, m, wctx, ONE["attn" + m, l])
                if m == "A":
                    qkv("B")
                    wout("A")
                if m == "B":
                    qkv("C")
                    wout("B")
                if m == "C":
                    wout("C")
            dve.wait_ge(freed, ONE["woutC", l].at["steps"] + 4)
            dve.sem_inc(x_done, 1)

        norm(START2["norms"] - 1, 2, smg[:, 0:8], last=True)

        assert chain.n == DVE_START2
        with dve.Fori(0, LAYERS) as layer:
            Place.layer = layer

            def small(name):
                a, b = SMALL2[name]
                return sm2[:, a:b]

            dve.tensor_copy(sm2[:, :], sm2all[:, bass.ds(layer * NSMALL2, NSMALL2)]).then_inc(small2_in, 1)
            dve.wait_ge(small2_in, now(small2_in, 1))

            def up(st, first_hidden, scales):
                n0, s0 = st.at["panels"], st.at["steps"]
                with dve.Fori(0, FT // 2) as turn:
                    Place.turn = turn
                    for j in range(2):
                        n, s, a = n0 + j, s0 + j, first_hidden + j
                        gu = work[:, (j % 2) * 512:(j % 2) * 512 + 512]
                        dve.wait_ge(rs_ready, now(rs_ready, scales))
                        dve.wait_ge(tick, now(tick, STEP_TICK[s]))
                        dve.tensor_tensor(tile4(gu, 2), tile4(step_banks(s)[0][:, :], 2), bcast(rs[:, :], 1, 2),
                                          ALU.mult).then_inc(freed, 1)
                        split_half(n + 2, 0)
                        dve.wait_ge(silu_ready, now(silu_ready, a + 1))
                        dve.tensor_tensor(gu[:, T:2 * T], gu[:, T:2 * T], gu[:, 0:T], ALU.mult).then_inc(hid_gated, 1)
                        split_half(n + 2, 1)
                        dve.wait_ge(hhi_ready, now(hhi_ready, a + 1))
                        f = [x[:, H2:H2 + FT * T].rearrange("p (f t) -> p f t", f=FT)[:, 2 * turn + j, :] for x in (ahi, alo)]
                        dve.tensor_tensor(f[1], gu[:, T:2 * T], f[0].bitcast(F32), ALU.subtract).then_inc(hid_split, 1)
                    Place.turn = None

            def residual(s, kt, factor, src):
                x = xT[:, :].rearrange("p (k t) -> p k t", k=KT)[:, kt:kt + 2, 0:T]
                return dve.scalar_tensor_tensor(x, tile4(src[:, :], 2), factor, x, ALU.mult, ALU.add)

            def down(st, k=None, weight=None):
                n = 0
                for j in range(4):
                    while (n + 1) * NB <= DOWN_STEP_ENDS[j]:
                        split_panel(st.at["panels"] + n + 2)
                        n += 1
                    if j and k is not None:
                        norm_lo(k, weight, j - 1)
                    s = st.at["steps"] + j
                    begin(s)
                    residual(s, 2 * j, 0.5, step_banks(s)[0]).then_inc(freed, 1)
                    if k is not None:
                        dve.wait_ge(freed, now(freed, s + 1))
                        norm_squares(j)
                if k is not None:
                    norm_lo(k, weight, 3)
                dve.wait_ge(freed, now(freed, st.at["steps"] + 4))
                dve.sem_inc(x_done, 1)

            dve.wait_ge(x_done, now(x_done, X_DONE2))
            norm_squares(0)
            for j in range(4):
                if j < 3:
                    norm_squares(j + 1)
                norm_lo(TWO["norm1"].at["norms"], small("n1"), j)
            norm_scale(TWO["norm1"].at["norms"])
            up(TWO["up1"], 0, 1)
            down(TWO["down1"], TWO["norm2"].at["norms"], small("n2"))
            norm_scale(TWO["norm2"].at["norms"])

            def rotate(tt, what):
                tabs = [const(x)[:, tt * HALF:(tt + 1) * HALF] for x in ("cos2", "sin2", "nsin2")]
                if what == "nsa":
                    q = tok[:, Q2 + tt * 512:Q2 + (tt + 1) * 512]
                    rope(q, q, 8, *tabs)
                    rope(tok[:, KS2 + tt * 256:KS2 + (tt + 1) * 256], work[:, 1024 + tt * 512:1024 + (tt + 1) * 512], 4,
                         *tabs, dup=True)
                else:
                    a = M2 + tt * 1536 + what * 512
                    rope(tok[:, a:a + 512], tok[:, a:a + 512], 8, *tabs)

            st = TWO["cmp_kv"]
            split_panel(st.at["panels"] + 2)
            dve.wait_ge(freed, now(freed, st.at["steps"] + 1))
            for tt in range(TT):
                kd = work[:, 1024 + tt * 512:1024 + (tt + 1) * 512].rearrange("p (k e f) -> p k e f", k=4, e=2)
                k = tok[:, KC2 + tt * 256:KC2 + (tt + 1) * 256].rearrange("p (k f) -> p k f", k=4)
                dve.tensor_copy(kd, bcast(k, 2, 2))
            x2 = gates[:, 0:4 * 272].rearrange("p (k t) -> p k t", k=4)
            dve.memset(x2[:, :, T - 1:272], 0.0).then_inc(roped, 1)
            split_panel(TWO["nsa_g"].at["panels"] + 2)
            dve.wait_ge(turn_out, now(turn_out, st.at["turns"] + 2))
            pos = small("pos")
            for kg in range(4):
                base = gates[:, kg * 272:kg * 272 + 256]
                src = bass.AP(base.tensor, base.offset, [base.ap[0], [16, NCMP], [2, 16]])
                o = dve.tensor_tensor(work[:, kg * 256:(kg + 1) * 256].rearrange("p (n j) -> p n j", n=NCMP), src,
                                      bcast(pos[:, (kg // 2) * 16:(kg // 2 + 1) * 16], 1, NCMP), ALU.add)
            o.then_inc(cm_dve, 1)
            split_panel(TWO["nsa_q"].at["panels"] + 2)
            dve.wait_ge(cm_act, now(cm_act, 1))
            dve.tensor_tensor(alo[:, H2:H2 + 1024], work[:, 0:1024], ahi[:, H2:H2 + 1024].bitcast(F32),
                              ALU.subtract).then_inc(cm_dve, 1)
            dve.wait_ge(cm_dve, now(cm_dve, 2))
            split_panel(TWO["nsa_q"].at["panels"] + 3)
            for name in ("nsa_kv", "cmp_w1"):
                for j in range(2):
                    split_panel(TWO[name].at["panels"] + j + 2)
            m0, s0 = TWO["moba_qkv"].at["panels"], TWO["moba_qkv"].at["steps"]
            rotate(0, "nsa")
            split_panel(m0 + 2)
            rotate(1, "nsa")
            dve.sem_inc(roped, 1)
            split_panel(m0 + 3)
            dve.wait_ge(cm_act, now(cm_act, 2))
            rope(kct[0:32, 0:HD], kct[0:32, P:2 * P], 1, *[const(x)[0:32] for x in ("cosc", "sinc", "nsinc")], rows=32, dup=True)
            dve.sem_inc(cm_dve, 1)
            split_panel(m0 + 4)
            dve.wait_ge(freed, now(freed, s0 + 2))
            rotate(0, 0)
            rotate(1, 0)
            split_panel(m0 + 5)
            dve.wait_ge(cm_pe, now(cm_pe, 3))
            dve.tensor_tensor(cmpw[:, :].rearrange("p (q h c) -> p q h c", q=2, h=NH),
                              banks[7][:, 0:256].rearrange("p (q h c) -> p q h c", q=2, h=NH),
                              bcast(tile4(const("cmp_add"), 2), 2, NH), ALU.add).then_inc(dve_chain, 1)
            dve.wait_ge(dve_chain, chain.next())
            heads = cmpw[:, :].rearrange("p (a c) -> p a c", c=NCMP)
            dve.reduce_max(cstat[:, 0:16], heads, AX.X, negate=True).then_inc(dve_chain, 1)
            dve.wait_ge(dve_chain, chain.next())
            dve.tensor_tensor(heads, heads, bcast(cstat[:, 0:16], 2, NCMP), ALU.add).then_inc(cm_dve, 1)
            dve.wait_ge(freed, now(freed, s0 + 4))
            rotate(0, 1)
            split_panel(m0 + 6)
            dve.wait_ge(cm_act, now(cm_act, 4))
            keep = bcast(tile4(const("cmp_keep"), 2), 2, NH)
            w4 = cmpw[:, :].rearrange("p (q h c) -> p q h c", q=2, h=NH)
            dve.tensor_tensor(w4, w4, keep, ALU.mult).then_inc(dve_chain, 1)
            dve.wait_ge(dve_chain, chain.next())
            dve.reduce_sum(cstat[:, 0:16], heads, AX.X).then_inc(dve_chain, 1)
            dve.wait_ge(dve_chain, chain.next())
            dve.tensor_scalar(cstat[:, 0:16], cstat[:, 0:16], TINY, None, ALU.max).then_inc(dve_chain, 1)
            dve.wait_ge(dve_chain, chain.next())
            dve.reciprocal(cstat[:, 0:16], cstat[:, 0:16]).then_inc(dve_chain, 1)
            dve.wait_ge(dve_chain, chain.next())
            g0 = tile4(gT[:, :], 2).rearrange("p q (h b) -> p q h b", b=3)[:, :, :, 0]
            dve.tensor_tensor(tile4(cstat[:, 0:16], 2), tile4(cstat[:, 0:16], 2), g0, ALU.mult).then_inc(dve_chain, 1)
            dve.wait_ge(dve_chain, chain.next())
            dve.wait_ge(cm_pe, now(cm_pe, 4))
            dve.tensor_tensor(vblk.rearrange("p (h f) -> p h f", h=NH), bcast(banks[7][:, 256:256 + HD], 1, NH),
                              bcast(const("head_of"), 2, HD), ALU.mult)
            dve.tensor_tensor(heads, heads, bcast(cstat[:, 0:16], 2, NCMP), ALU.mult).then_inc(cm_dve, 1)
            rotate(1, 1)
            dve.sem_inc(roped, 1)
            split_panel(m0 + 7)
            attention(2, None, False, TWO["attn"])
            st = TWO["merge"]
            for j in range(4):
                for c in range(3):
                    s = st.at["steps"] + 3 * j + c
                    begin(s)
                    if c < 2:
                        dve.wait_ge(rs_ready, now(rs_ready, 2))
                        g = gates[:, (j % 2) * 1024 + c * 512:(j % 2) * 1024 + (c + 1) * 512]
                        dve.tensor_tensor(tile4(g, 2), tile4(step_banks(s)[0][:, :], 2), bcast(rs[:, :], 1, 2),
                                          ALU.mult).then_inc(freed, 1)
                    split_panel(st.at["panels"] + 3 * j + c + 2)
                dve.wait_ge(merge_gate, now(merge_gate, 2 * j + 2))
                ga = gates[:, (j % 2) * 1024:(j % 2) * 1024 + 512]
                gb = gates[:, (j % 2) * 1024 + 512:(j % 2) * 1024 + 1024]
                m1 = work[:, (j % 2) * 1024:(j % 2) * 1024 + 512]
                m2 = work[:, (j % 2) * 1024 + 512:(j % 2) * 1024 + 1024]
                dve.tensor_tensor(m1, step_banks(s)[0][:, :], ga, ALU.mult)
                dve.tensor_tensor(m2, step_banks(s)[1][:, :], gb, ALU.mult).then_inc(freed, 1)
                dve.wait_ge(freed, now(freed, s + 1))
                dve.tensor_tensor(m2, m2, m1, ALU.add).then_inc(merged, 1)
                dve.wait_ge(mhi_ready, now(mhi_ready, st.at["merges"] + j + 1))
                dve.tensor_tensor(alo[:, H2 + 2048 + j * 512:H2 + 2048 + (j + 1) * 512], m2,
                                  ahi[:, H2 + 2048 + j * 512:H2 + 2048 + (j + 1) * 512].bitcast(F32),
                                  ALU.subtract).then_inc(m_split, 1)
            st = TWO["out"]
            for j in range(4):
                s = st.at["steps"] + j
                begin(s)
                residual(s, 2 * j, 1.0, step_banks(s)[0]).then_inc(freed, 1)
                dve.wait_ge(freed, now(freed, s + 1))
                norm_squares(j)
                split_panel(st.at["panels"] + j + 2)
                norm_lo(TWO["norm3"].at["norms"], small("n3"), j)
            dve.wait_ge(freed, now(freed, st.at["steps"] + 4))
            dve.sem_inc(x_done, 1)
            norm_scale(TWO["norm3"].at["norms"])
            up(TWO["up2"], FT, 3)
            down(TWO["down2"])
            assert chain.n == DVE_START2 + DVE_LAYER
            Place.layer = None
        chain.n = DVE_START2 + LAYERS * DVE_LAYER
        norm(START2["norms"] + LAYERS * PER_LAYER["norms"], 2, smg[:, 8:16], last=True)

    @block.tensor
    def _(pe):
        Place.layer = Place.turn = None

        def mm3(dst, whi_, wlo_, xhi_, xlo_, start, stop):
            pe.matmul(dst, whi_, xhi_, start=start, stop=False, skip_group_check=True)
            pe.matmul(dst, whi_, xlo_, start=False, stop=False, skip_group_check=True)
            return pe.matmul(dst, wlo_, xhi_, start=False, stop=stop, skip_group_check=True)

        def need(n, half):
            pe.wait_ge(lo_ready, now(lo_ready, 2 * n + half + 1))

        def take(s):
            if s - 1 >= 1:
                pe.wait_ge(freed, now(freed, s - 1))

        def wblock(n, b, c0=0, c1=PW):
            return slot_hi(n, b * PW + c0, b * PW + c1), slot_lo(n, b * PW + c0, b * PW + c1)

        def feature_major(n, dst, m, rhs, blocks=range(NB), inputs=None):
            bl = list(blocks)
            for b in bl:
                need(n, b // 4)
                if inputs is not None:
                    pe.wait_ge(inputs[0], now(inputs[0], inputs[1] + b // inputs[2] + 1))
                wh, wl = wblock(n, b, m * P, (m + 1) * P)
                xh, xl = rhs(b)
                o = mm3(dst, wh, wl, xh, xl, b == bl[0], b == bl[-1])
            return o

        def token_major(n, dst, blk, tt, width=PW, inputs=None):
            for kt in range(KT):
                need(n, kt // 4)
                if inputs is not None:
                    pe.wait_ge(x_split, now(x_split, inputs + kt + 1))
                wh, wl = wblock(n, kt, 0, width)
                xh, xl = (act_x(x, blk, kt, tt * P, (tt + 1) * P) for x in (ahi, alo))
                o = mm3(dst, xh, xl, wh, wl, kt == 0, kt == KT - 1)
            return o

        def norm(k, blk):
            w = XW[blk]
            if k:
                pe.wait_ge(std_ready, now(std_ready, k))
            for kt in range(KT):
                pe.wait_ge(sq_ready, now(sq_ready, 8 * k + kt + 1))
                pe.matmul(banks[7][:, 0:w], ones, work[:, (kt % 2) * 512:(kt % 2) * 512 + w],
                          start=kt == 0, stop=kt == KT - 1).then_inc(sq_used, 1)

        def norm_sums(k, tiles):
            if 0 in tiles:
                pe.wait_ge(std_ready, now(std_ready, k))
            for kt in tiles:
                pe.wait_ge(sq_ready, now(sq_ready, 8 * k + kt + 1))
                pe.matmul(banks[7][:, 0:T], ones, work[:, kt * T:(kt + 1) * T],
                          start=kt == 0, stop=kt == KT - 1).then_inc(sq_used, 1)

        def turn(st, b, blocks):
            if b - 1 >= 1:
                pe.wait_ge(turn_out, now(turn_out, b - 1))
            for k, src in enumerate(blocks):
                o = pe.transpose(turn_bank(b)[:, k * P:(k + 1) * P], src, ident)
            o.then_inc(turned, 1)

        def attention(blk, mixer, with_ctx, st, after):
            units, groups, pairs = attention_plan(blk, mixer, with_ctx)
            u0, g0, p0 = st.at["units"], st.at["groups"], st.at["pairs"]
            pe.wait_ge(freed, now(freed, after))
            for i in range(len(units) + 4):
                if i < len(units):
                    un, u = units[i], u0 + i
                    if u - 2 >= 1:
                        pe.wait_ge(exped, now(exped, u - 2))
                    for k, (keys, c, w) in enumerate(un.keys):
                        o = pe.matmul(score_bank(u)[:, c:c + w], un.q, keys, start=True, stop=True, skip_group_check=True)
                    o.then_inc(scores, 1)
                j = i - 2
                if 0 <= j < len(units):
                    un, u = units[j], u0 + j
                    pe.wait_ge(normed, now(normed, u + 1))
                    if u - 1 >= 1:
                        pe.wait_ge(probT_out, now(probT_out, u - 1))
                    for c, b in un.blocks:
                        o = pe.transpose(prob_bank(u)[:, b * P:(b + 1) * P], probs(u)[:, c:c + P], ident)
                    o.then_inc(probT, 1)
                j = i - 4
                if 0 <= j < len(units) and last_unit_of(units, units[j].group) == j:
                    g = units[j].group
                    gr = groups[g]
                    pe.wait_ge(probT_out, now(probT_out, u0 + j + 1))
                    if p0 + gr.pair - 1 >= 1:
                        pe.wait_ge(omul, now(omul, p0 + gr.pair - 1))
                    ob = out_bank(p0 + gr.pair)
                    if gr.cmp:
                        pr = pairs[gr.pair][0]
                        pe.matmul(ob[:, 0:T], vblk[:, pr * P:(pr + 1) * P], pcT, start=True, stop=False,
                                  skip_group_check=True)
                    for k, (half, v, b, q0, start) in enumerate(gr.adds):
                        o = pe.matmul(ob[half * HD:(half + 1) * HD, q0:T], v, probsT(g0 + g)[:, b, q0:T],
                                      start=start, stop=k == len(gr.adds) - 1, skip_group_check=True)
                    o.then_inc(pv, 1)

        pe.wait_ge(consts_in, 64)
        pe.wait_ge(pads_zero, 2)
        for l in range(LAYERS):
            wctx = l == 0
            nt = 4 if wctx else 2
            w = 2 * T if wctx else T
            st = ONE["ada", l]
            pe.wait_ge(c_split, 2)
            cpad = ahi[:, CP:CP + KT * P].rearrange("p (k m) -> p k m", k=KT)
            for j in range(12):
                n, s = st.at["panels"] + j, st.at["steps"] + j
                take(s)
                for kt in range(KT):
                    need(n, kt // 4)
                    wh, wl = wblock(n, kt)
                    pe.matmul(step_banks(s)[0][:, 0:PW], cpad[:, kt, :], wh, start=kt == 0, stop=False)
                    o = pe.matmul(step_banks(s)[0][:, 0:PW], cpad[:, kt, :], wl, start=False, stop=kt == KT - 1)
                o.then_inc(tick, 1)
            pe.wait_ge(freed, now(freed, st.at["steps"] + 12))
            for t in range(24):
                o = pe.matmul(banks[7][:, 2 * t:2 * t + 2], tok[0:4, t * P:(t + 1) * P], const("sel", slice(0, 4)),
                              start=True, stop=True)
            o.then_inc(mod_cols, 1)
            pe.wait_ge(mod_ready, l + 1)
            norm(ONE["norm", l].at["norms"], 1)

            def qkv(m):
                st = ONE["qkv" + m, l]
                for j in range(st.panels):
                    n, s = st.at["panels"] + j, st.at["steps"] + j
                    take(s)
                    if j == 0 and m == "A":
                        pe.wait_ge(x_split, now(x_split, 8 * k_x(ONE["norm", l].at["norms"]) + KT))
                    full = qkv_places(m, j)[0][0] != Q1 or wctx
                    for tt in range(4 if full else 2):
                        o = token_major(n, step_banks(s)[tt // 2][:, (tt % 2) * PW:(tt % 2 + 1) * PW], 1, tt)
                    o.then_inc(tick, 1)

            def gate(m):
                st = ONE["gate" + m, l]
                for j in range(2):
                    n, s = st.at["panels"] + j, st.at["steps"] + j
                    take(s)
                    for c in range(2):
                        o = feature_major(n, step_banks(s)[c][:, 0:w], c,
                                          lambda b: (act_x(ahi, 1, b, 0, w), act_x(alo, 1, b, 0, w)))
                    o.then_inc(tick, 1)

            def wout(m):
                st = ONE["wout" + m, l]
                at = ONE["attn" + m, l]
                pe.wait_ge(usplit, now(usplit, at.at["pairs"] + at.pairs))
                for j in range(2):
                    n = st.at["panels"] + j
                    for c in range(2):
                        s = st.at["steps"] + 2 * j + c
                        take(s)
                        for e in range(2):
                            for kt in range(4):
                                a = kt * 512 + (2 * c + e) * P
                                need(n, (a + P - 1) // (PAN // 2))
                                ux = [x[:, U1 + kt * 512:U1 + kt * 512 + w] for x in (ahi, alo)]
                                o = mm3(step_banks(s)[e][:, 0:w], slot_hi(n, a, a + P), slot_lo(n, a, a + P), *ux,
                                        kt == 0, kt == 3)
                        o.then_inc(tick, 1)

            for m in MIX1:
                if m == "A":
                    qkv("A")
                gate(m)
                st = ONE["turn" + m, l]
                b = st.at["turns"]
                pe.wait_ge(roped, 2 * l + (1 if m == "A" else 2)) if m != "B" else None
                pe.wait_ge(freed, now(freed, ONE["qkv" + m, l].at["steps"] + ONE["qkv" + m, l].steps))
                if ONE["attn" + m, l].at["pairs"] >= 1:
                    pe.wait_ge(omul, now(omul, ONE["attn" + m, l].at["pairs"]))
                for tt in range(nt):
                    turn(st, b, [tok[:, Q1 + tt * 512 + i * P:Q1 + tt * 512 + (i + 1) * P] for i in range(4)])
                    b += 1
                if m == "B":
                    for tt in range(4):
                        turn(st, b, [tok[:, K1 + tt * 512 + i * P:K1 + tt * 512 + (i + 1) * P] for i in range(4)])
                        b += 1
                else:
                    for c in range(2):
                        turn(st, b, [work[:, 1024 + tt * 256 + g * P:1024 + tt * 256 + (g + 1) * P]
                                     for g in range(2) for tt in (2 * c, 2 * c + 1)])
                        b += 1
                pe.wait_ge(turn_out, now(turn_out, b))
                attention(1, m, wctx, ONE["attn" + m, l], ONE["gate" + m, l].at["steps"] + 2)
                if m == "A":
                    qkv("B")
                    wout("A")
                if m == "B":
                    qkv("C")
                    wout("B")
                if m == "C":
                    wout("C")

        norm(START2["norms"] - 1, 2)

        pe.wait_ge(pads_zero, 4)
        with pe.Fori(0, LAYERS) as layer:
            Place.layer = layer

            def small(name):
                a, b = SMALL2[name]
                return sm2[:, a:b]

            def up(st, k):
                n0, s0 = st.at["panels"], st.at["steps"]
                with pe.Fori(0, FT // 2) as turn_:
                    Place.turn = turn_
                    for j in range(2):
                        n, s = n0 + j, s0 + j
                        take(s)
                        for c in range(2):
                            o = feature_major(n, step_banks(s)[0][:, c * T:(c + 1) * T], c,
                                              lambda b: (act_x(ahi, 2, b, 0, T), act_x(alo, 2, b, 0, T)),
                                              inputs=(x_split, 8 * k_x(k), 1) if j == 0 and c == 0 else None)
                        o.then_inc(tick, 1)
                    Place.turn = None

            def down(st, first_hidden, k=None):
                for blkno in range(FT * D // PW):
                    n, b = st.at["panels"] + blkno // NB, blkno % NB
                    j, kt = blkno // FT, blkno % FT
                    s = st.at["steps"] + j
                    need(n, b // 4)
                    if kt == 0:
                        take(s)
                    if j == 0:
                        pe.wait_ge(hid_split, now(hid_split, first_hidden + kt + 1))
                    xh, xl = (x[:, H2 + kt * T:H2 + (kt + 1) * T] for x in (ahi, alo))
                    for c in range(2):
                        wh, wl = wblock(n, b, c * P, (c + 1) * P)
                        o = mm3(step_banks(s)[0][:, c * T:(c + 1) * T], wh, wl, xh, xl, kt == 0 and c == 0, kt == FT - 1)
                    if b == NB - 1 or kt == FT - 1:
                        o.then_inc(tick, 1)
                    if k is not None and j and kt == FT - 1:
                        norm_sums(k, (2 * j - 2, 2 * j - 1))
                if k is not None:
                    norm_sums(k, (6, 7))

            norm_sums(TWO["norm1"].at["norms"], range(KT))
            up(TWO["up1"], TWO["norm1"].at["norms"])
            down(TWO["down1"], 0, TWO["norm2"].at["norms"])
            def tok_panels(name, width=PW, which=None):
                st = TWO[name]
                for j in range(st.panels) if which is None else (which,):
                    n, s = st.at["panels"] + j, st.at["steps"] + j
                    take(s)
                    inputs = 8 * k_x(TWO["norm2"].at["norms"]) if name == "cmp_kv" else None
                    for tt in range(TT):
                        o = token_major(n, step_banks(s)[0][:, tt * PW:tt * PW + width], 2, tt, width,
                                        inputs if tt == 0 else None)
                    o.then_inc(tick, 1)

            tok_panels("cmp_kv")
            pe.wait_ge(rs_ready, now(rs_ready, 2))
            for tt in range(TT):
                o = pe.matmul(banks[7][:, T + 2 * tt:T + 2 * tt + 2], rs[:, tt * P:(tt + 1) * P], ident[:, 0:2],
                              start=True, stop=True, skip_group_check=True)
            o.then_inc(rcol_turned, 1)
            tok_panels("nsa_g", 24)
            b = TWO["cmp_kv"].at["turns"]
            pe.wait_ge(roped, now(roped, ROPED2 + 1))
            for tt in range(TT):
                turn(None, b, [work[:, 1024 + tt * 512 + i * P:1024 + tt * 512 + (i + 1) * P] for i in range(4)])
                b += 1
            tok_panels("nsa_q")
            tok_panels("nsa_kv")
            st = TWO["cmp_w1"]
            pe.wait_ge(cm_dve, now(cm_dve, 2))
            for j in range(2):
                n, s = st.at["panels"] + j, st.at["steps"] + j
                take(s)
                xs = [x[:, H2 + j * 512:H2 + (j + 1) * 512].rearrange("p (n j) -> p n j", j=16) for x in (ahi, alo)]
                for q in range(16):
                    need(n, q // 8)
                    o = mm3(step_banks(s)[0][:, 0:32], slot_hi(n, q * P, (q + 1) * P), slot_lo(n, q * P, (q + 1) * P),
                            xs[0][:, :, q], xs[1][:, :, q], q == 0, q == 15)
                o.then_inc(tick, 1)
            tok_panels("moba_qkv", which=0)
            pe.wait_ge(freed, now(freed, st.at["steps"] + 2))
            pe.matmul(banks[7][0:32, 0:HD], glu[:, 0:32], small("w2k"), start=True, stop=True).then_inc(cm_pe, 1)
            tok_panels("moba_qkv", which=1)
            pe.wait_ge(roped, now(roped, ROPED2 + 2))
            b = TWO["turn_nsa"].at["turns"]
            for tt in range(TT):
                turn(None, b, [tok[:, Q2 + tt * 512 + i * P:Q2 + tt * 512 + (i + 1) * P] for i in range(4)])
                b += 1
            tok_panels("moba_qkv", which=2)
            for tt in range(TT):
                turn(None, b, [work[:, 1024 + tt * 512 + i * P:1024 + tt * 512 + (i + 1) * P] for i in range(4)])
                b += 1
            pe.wait_ge(cm_dve, now(cm_dve, 3))
            pe.transpose(banks[7][:, 0:P], kct[:, P:2 * P], ident).then_inc(cm_pe, 1)
            tok_panels("moba_qkv", which=3)
            pe.wait_ge(turn_out, now(turn_out, b))
            pe.wait_ge(cm_act, now(cm_act, 3))
            qv = qT[:, :].rearrange("p (a t) -> p a t", a=4)
            for qt in range(TT):
                for p in range(NPAIR):
                    o = pe.matmul(banks[7][:, qt * P + p * 32:qt * P + (p + 1) * 32], qv[:, p, qt * P:(qt + 1) * P],
                                  kcp[:, (p // 2) * 32:(p // 2 + 1) * 32], start=True, stop=True, skip_group_check=True)
            o.then_inc(cm_pe, 1)
            tok_panels("moba_qkv", which=4)
            pe.wait_ge(cm_dve, now(cm_dve, 4))
            pe.matmul(banks[7][:, 256:256 + HD], glu[:, 32:32 + P], small("w2v"), start=True, stop=True,
                      skip_group_check=True).then_inc(cm_pe, 1)
            tok_panels("moba_qkv", which=5)
            pe.wait_ge(cm_dve, now(cm_dve, 5))
            for qt in range(TT):
                o = pe.transpose(banks[7][:, qt * P:(qt + 1) * P], cmpw[:, qt * P:(qt + 1) * P], ident)
            o.then_inc(cm_pe, 1)
            pe.wait_ge(roped, now(roped, ROPED2 + 3))
            b = TWO["turn_moba"].at["turns"]
            for c in range(2):
                for tt in range(TT):
                    a = M2 + tt * 1536 + c * 512
                    turn(None, b, [tok[:, a + i * P:a + (i + 1) * P] for i in range(4)])
                    b += 1
            pe.wait_ge(turn_out, now(turn_out, b))
            pe.wait_ge(cm_act, now(cm_act, 5))
            attention(2, None, False, TWO["attn"], TWO["moba_qkv"].at["steps"] + 6)
            st = TWO["merge"]
            at = TWO["attn"]
            pe.wait_ge(usplit, now(usplit, at.at["pairs"] + at.pairs))
            for j in range(4):
                for c in range(3):
                    n, s = st.at["panels"] + 3 * j + c, st.at["steps"] + 3 * j + c
                    take(s)
                    if c < 2:
                        for e in range(2):
                            o = feature_major(n, step_banks(s)[0][:, e * T:(e + 1) * T], e,
                                              lambda b: (act_x(ahi, 2, b, 0, T), act_x(alo, 2, b, 0, T)))
                    else:
                        for branch in range(2):
                            for e in range(2):
                                o = feature_major(n, step_banks(s)[branch][:, e * T:(e + 1) * T], e,
                                                  lambda b: tuple(x[:, H2 + b * T:H2 + (b + 1) * T] for x in (ahi, alo)),
                                                  range(4 * branch, 4 * branch + 4))
                    o.then_inc(tick, 1)
            st = TWO["out"]
            for j in range(4):
                n, s = st.at["panels"] + j, st.at["steps"] + j
                take(s)
                for e in range(2):
                    o = feature_major(n, step_banks(s)[0][:, e * T:(e + 1) * T], e,
                                      lambda b: tuple(x[:, H2 + 2048 + b * T:H2 + 2048 + (b + 1) * T] for x in (ahi, alo)),
                                      inputs=(m_split, TWO["merge"].at["merges"], 2) if j == 0 and e == 0 else None)
                o.then_inc(tick, 1)
                if j:
                    norm_sums(TWO["norm3"].at["norms"], (2 * j - 2, 2 * j - 1))
            norm_sums(TWO["norm3"].at["norms"], (6, 7))
            up(TWO["up2"], TWO["norm3"].at["norms"])
            down(TWO["down2"], FT)
            Place.layer = None
        norm(START2["norms"] + LAYERS * PER_LAYER["norms"], 2)


def columns(w, c0, width=PW):
    k = w.shape[0] // P
    return w[:, c0:c0 + width].reshape(k, P, width).transpose(1, 0, 2).reshape(P, k * width)


def weight_stream(a):
    out = np.zeros((PANELS + SPARE, P, PAN), np.float32)
    n = 0

    def put(*parts):
        nonlocal n
        c = 0
        for x in parts:
            out[n, :, c:c + x.shape[1]] = x
            c += x.shape[1]
        n += 1

    hb = NH * HD
    at = {"A": (0, hb, 0), "B": (768, 1280, 1), "C": (2304, 2816, 2)}
    for l in range(LAYERS):
        w_in, w_out = a["w_in"][l], a["w_out"][l]
        gate0 = w_in.shape[1] - 3 * hb

        def qkv(m):
            for j in range(QKV_PANELS[m]):
                put(columns(w_in, at[m][0] + j * PW))

        def gate(m):
            for j in range(2):
                put(columns(w_in, gate0 + at[m][2] * hb + j * PW))

        def wout(m):
            for j in range(2):
                put(columns(w_out[at[m][2] * hb:(at[m][2] + 1) * hb], j * 2 * PW, 2 * PW))

        for j in range(12):
            put(columns(a["ada_w"][l], j * PW))
        qkv("A")
        gate("A")
        qkv("B")
        wout("A")
        gate("B")
        qkv("C")
        wout("B")
        gate("C")
        wout("C")
    for l in range(LAYERS):
        w_in = a["w_in_2"][l]

        def ffn(which):
            wg, wu, wd = (a[f"ffn{which}_{x}_2"][l] for x in ("wg", "wu", "wd"))
            for j in range(FT):
                put(np.concatenate([wg[:, j * P:(j + 1) * P].reshape(KT, P, P), wu[:, j * P:(j + 1) * P].reshape(KT, P, P)], 2)
                    .transpose(1, 0, 2).reshape(P, PAN))
            blocks = np.concatenate([columns(wd, m * PW) for m in range(D // PW)], 1)
            for j in range(DOWN_PANELS):
                put(blocks[:, j * PAN:(j + 1) * PAN])

        ffn(1)
        kv0 = hb + 3 * NH
        put(columns(w_in, kv0))
        g = np.zeros((P, KT, PW), np.float32)
        g[:, :, 0:3 * NH] = w_in[:, hb:kv0].reshape(KT, P, 3 * NH).transpose(1, 0, 2)
        put(g.reshape(P, PAN))
        for j in range(2):
            put(columns(w_in, j * PW))
        for j in range(2):
            put(columns(w_in, kv0 + PW + j * PW))
        for x in ("cmpk_w1_2", "cmpv_w1_2"):
            put(a[x][l].reshape(16, P, P).transpose(1, 0, 2).reshape(P, PAN))
        moba0 = kv0 + 6 * P
        for j in range(6):
            put(columns(w_in, moba0 + j * PW))
        ga0 = moba0 + 3 * hb
        for j in range(4):
            put(columns(w_in, ga0 + j * PW))
            put(columns(w_in, ga0 + D + j * PW))
            put(columns(a["w_branch_nsa_2"][l], j * PW), columns(a["w_branch_moba_2"][l], j * PW))
        for j in range(4):
            put(columns(a["w_out_2"][l], j * PW))
        ffn(2)
    assert n == PANELS
    return out


def by_feature(v):
    return v.reshape(-1, P).T


def constants():
    c = np.zeros((P, NCONST), np.float32)

    def put(name, v, rows=P):
        a, b = CONST[name]
        c[0:rows, a:b] = v

    i, j = np.arange(P)[:, None], np.arange(P)[None, :]
    put("ident", np.eye(P))
    put("ones", np.full((P, P), 1.0 / D))
    put("tri_le", np.where(j <= i, 0.0, NEG))
    put("tri_ge", np.where(j >= i, 0.0, NEG))
    q = np.arange(T)
    col = q % GRID_W
    first = np.clip(col - NB_COLS // 2, 0, GRID_W - NB_COLS)
    near = (col[None, :] >= first[:, None]) & (col[None, :] < first[:, None] + NB_COLS)
    put("near", np.where(near, 0.0, NEG).reshape(TT, P, T).transpose(1, 0, 2).reshape(P, TT * T))
    theta = np.float32(10000.0)
    t = np.arange(T)
    nf = HD // 4
    fr = (theta ** (-np.arange(nf, dtype=np.float32) / np.float32(nf))).astype(np.float32)
    ang1 = np.concatenate([(t // GRID_W).astype(np.float32)[:, None] * fr, (t % GRID_W).astype(np.float32)[:, None] * fr], 1)
    inv = (theta ** (-np.arange(0, HD, 2, dtype=np.float32) / np.float32(HD))).astype(np.float32)
    ang2 = t.astype(np.float32)[:, None] * inv
    for k, ang in (("1", ang1), ("2", ang2)):
        for name, v in (("cos", np.cos(ang)), ("sin", np.sin(ang)), ("nsin", -np.sin(ang))):
            put(name + k, v.astype(np.float32).reshape(TT, P, HALF).transpose(1, 0, 2).reshape(P, TT * HALF))
    end = np.arange(NCMP) * 16 + 31
    angc = np.tile(end.astype(np.float32)[:, None] * inv, (2, 1))
    put("cosc", np.cos(angc), 32)
    put("sinc", np.sin(angc), 32)
    put("nsinc", -np.sin(angc), 32)
    ok = (end[None, :] <= q[:, None]) & (np.arange(NCMP) < NCMP - 1)[None, :]
    put("cmp_add", np.where(ok, 0.0, NEG).reshape(TT, P, NCMP).transpose(1, 0, 2).reshape(P, TT * NCMP))
    put("cmp_keep", ok.astype(np.float32).reshape(TT, P, NCMP).transpose(1, 0, 2).reshape(P, TT * NCMP))
    put("head_of", (np.arange(P)[:, None] // NCMP == np.arange(NH)[None, :]).astype(np.float32))
    sel = np.zeros((P, 2), np.float32)
    sel[[0, 2], 0] = 1.0
    sel[[1, 3], 1] = 1.0
    put("sel", sel)
    put("eps", np.full((P, 1), EPS))
    return c


def bias_tiles(rpb):
    t = np.arange(T)
    row, col = t // GRID_W, t % GRID_W
    dr = row[None, :] - row[:, None] + NB_ROWS - 1
    dc = np.clip(col[None, :] - col[:, None] + NB_COLS - 1, 0, 2 * NB_COLS - 2)
    tiles = rpb.reshape(LAYERS * NH, 2 * NB_ROWS - 1, 2 * NB_COLS - 1)[:, dr, dc]
    return tiles.reshape(LAYERS * NH, TT, P, T).transpose(0, 2, 1, 3).reshape(LAYERS * NH, P, TT * T)


def small_tiles(a):
    s1 = np.zeros((P, LAYERS, NSMALL1), np.float32)
    s2 = np.zeros((P, LAYERS, NSMALL2), np.float32)
    for l in range(LAYERS):
        for name, v in (("norm_w", by_feature(a["norm_w"][l])), ("ada_b", by_feature(a["ada_b"][l])),
                        ("qn", a["q_norm_a"][l][None]), ("kn", a["k_norm_a"][l][None]), ("sink", a["sink_c"][l][None])):
            s1[:, l, slice(*SMALL1[name])] = v
        for name, v in (("n1", by_feature(a["ffn1_norm_2"][l])), ("n2", by_feature(a["mix_norm_2"][l])),
                        ("n3", by_feature(a["ffn2_norm_2"][l])), ("w2k", a["cmpk_w2_2"][l]), ("w2v", a["cmpv_w2_2"][l])):
            s2[:, l, slice(*SMALL2[name])] = v
        for k, x in enumerate(("cmpk_pos_2", "cmpv_pos_2")):
            p0 = SMALL2["pos"][0] + 16 * k
            s2[:, l, p0:p0 + 16] = a[x][l].reshape(16, P).T
    g = np.zeros((P, NSMALLG), np.float32)
    g[:, 0:8], g[:, 8:16] = by_feature(a["final_norm_w"]), by_feature(a["final_norm_2"])
    g[:, 16:] = np.stack([by_feature(a["c"][0]), by_feature(a["c_ctx"])], 2).reshape(P, 2 * KT)
    return s1.reshape(P, -1), s2.reshape(P, -1), g


def kernel(**inputs):
    import concourse.bacc as bacc
    from concourse.bass_utils import run_bass_kernel_spmd

    a = {k: np.asarray(v) for k, v in inputs.items()}
    both = np.concatenate([a["x"][0].T.reshape(KT, P, T), a["ctx"][0].T.reshape(KT, P, T)], 2)
    s1, s2, sg = small_tiles(a)
    arrays = {"xin": both.transpose(1, 0, 2).reshape(P, -1), "small1": s1, "small2": s2, "smallg": sg,
              "consts": constants(), "rpb": bias_tiles(a["rpb_b"]), "weights": weight_stream(a)}
    arrays = {k: np.ascontiguousarray(v, dtype=np.float32) for k, v in arrays.items()}
    nc = bacc.Bacc("TRN2", target_bir_lowering=False, num_devices=1)
    t = {k: nc.dram_tensor(k, v.shape, F32, kind="ExternalInput").ap() for k, v in arrays.items()}
    out = nc.dram_tensor("out", (D, T), F32, kind="ExternalOutput").ap()
    with ExitStack() as ctx:
        program(nc, ctx, t["xin"], t["smallg"], t["small1"], t["small2"], t["consts"], t["rpb"], t["weights"], out)
    r = run_bass_kernel_spmd(nc, [arrays], core_ids=[0])
    return np.ascontiguousarray(r.results[0]["out"].T).reshape(1, T, D)
```

```python
from contextlib import ExitStack
from dataclasses import asdict, dataclass

import numpy as np

import concourse.bass as bass
from concourse import mybir

F32 = mybir.dt.float32
F32R = mybir.dt.float32r
ACT = mybir.ActivationFunctionType
ALU = mybir.AluOpType
AX = mybir.AxisListType

P = 128
D = 1024
KT = D // P
T = 256
TT = T // P
HD = 64
HALF = HD // 2
NH = 8
NPAIR = NH // 2
GRID_W = 64
NB_ROWS, NB_COLS = 8, 16
assert T // GRID_W <= NB_ROWS
LAYERS = 2
FF = 2816
FT = FF // P
NCMP = 16
PAN = 2048
PW = 256
NB = PAN // PW
EPS = 1e-6
TINY = 1e-30
NEG = -1e30

GATE_SLOTS = tuple(range(1, 24, 3))
MIX1 = ("A", "B", "C")
ADA_PANELS = 3 * D // PW
ADA_SLOTS = (2, 7, 12, 17)
QKV_PANELS = {"A": 3, "B": 6, "C": 3}
DOWN_PANELS = FT * D // PAN
DOWN_STEP_ENDS = [(m + 1) * FT for m in range(D // PW)]


@dataclass
class Stage:
    name: str
    layer: int
    panels: int = 0
    steps: int = 0
    ticks: int = 0
    units: int = 0
    groups: int = 0
    pairs: int = 0
    turns: int = 0
    norms: int = 0
    xtiles: int = 0
    merges: int = 0
    cmps: int = 0
    at: dict = None


COUNTED = ("panels", "steps", "ticks", "units", "groups", "pairs", "turns", "norms", "xtiles", "merges", "cmps")


def block1_stages(l):
    ctx = l == 0
    nq = 4 if ctx else 2

    def qkv(m):
        n = QKV_PANELS[m]
        return Stage("qkv" + m, l, panels=n, steps=n, ticks=n)

    def gate(m):
        return Stage("gate" + m, l, panels=2, steps=2, ticks=2)

    def wout(m):
        return Stage("wout" + m, l, panels=2, steps=4, ticks=4)

    def turn(m):
        return Stage("turn" + m, l, turns=nq + (4 if m == "B" else 2))

    def attn(m):
        return Stage("attn" + m, l, panels=ADA_PANELS // 3 if ctx else 0, ticks=ADA_PANELS // 3 if ctx else 0,
                     units=24 if ctx else 16, groups=12 if ctx else 8, pairs=8 if ctx else 4)

    ada = [Stage("ada", l, panels=ADA_PANELS, steps=ADA_PANELS, ticks=ADA_PANELS)] if ctx else []
    return [*ada, Stage("norm", l, norms=1, xtiles=8),
            qkv("A"), gate("A"), turn("A"), attn("A"),
            qkv("B"), wout("A"), gate("B"), turn("B"), attn("B"),
            qkv("C"), wout("B"), gate("C"), turn("C"), attn("C"), wout("C")]


def block2_stages():
    down = Stage("down1", 0, panels=DOWN_PANELS, steps=4, ticks=DOWN_PANELS + 3)
    return [Stage("norm1", 0, norms=1, xtiles=8), Stage("up1", 0, panels=FT, steps=FT, ticks=FT), down,
            Stage("norm2", 0, norms=1, xtiles=8),
            Stage("cmp_kv", 0, panels=1, steps=1, ticks=1, turns=2),
            Stage("nsa_g", 0, panels=1, steps=1, ticks=1), Stage("nsa_q", 0, panels=2, steps=2, ticks=2),
            Stage("nsa_kv", 0, panels=4, steps=4, ticks=4),
            Stage("moba_qkv", 0, panels=6, steps=6, ticks=6),
            Stage("turn_nsa", 0, turns=4), Stage("cmp_attn", 0, cmps=1),
            Stage("turn_moba", 0, turns=4),
            Stage("attn", 0, panels=2 * D // PW, ticks=2 * D // PW, units=24, groups=12, pairs=8),
            Stage("merge", 0, panels=D // PW, steps=D // PW, ticks=D // PW, merges=4),
            Stage("out", 0, panels=4, steps=4, ticks=4),
            Stage("norm3", 0, norms=1, xtiles=8), Stage("up2", 0, panels=FT, steps=FT, ticks=FT),
            Stage("down2", 0, panels=DOWN_PANELS, steps=4, ticks=DOWN_PANELS + 3)]


def plan():
    one = {}
    at = dict.fromkeys(COUNTED, 0)
    for l in range(LAYERS):
        for s in block1_stages(l):
            s.at = dict(at)
            one[s.name, l] = s
            uses = asdict(s)
            for c in COUNTED:
                at[c] += uses[c]
    at["norms"] += 1
    two = {}
    start = dict(at)
    for s in block2_stages():
        s.at = dict(at)
        two[s.name] = s
        uses = asdict(s)
        for c in COUNTED:
            at[c] += uses[c]
    per_layer = {c: at[c] - start[c] for c in COUNTED}
    return one, two, start, per_layer


ONE, TWO, START2, PER_LAYER = plan()


def tick_tables():
    of_panel, of_step = {}, {}
    for s in [*ONE.values(), *TWO.values()]:
        p, q, t = s.at["panels"], s.at["steps"], s.at["ticks"]
        if s.name.startswith("down"):
            ends = sorted({*DOWN_STEP_ENDS, *((i + 1) * NB for i in range(DOWN_PANELS))})
            for i in range(DOWN_PANELS):
                of_panel[p + i] = t + ends.index((i + 1) * NB) + 1
            for i, e in enumerate(DOWN_STEP_ENDS):
                of_step[q + i] = t + ends.index(e) + 1
            assert len(ends) == s.ticks
            continue
        for i in range(s.panels):
            of_panel[p + i] = t + (i + 1) * s.ticks // s.panels
        for i in range(s.steps):
            of_step[q + i] = t + i + 1
    return of_panel, of_step


PANEL_TICK, STEP_TICK = tick_tables()



def k_x(k):
    return k if k < LAYERS else k - 1


def qkv_places(mixer, j):
    if mixer == "B":
        return [((Q1, K1, V1)[j // 2], (j % 2) * PW, 0, PW)]
    return [(Q1, j * PW, 0, PW)] if j < 2 else [(K1, 0, 0, P), (V1, 0, P, P)]


def bcast(ap, axis, n):
    dims = [list(d) for d in ap.ap]
    return bass.AP(ap.tensor, ap.offset, dims[:axis] + [[0, n]] + dims[axis:])


ROPED2 = 2 * LAYERS
X_DONE2 = LAYERS + 1
OUT_DONE = X_DONE2 + 3 * LAYERS + 1
DVE_START2, DVE_LAYER = 325, 92
PANELS = START2["panels"] + LAYERS * PER_LAYER["panels"]
SPARE = 2
assert START2["panels"] % 2 == 0 and PER_LAYER["panels"] % 2 == 0
assert START2["steps"] % 2 == 0 and PER_LAYER["steps"] % 2 == 0

CONST = {}
_at = 0
for _name, _n in (("ident", P), ("ones", P), ("tri_le", P), ("tri_ge", P), ("near", 2 * T),
                  ("cos1", TT * HALF), ("sin1", TT * HALF), ("nsin1", TT * HALF),
                  ("cos2", TT * HALF), ("sin2", TT * HALF), ("nsin2", TT * HALF),
                  ("cosc", HALF), ("sinc", HALF), ("nsinc", HALF),
                  ("cmp_add", TT * NCMP), ("cmp_keep", TT * NCMP), ("head_of", NH), ("sel", 2), ("eps", 1)):
    CONST[_name] = (_at, _at + _n)
    _at += _n
NCONST = _at
SMALL1 = {"norm_w": (0, 8), "ada_b": (8, 32), "qn": (32, 96), "kn": (96, 160), "sink": (160, 168)}
NSMALL1 = 168
SMALL2 = {"n1": (0, 8), "n2": (8, 16), "n3": (16, 24), "pos": (24, 56), "w2k": (56, 120), "w2v": (120, 184)}
NSMALL2 = 184
NSMALLG = 16 + 2 * KT

Q1, K1, V1 = 0, 2048, 4096
Q2, KC2, KS2, VS2, M2 = 0, 1024, 1536, 2048, 2560
PT0 = 0


def program(nc, ctx, xin, smallg, small1, small2, consts, rpb, weights, out):
    def sb(name, cols, dt=F32):
        return ctx.enter_context(nc.sbuf_tensor(name, [P, cols], dt))

    def sem(name):
        return ctx.enter_context(nc.semaphore(name))

    raw = sb("raw_panels", 2 * PAN)
    whi = sb("panels_hi", 2 * PAN, F32R)
    wlo = sb("panels_lo", 2 * PAN, F32R)
    xT = sb("xT", KT * 2 * T)
    NACT = 2048 + FT * T
    ahi = sb("acts_hi", NACT, F32R)
    alo = sb("acts_lo", NACT, F32R)
    tok = sb("token_major", 3 * 2048)
    work = sb("work", 2048)
    qT = sb("qT", 2048)
    kP = sb("kT_padded", 4096)
    gates = sb("gates", 2048)
    bias = sb("near_bias", 2 * 512)
    cst = sb("consts_sb", NCONST)
    sm1 = sb("small1_sb", LAYERS * NSMALL1)
    sm2all = sb("small2_layers", LAYERS * NSMALL2)
    sm2 = sb("small2_sb", NSMALL2)
    smg = sb("smallg_sb", NSMALLG)
    mod = sb("modulation", LAYERS * 48)
    moda = sb("modulation_scale", LAYERS * 16)
    rs = sb("token_scale", T)
    rcol = sb("token_scale_columns", 2)
    warm = sb("table_scratch", 1)
    stats = sb("softmax_stats", 3 * 8)
    hstat = sb("head_stats", 40)
    gT = sb("branch_gates", 48)
    cmpw = sb("cmp_work", 256)
    cstat = sb("cmp_stats", 16)
    pcT = gates[:, 1280:1280 + T]
    vblk = gates[:, 1536:1536 + 4 * P]
    kcp = sb("cmp_keys", 4 * NCMP)
    glu = sb("cmp_hidden", 32 + P)
    kct = sb("cmp_keys_tok", 2 * P)
    banks = [ctx.enter_context(nc.psum_tensor(f"bank{i}", [P, 512], F32)) for i in range(8)]

    def const(name, rows=slice(0, P)):
        a, b = CONST[name]
        return cst[rows, a:b]

    ident, ones, eps = const("ident"), const("ones"), const("eps")

    loaded = [sem(f"panel_loaded{i}") for i in range(2)]
    hi_ready, lo_ready = sem("panel_hi_ready"), sem("panel_lo_ready")
    tick = sem("pe_panel_or_step_done")
    freed = sem("projection_banks_freed")
    c_in = sem("c_in")
    inputs_in = [sem(f"inputs_in{i}") for i in range(4)]
    consts_in, small2_in, bias_in = sem("consts_in"), sem("layer_weights_ready"), sem("bias_in")
    pads_zero = sem("pads_zero")
    sq_ready, sq_used = sem("squares_ready"), sem("squares_summed")
    std_ready, tile_ready = sem("std_ready"), sem("tile_ready_to_round")
    rs_ready, rcol_turned, rcol_ready = sem("token_scale_ready"), sem("token_scale_turned"), sem("token_scale_columns_ready")
    table_in, hid_gated = sem("silu_table_loaded"), sem("hidden_gated")
    xhi_ready, x_split = sem("x_hi_ready"), sem("x_split_ready")
    c_silu, c_hi, c_split = sem("c_silu"), sem("c_hi"), sem("c_split_ready")
    row_out, row_turned = sem("modulation_row_out"), sem("modulation_row_turned")
    mod_cols, mod_ready = sem("mod_columns"), sem("mod_ready")
    hs_sum, hs_std = sem("head_squares_summed"), sem("head_std_ready")
    roped = sem("queries_keys_ready")
    turned, turn_out = sem("turned"), sem("turned_out")
    scores, negmax, exped, normed = sem("scores"), sem("negmax"), sem("exped"), sem("probs_normed")
    probT, probT_out, pv = sem("probs_turned"), sem("probs_turned_out"), sem("values_added")
    omul, uhi, usplit = sem("heads_gated"), sem("u_hi_ready"), sem("u_split_ready")
    biased = sem("near_bias_masked")
    bias_used = sem("near_bias_used")
    silu_ready, hhi_ready, hid_split = sem("silu_ready"), sem("hid_hi"), sem("hidden_split")
    merge_scaled, merge_gate = sem("merge_gate_scaled"), sem("merge_gate_ready")
    merged, mhi_ready, m_split = sem("merged"), sem("merged_hi"), sem("merged_split")
    cm_pe, cm_act, cm_dve = sem("cmp_pe"), sem("cmp_act"), sem("cmp_dve")
    x_done = sem("residual_done")
    dve_chain, act_chain = sem("dve_chain"), sem("act_chain")
    stored = sem("stored")

    L = PER_LAYER
    grows = {
        loaded[0]: (16 * L["panels"] // 2, 16), loaded[1]: (16 * L["panels"] // 2, 16),
        hi_ready: (2 * L["panels"], 4), lo_ready: (2 * L["panels"], 4),
        tick: (L["ticks"], 2), freed: (L["steps"], 2),
        sq_ready: (8 * L["norms"], 0), sq_used: (8 * L["norms"], 0), std_ready: (L["norms"], 0),
        rs_ready: (3, 0), rcol_turned: (1, 0), rcol_ready: (1, 0),
        table_in: (FT, 1), hid_gated: (2 * FT, 2), xhi_ready: (8 * L["norms"], 0), x_split: (8 * L["norms"], 0),
        small2_in: (1, 0), turned: (L["turns"], 0), turn_out: (L["turns"], 0),
        scores: (L["units"], 0), negmax: (L["units"], 0), exped: (L["units"], 0), normed: (L["units"], 0),
        probT: (L["units"], 0), probT_out: (L["units"], 0), pv: (L["groups"], 0),
        omul: (L["pairs"], 0), uhi: (L["pairs"], 0), usplit: (L["pairs"], 0), roped: (3, 0),
        silu_ready: (2 * FT, 2), hhi_ready: (2 * FT, 2), hid_split: (2 * FT, 2),
        merge_scaled: (8, 0), merge_gate: (8, 0), merged: (L["merges"], 0), mhi_ready: (L["merges"], 0), m_split: (L["merges"], 0),
        cm_pe: (5, 0), cm_act: (5, 0), cm_dve: (5, 0), x_done: (3, 0), dve_chain: (DVE_LAYER, 0),
    }

    class Place:
        layer = None
        turn = None

    def now(s, n):
        if Place.layer is not None:
            n = n + Place.layer * grows[s][0]
        if Place.turn is not None and grows[s][1]:
            n = n + Place.turn * grows[s][1]
        return n

    class Chain:

        def __init__(self, s):
            self.s, self.n = s, 0

        def next(self):
            self.n += 1
            return now(self.s, self.n)

    def slot_hi(n, a, b):
        return whi[:, (n % 2) * PAN + a:(n % 2) * PAN + b]

    def slot_lo(n, a, b):
        return wlo[:, (n % 2) * PAN + a:(n % 2) * PAN + b]

    def step_banks(s):
        return banks[2 * (s % 2)], banks[2 * (s % 2) + 1]

    def tile4(ap, n):
        return ap.rearrange("p (a b) -> p a b", a=n)

    def x_of(kt, t0=0, t1=T):
        return xT[:, kt * 2 * T + t0:kt * 2 * T + t1]

    XW = {1: 2 * T, 2: T}

    def act_x(part, blk, kt, t0, t1):
        return part[:, kt * XW[blk] + t0:kt * XW[blk] + t1]

    CP = 6144
    MOD_COLS = 512 - 4 * ADA_PANELS
    U1 = 8 * 2 * T
    H2 = 8 * T

    @dataclass
    class Unit:
        q: object
        keys: list
        segs: list
        masks: list
        blocks: list
        qt: int
        group: int

    @dataclass
    class Group:
        adds: list
        pair: int
        last: bool
        cmp: bool = False
        head: object = None

    def attention_plan(blk, mixer, with_ctx):
        units, groups, pairs = [], [], []
        qv = qT[:, :].rearrange("p (a t) -> p a t", a=4)

        def val(tt, col):
            base = V1 + tt * 512 + col
            return tok[:, base:base + HD]

        if blk == 1:
            kv = kP[:, :].rearrange("p (i t) -> p i t", i=8)
            gqa = mixer != "B"
            for h in range(NH):
                idx = 2 * (h // 4) + h % 2 if gqa else h
                vcol = (h // 4 if gqa else h) * HD
                for qt in range(TT):
                    masks = []
                    if mixer == "C":
                        masks = [(P, P, 1, const("tri_le"))] if qt == 0 else [(0, P, 1, const("tri_ge"))]
                    if mixer == "B":
                        masks = [(0, T, 1, ("bias", h, qt))]
                    units.append(Unit(qv[:, h // 2, qt * P:(qt + 1) * P], [(kv[:, idx, :], 0, 512)],
                                      [(0, 512, h if mixer == "C" else None, None)], masks,
                                      [(b * P, b) for b in range(4)], qt, len(groups)))
                groups.append(Group([(h % 2, val(b, vcol), b, 0, b == 0) for b in range(4)], len(pairs), h % 2 == 1, head=h))
                if h % 2:
                    pairs.append((h // 2, 0))
            if with_ctx:
                for p in range(NPAIR):
                    for qt in range(TT):
                        keys, segs, blocks = [], [], []
                        for e in range(2):
                            h = 2 * p + e
                            idx = 2 * (h // 4) + h % 2 if gqa else h
                            keys.append((kv[:, idx, T:2 * T], e * T, T))
                            segs.append((e * T, T, h if mixer == "C" else None, None))
                            blocks += [(e * T + b * P, 2 * e + b) for b in range(2)]
                        units.append(Unit(qv[:, p, T + qt * P:T + (qt + 1) * P], keys, segs, [], blocks, qt, len(groups)))
                    adds = []
                    for e in range(2):
                        h = 2 * p + e
                        vcol = (h // 4 if gqa else h) * HD
                        adds += [(e, val(2 + b, vcol), 2 * e + b, 0, b == 0) for b in range(2)]
                    groups.append(Group(adds, len(pairs), True))
                    pairs.append((p, 1))
            return units, groups, pairs
        kv = kP[:, :].rearrange("p (i t) -> p i t", i=16)

        def causal_adds(e, vals, kind, started):
            return [(e, vals[b], 2 * kind + b, b * P, b == 0 and kind == 0 and not started) for b in range(2)]

        for h in range(NH):
            g = h // 4
            for qt in range(TT):
                w = (qt + 1) * P
                units.append(Unit(qv[:, h // 2, 0 + qt * P:(qt + 1) * P],
                                  [(kv[:, 4 * k + 2 * g + h % 2, 0:w], k * T, w) for k in range(2)],
                                  [(k * T, w, None, (qt, 3 * h + 1 + k)) for k in range(2)],
                                  [(qt * P, P, 2, const("tri_le"))],
                                  [(k * T + b * P, 2 * k + b) for k in range(2) for b in range(qt + 1)], qt, len(groups)))
            adds = []
            for k in range(2):
                vals = [tok[:, VS2 + b * 256 + k * P + g * HD:VS2 + b * 256 + k * P + (g + 1) * HD] for b in range(2)]
                adds += causal_adds(h % 2, vals, k, True)
            groups.append(Group(adds, len(pairs), h % 2 == 1, cmp=h % 2 == 0))
            if h % 2:
                pairs.append((h // 2, 0))
        for p in range(NPAIR):
            for qt in range(TT):
                w = (qt + 1) * P
                units.append(Unit(qv[:, p, T + qt * P:T + (qt + 1) * P],
                                  [(kv[:, 8 + 2 * p + e, 0:w], e * T, w) for e in range(2)],
                                  [(e * T, w, None, None) for e in range(2)],
                                  [(qt * P, P, 2, const("tri_le"))],
                                  [(e * T + b * P, 2 * e + b) for e in range(2) for b in range(qt + 1)], qt, len(groups)))
            adds = []
            for e in range(2):
                c = M2 + 1024 + (2 * p + e) * HD
                vals = [tok[:, c + b * 1536:c + b * 1536 + HD] for b in range(2)]
                adds += [(e, vals[b], 2 * e + b, b * P, b == 0) for b in range(2)]
            groups.append(Group(adds, len(pairs), True))
            pairs.append((p, 1))
        return units, groups, pairs

    def last_unit_of(units, g):
        return max(i for i, u in enumerate(units) if u.group == g)

    def merge_gate_place(r):
        j = r // 2
        if r % 2 == 0:
            return xT[:, :].rearrange("p (k t) -> p k t", k=KT)[:, 2 * j:2 * j + 2, T:2 * T]
        return tile4((gates[:, 0:512], gates[:, 512:1024], tok[:, M2 + 3072:M2 + 3584], tok[:, M2:M2 + 512])[j], 2)

    def head_part(j, wctx):
        return (Q1, j * PW, 4, 4 if wctx else 2) if j < 2 else (K1, 0, 2, 4)

    def head_stats(j, wctx):
        _, _, heads, tiles = head_part(j, wctx)
        return hstat[:, 16 * j:16 * j + heads * tiles]

    def score_bank(u):
        return banks[u % 3]

    def prob_bank(u):
        return banks[3 + u % 2]

    def out_bank(p):
        return banks[5 + p % 2]

    def turn_bank(b):
        return banks[5 + b % 2]

    def probs(u):
        return work[:, (u % 3) * 512:(u % 3) * 512 + 512]

    def probsT(g):
        return tok[:, PT0 + (g % 2) * 1024:PT0 + (g % 2) * 1024 + 1024].rearrange("p (b q) -> p b q", b=4)

    def gated(p):
        return work[:, 1536 + (p % 2) * T:1536 + (p % 2) * T + T]

    def gate_of(blk, pair):
        i, c = pair
        return gates[:, i * 512 + c * T:i * 512 + c * T + T]

    def u_of(part, blk, pair):
        i, c = pair
        if blk == 1:
            return part[:, U1 + i * 512 + c * T:U1 + i * 512 + c * T + T]
        return part[:, H2 + c * 1024 + i * T:H2 + c * 1024 + (i + 1) * T]

    block = ctx.enter_context(nc.Block())

    @block.sync
    def _(sp):
        for n in range(2):
            sp.dma_start(raw[:, n * PAN:(n + 1) * PAN], weights[n]).then_inc(loaded[n], 16)
        with sp.Fori(1, (PANELS + SPARE) // 2) as i:
            for j in range(2):
                sp.wait_ge(lo_ready, 4 * i + 2 * j - 2)
                sp.dma_start(raw[:, j * PAN:(j + 1) * PAN], weights[2 * i + j]).then_inc(loaded[j], 16)
        sp.wait_ge(x_done, OUT_DONE)
        sp.dma_start(out.rearrange("(k p) t -> p k t", p=P),
                     xT[:, :].rearrange("p (k t) -> p k t", k=KT)[:, :, 0:T]).then_inc(stored, 16)
        sp.wait_ge(stored, 16)

    @block.gpsimd
    def _(pool):
        pool.dma_start(smg[:, :], smallg).then_inc(c_in, 16)
        pool.dma_start(cst[:, :], consts).then_inc(consts_in, 16)
        pool.dma_start(sm1[:, :], small1).then_inc(consts_in, 16)
        pool.dma_start(sm2all[:, :], small2).then_inc(consts_in, 16)
        pool.memset(kP[:, :], 0.0).then_inc(pads_zero, 1)
        pool.memset(kct[:, :], 0.0)
        pool.memset(kcp[:, :], 0.0).then_inc(pads_zero, 1)
        for i in range(4):
            if i >= 1:
                pool.wait_ge(tick, 2 * i - 1)
            pool.dma_start(xT[:, i * 4 * T:(i + 1) * 4 * T], xin[:, i * 4 * T:(i + 1) * 4 * T]).then_inc(inputs_in[i], 16)
        pool.wait_ge(consts_in, 48)
        for l in range(LAYERS):
            for h in range(NH):
                n = l * NH + h
                if n >= 2:
                    pool.wait_ge(bias_used, 2 * (n - 1))
                buf = bias[:, (n % 2) * 512:(n % 2) * 512 + 512]
                pool.dma_start(buf, rpb[n]).then_inc(bias_in, 16)
                pool.wait_ge(bias_in, 16 * (n + 1))
                pool.tensor_tensor(buf, buf, const("near"), ALU.add).then_inc(biased, 1)
        pool.wait_ge(x_done, LAYERS)
        kv = kP[:, :].rearrange("p (i t) -> p i t", i=16)
        pool.memset(kv[HD:P, 0:16:2, :], 0.0).then_inc(pads_zero, 1)
        pool.memset(kv[0:HD, 1:16:2, :], 0.0).then_inc(pads_zero, 1)

    @block.scalar
    def _(act):
        chain = Chain(act_chain)
        Place.layer = Place.turn = None

        def round_half(n, h):
            if h == 0:
                act.wait_ge(loaded[n % 2], now(loaded[n % 2], 16 * (n // 2 + 1)))
                if n >= 2:
                    act.wait_ge(tick, now(tick, PANEL_TICK[n - 2]))
            a, b = h * PAN // 2, (h + 1) * PAN // 2
            act.activation(slot_hi(n, a, b), raw[:, (n % 2) * PAN + a:(n % 2) * PAN + b], ACT.Copy).then_inc(hi_ready, 1)

        def round_panel(n):
            round_half(n, 0)
            round_half(n, 1)

        def begin(s):
            act.wait_ge(tick, now(tick, STEP_TICK[s]))
            if s >= 1:
                act.wait_ge(freed, now(freed, s))

        def square(k, blk, kt):
            w = XW[blk]
            if kt >= 2:
                act.wait_ge(sq_used, now(sq_used, 8 * k + kt - 1))
            act.activation(work[:, (kt % 2) * 512:(kt % 2) * 512 + w], x_of(kt, 0, w), ACT.Square).then_inc(sq_ready, 1)

        def root(k, blk):
            w = XW[blk]
            act.wait_ge(sq_used, now(sq_used, 8 * k + 8))
            act.activation(work[:, 1024:1024 + w], banks[7][:, 0:w], ACT.Sqrt, bias=eps).then_inc(std_ready, 1)

        def modulate(k, l):
            act.wait_ge(mod_ready, l + 1)
            for kt in range(KT + 1):
                if kt < KT:
                    buf = gates[:, (kt % 4) * 512:(kt % 4) * 512 + 512]
                    act.wait_ge(tile_ready, 8 * k + kt + 1)
                    for c in range(2):
                        i = kt * 2 + c
                        y = act.activation(buf[:, c * T:(c + 1) * T], buf[:, c * T:(c + 1) * T], ACT.Identity,
                                           scale=moda[:, l * 16 + i:l * 16 + i + 1], bias=mod[:, l * 48 + i:l * 48 + i + 1])
                    y.then_inc(act_chain, 1)
                if kt > 0:
                    buf = gates[:, ((kt - 1) % 4) * 512:((kt - 1) % 4) * 512 + 512]
                    act.wait_ge(act_chain, chain.n + kt)
                    act.activation(act_x(ahi, 1, kt - 1, 0, 512), buf, ACT.Copy).then_inc(xhi_ready, 1)
            chain.n += KT

        def norm_hi(weight, tiles):
            for kt in tiles:
                act.activation(act_x(ahi, 2, kt, 0, T), x_of(kt), ACT.Identity,
                               scale=weight[:, kt:kt + 1]).then_inc(xhi_ready, 1)

        def norm_root(k):
            act.wait_ge(sq_used, now(sq_used, 8 * k + 8))
            act.activation(rs[:, :], banks[7][:, 0:T], ACT.Sqrt, bias=eps).then_inc(std_ready, 1)

        def attention(blk, mixer, with_ctx, st):
            units, groups, pairs = attention_plan(blk, mixer, with_ctx)
            u0, g0, p0 = st.at["units"], st.at["groups"], st.at["pairs"]
            for i in range(len(units) + 7):
                for r, slot in enumerate(ADA_SLOTS if st.panels and blk == 1 else ()):
                    n, row = st.at["panels"] + r, MIX1.index(mixer) * len(ADA_SLOTS) + r
                    if i == slot + 1:
                        round_half(n + 2, 0)
                        if row:
                            act.wait_ge(row_turned, row)
                        act.activation(cmpw[0:4, 0:PW], banks[7][0:4, 0:PW], ACT.Copy).then_inc(row_out, 1)
                    if i == slot + 2:
                        round_half(n + 2, 1)
                for r, slot in enumerate(GATE_SLOTS if blk == 2 else ()):
                    for h in range(2):
                        if i == slot + 2 + h:
                            round_half(st.at["panels"] + r + 2, h)
                j = i - 3
                if 0 <= j < len(units):
                    un, u = units[j], u0 + j
                    act.wait_ge(probT, now(probT, u + 1))
                    if g0 + un.group - 1 >= 1:
                        act.wait_ge(pv, now(pv, g0 + un.group - 1))
                    w = len(un.blocks) * P
                    dst = probsT(g0 + un.group)[:, :, un.qt * P:(un.qt + 1) * P]
                    src = prob_bank(u)[:, :].rearrange("p (b q) -> p b q", b=4)
                    if len(un.blocks) < 4:
                        dst, src = dst[:, 0:4:2, :], src[:, 0:4:2, :]
                    act.activation(dst, src, ACT.Copy).then_inc(probT_out, 1)
                if i < len(units):
                    un, u = units[i], u0 + i
                    act.wait_ge(negmax, now(negmax, u + 1))
                    if u - 2 >= 1:
                        act.wait_ge(probT, now(probT, u - 2))
                    sbase = (u % 3) * 8
                    for k, (c, w, sink, _) in enumerate(un.segs):
                        if sink is not None:
                            a = SMALL1["sink"][0] + st.layer * NSMALL1 + sink
                            act.activation(stats[:, sbase + 6 + k:sbase + 7 + k], sm1[:, a:a + 1], ACT.Exp,
                                           bias=stats[:, sbase + k:sbase + k + 1])
                        e = act.activation(probs(u)[:, c:c + w], score_bank(u)[:, c:c + w], ACT.Exp,
                                           bias=stats[:, sbase + k:sbase + k + 1],
                                           accum_out=stats[:, sbase + 2 + k:sbase + 3 + k])
                        if k == len(un.segs) - 1:
                            e.then_inc(exped, 1)
                j = i - 6
                if 0 <= j < len(units) and last_unit_of(units, units[j].group) == j and groups[units[j].group].last:
                    pr = groups[units[j].group].pair
                    act.wait_ge(omul, now(omul, p0 + pr + 1))
                    act.activation(u_of(ahi, blk, pairs[pr]), gated(p0 + pr), ACT.Copy).then_inc(uhi, 1)

        def turns(b, top, bottom, scale=1.0):
            act.wait_ge(turned, now(turned, b + 1))
            for k, (dst, src) in enumerate([x for x in (top, bottom) if x is not None]):
                m = act.activation(dst, src, ACT.Copy, scale=scale)
            m.then_inc(turn_out, 1)

        round_panel(0)
        act.wait_ge(c_in, 16)
        cc = smg[:, 16:16 + 2 * KT]
        cs = cmpw[:, 0:2 * KT]
        act.activation(cs, cc, ACT.Silu).then_inc(act_chain, 1)
        act.wait_ge(act_chain, chain.next())
        cpad = ahi[:, CP:CP + KT * P].rearrange("p (k m) -> p k m", k=KT)
        act.wait_ge(c_split, 1)
        act.activation(cpad[:, :, 0:2], tile4(cs, KT), ACT.Copy).then_inc(c_hi, 1)
        round_panel(1)

        for l in range(LAYERS):
            wctx = l == 0
            nq = 4 if wctx else 2
            k = ONE["norm", l].at["norms"]
            if wctx:
                st = ONE["ada", l]
                for j in range(ADA_PANELS):
                    n, s = st.at["panels"] + j, st.at["steps"] + j
                    round_panel(n + 2)
                    begin(s)
                    act.activation(tok[0:4, j * PW:(j + 1) * PW], step_banks(s)[0][0:4, 0:PW], ACT.Copy).then_inc(freed, 1)
                    if 2 <= j < KT + 2:
                        act.wait_ge(inputs_in[(j - 2) // 2], 16)
                        square(k, 1, j - 2)
                act.wait_ge(consts_in, 48)
            else:
                for kt in range(KT):
                    act.wait_ge(freed, ONE["woutC", l - 1].at["steps"] + kt // 2 + 1)
                    square(k, 1, kt)
            root(k, 1)
            modulate(k, l)
            for m in MIX1:
                def qkv(m):
                    st = ONE["qkv" + m, l]
                    for j in range(st.panels):
                        n, s = st.at["panels"] + j, st.at["steps"] + j
                        round_panel(n + 2)
                        begin(s)
                        kinds = qkv_places(m, j)
                        full = kinds[0][0] != Q1 or wctx
                        for c in range(2 if full else 1):
                            bk = step_banks(s)[c][:, :].rearrange("p (t w) -> p t w", t=2)
                            for a, w, (sec, col) in [(x[2], x[3], (x[0], x[1])) for x in kinds]:
                                dst = tok[:, sec:sec + 2048].rearrange("p (t w) -> p t w", t=4)[:, 2 * c:2 * c + 2, col:col + w]
                                e = act.activation(dst, bk[:, :, a:a + w], ACT.Copy)
                        e.then_inc(freed, 1)
                        if m == "A":
                            act.wait_ge(hs_sum, 3 * l + j + 1)
                            h = head_stats(j, wctx)
                            act.activation(h, h, ACT.Sqrt, scale=1.0 / HD, bias=eps).then_inc(hs_std, 1)

                def wout(m):
                    st = ONE["wout" + m, l]
                    for j in range(2):
                        round_panel(st.at["panels"] + j + 2)

                def gate(m):
                    st = ONE["gate" + m, l]
                    for j in range(2):
                        n, s = st.at["panels"] + j, st.at["steps"] + j
                        round_panel(n + 2)
                        begin(s)
                        w = 2 * T if wctx else T
                        for c in range(2):
                            i = 2 * j + c
                            e = act.activation(gates[:, i * 512:i * 512 + w], step_banks(s)[c][:, 0:w], ACT.Silu)
                        e.then_inc(freed, 1)

                if m == "A":
                    qkv("A")
                gate(m)
                st = ONE["turn" + m, l]
                b = st.at["turns"]
                qv = qT[:, :].rearrange("p (a t) -> p a t", a=4)
                kv = kP[:, :].rearrange("p (i t) -> p i t", i=8)
                for tt in range(nq):
                    turns(b, (qv[:, :, tt * P:(tt + 1) * P], tile4(turn_bank(b)[:, :], 4)), None, HD ** -0.5)
                    b += 1
                if m == "B":
                    for tt in range(4):
                        src = tile4(turn_bank(b)[:, :], 4)
                        turns(b, (kv[0:HD, 0:8:2, tt * P:(tt + 1) * P], src[0:HD]),
                              (kv[HD:P, 1:8:2, tt * P:(tt + 1) * P], src[HD:P]))
                        b += 1
                else:
                    for c in range(2):
                        src = turn_bank(b)[:, :].rearrange("p (g t) -> p g t", g=2)
                        turns(b, (kv[0:HD, 0:4:2, 2 * c * P:2 * (c + 1) * P], src[0:HD]),
                              (kv[HD:P, 1:4:2, 2 * c * P:2 * (c + 1) * P], src[HD:P]))
                        b += 1
                attention(1, m, wctx, ONE["attn" + m, l])
                if m == "A":
                    qkv("B")
                    wout("A")
                if m == "B":
                    qkv("C")
                    wout("B")
                if m == "C":
                    wout("C")

        for kt in range(KT):
            act.wait_ge(freed, ONE["woutC", LAYERS - 1].at["steps"] + kt // 2 + 1)
            square(START2["norms"] - 1, 2, kt)
        root(START2["norms"] - 1, 2)

        with act.Fori(0, LAYERS) as layer:
            Place.layer = layer
            def small(name):
                a, b = SMALL2[name]
                return sm2[:, a:b]

            def up(st, first_hidden):
                s0, n0 = st.at["steps"], st.at["panels"]
                with act.Fori(0, FT // 2) as turn:
                    Place.turn = turn
                    act.activation(warm[:, :], eps, ACT.Silu).then_inc(table_in, 1)
                    act.wait_ge(table_in, now(table_in, first_hidden // 2 + 1))
                    for j in range(2):
                        n, s, a = n0 + j, s0 + j, first_hidden + j
                        gu = work[:, (j % 2) * 512:(j % 2) * 512 + 512]
                        round_half(n + 2, 0)
                        act.wait_ge(freed, now(freed, s + 1))
                        act.activation(gu[:, 0:T], gu[:, 0:T], ACT.Silu).then_inc(silu_ready, 1)
                        round_half(n + 2, 1)
                        act.wait_ge(hid_gated, now(hid_gated, a + 1))
                        dst = ahi[:, H2:H2 + FT * T].rearrange("p (f t) -> p f t", f=FT)[:, 2 * turn + j, :]
                        act.activation(dst, gu[:, T:2 * T], ACT.Copy).then_inc(hhi_ready, 1)
                    Place.turn = None

            def down(st, next_weight=None):
                for n in range(DOWN_PANELS):
                    round_half(st.at["panels"] + n + 2, 0)
                    for j, e in enumerate(DOWN_STEP_ENDS):
                        if next_weight is not None and (e - 1) // NB == n:
                            act.wait_ge(freed, now(freed, st.at["steps"] + j + 1))
                            norm_hi(next_weight, (2 * j, 2 * j + 1))
                    round_half(st.at["panels"] + n + 2, 1)

            act.wait_ge(x_done, now(x_done, X_DONE2))
            act.wait_ge(small2_in, now(small2_in, 1))
            norm_hi(small("n1"), range(KT))
            norm_root(TWO["norm1"].at["norms"])
            up(TWO["up1"], 0)
            down(TWO["down1"], small("n2"))
            norm_root(TWO["norm2"].at["norms"])

            st = TWO["cmp_kv"]
            n, s = st.at["panels"], st.at["steps"]
            round_panel(n + 2)
            begin(s)
            act.wait_ge(rcol_turned, now(rcol_turned, 1))
            act.activation(rcol[:, :], banks[7][:, T:T + 4:2], ACT.Copy).then_inc(rcol_ready, 1)
            act.wait_ge(rcol_ready, now(rcol_ready, 1))
            for tt in range(TT):
                e = act.activation(tok[:, KC2 + tt * PW:KC2 + (tt + 1) * PW], step_banks(s)[0][:, tt * PW:(tt + 1) * PW],
                                   ACT.Identity, scale=rcol[:, tt:tt + 1])
            e.then_inc(freed, 1)
            def tokens(name, j):
                st, j_ = TWO[name], 2 * j if name == "nsa_kv" else j
                n, s = st.at["panels"] + j_, st.at["steps"] + j_
                round_panel(n + 2)
                begin(s)
                bk = step_banks(s)[0][:, :].rearrange("p (t w) -> p t w", t=2)
                for tt in range(TT):
                    scale = rcol[:, tt:tt + 1]
                    if name == "nsa_g":
                        e = act.activation(gT[:, tt * 24:(tt + 1) * 24], bk[:, tt, 0:24], ACT.Sigmoid, scale=scale)
                    elif name == "nsa_q":
                        a = Q2 + tt * 512 + j * PW
                        e = act.activation(tok[:, a:a + PW], bk[:, tt, :], ACT.Identity, scale=scale)
                    elif name == "nsa_kv":
                        dst = tok[:, KS2:KS2 + 1024].rearrange("p (c t w) -> p c t w", c=2, t=2)
                        e = act.activation(dst[:, :, tt, j * P:(j + 1) * P], tile4(bk[:, tt, :], 2), ACT.Identity,
                                           scale=scale)
                    else:
                        a = M2 + tt * 1536 + j * PW
                        e = act.activation(tok[:, a:a + PW], bk[:, tt, :], ACT.Identity, scale=scale)
                e.then_inc(freed, 1)

            tokens("nsa_g", 0)
            b = st.at["turns"]
            x2 = gates[:, 0:4 * 272].rearrange("p (k t) -> p k t", k=4)
            for tt in range(TT):
                src = tile4(turn_bank(b)[:, :], 4)
                o = 1 - tt
                turns(b, (x2[0:HD, :, tt * P:(tt + 1) * P], src[0:HD]),
                      (x2[HD:P, :, tt * P - tt:tt * P + P - 1], src[HD:P, :, o:P]))
                b += 1
            tokens("nsa_q", 0)
            act.wait_ge(cm_dve, now(cm_dve, 1))
            act.activation(ahi[:, H2:H2 + 1024], work[:, 0:1024], ACT.Copy).then_inc(cm_act, 1)
            tokens("nsa_q", 1)
            st = TWO["nsa_kv"]
            for j in range(2):
                tokens("nsa_kv", j)
                n, s = st.at["panels"] + 2 * j + 1, st.at["steps"] + 2 * j + 1
                round_panel(n + 2)
                begin(s)
                dst, src = glu[:, 0:32], step_banks(s)[0][:, 0:32]
                if j == 1:
                    dst = glu[:, 32:32 + P].rearrange("p (g r c) -> p g r c", g=2, r=4)
                    src = bcast(src.rearrange("p (g c) -> p g c", g=2), 2, 4)
                act.activation(dst, src, ACT.Gelu_apprx_tanh).then_inc(freed, 1)
            qv = qT[:, :].rearrange("p (a t) -> p a t", a=4)
            kv = kP[:, :].rearrange("p (i t) -> p i t", i=16)
            b = TWO["turn_nsa"].at["turns"]
            tokens("moba_qkv", 0)
            act.wait_ge(cm_pe, now(cm_pe, 1))
            act.activation(kct[0:32, 0:HD], banks[7][0:32, 0:HD], ACT.Copy).then_inc(cm_act, 1)
            tokens("moba_qkv", 1)
            for tt in range(TT):
                turns(b, (qv[:, :, tt * P:(tt + 1) * P], tile4(turn_bank(b)[:, :], 4)), None, HD ** -0.5)
                b += 1
            tokens("moba_qkv", 2)
            for tt in range(TT):
                src = tile4(turn_bank(b)[:, :], 4)
                turns(b, (kv[0:HD, 0:8:2, tt * P:(tt + 1) * P], src[0:HD]),
                      (kv[HD:P, 1:8:2, tt * P:(tt + 1) * P], src[HD:P]))
                b += 1
            act.wait_ge(cm_pe, now(cm_pe, 2))
            act.activation(kcp[0:HD, :].rearrange("p (g e c) -> p g e c", g=2, e=2)[:, :, 0, :],
                           banks[7][0:HD, 0:32].rearrange("p (g c) -> p g c", g=2), ACT.Copy)
            act.activation(kcp[HD:P, :].rearrange("p (g e c) -> p g e c", g=2, e=2)[:, :, 1, :],
                           banks[7][HD:P, 0:32].rearrange("p (g c) -> p g c", g=2), ACT.Copy).then_inc(cm_act, 1)
            tokens("moba_qkv", 3)
            tokens("moba_qkv", 4)
            act.wait_ge(cm_dve, now(cm_dve, 4))
            act.activation(cmpw[:, :], cmpw[:, :], ACT.Exp).then_inc(cm_act, 1)
            tokens("moba_qkv", 5)
            act.wait_ge(cm_pe, now(cm_pe, 5))
            act.activation(pcT, banks[7][:, 0:T], ACT.Copy).then_inc(cm_act, 1)
            st = TWO["turn_moba"]
            b = st.at["turns"]
            for tt in range(TT):
                turns(b, (qv[:, :, T + tt * P:T + (tt + 1) * P], tile4(turn_bank(b)[:, :], 4)), None, HD ** -0.5)
                b += 1
            for tt in range(TT):
                src = tile4(turn_bank(b)[:, :], 4)
                turns(b, (kv[0:HD, 8:16:2, tt * P:(tt + 1) * P], src[0:HD]),
                      (kv[HD:P, 9:16:2, tt * P:(tt + 1) * P], src[HD:P]))
                b += 1
            attention(2, None, False, TWO["attn"])
            st = TWO["merge"]
            for j in range(4):
                act.wait_ge(merge_scaled, now(merge_scaled, 2 * j + 2))
                for c in range(2):
                    g = merge_gate_place(2 * j + c)
                    act.activation(g, g, ACT.Sigmoid).then_inc(merge_gate, 1)
                round_half(st.at["panels"] + j + 2, 0)
                act.wait_ge(merged, now(merged, st.at["merges"] + j + 1))
                act.activation(ahi[:, H2 + 2048 + j * 512:H2 + 2048 + (j + 1) * 512],
                               work[:, (j % 2) * 1024 + 512:(j % 2) * 1024 + 1024], ACT.Copy).then_inc(mhi_ready, 1)
                round_half(st.at["panels"] + j + 2, 1)
            st = TWO["out"]
            for j in range(4):
                round_half(st.at["panels"] + j + 2, 0)
                act.wait_ge(freed, now(freed, st.at["steps"] + j + 1))
                norm_hi(small("n3"), (2 * j, 2 * j + 1))
                round_half(st.at["panels"] + j + 2, 1)
            norm_root(TWO["norm3"].at["norms"])
            up(TWO["up2"], FT)
            down(TWO["down2"])
            Place.layer = None
        act.wait_ge(x_done, OUT_DONE - 1)
        for kt in range(KT):
            square(START2["norms"] + LAYERS * PER_LAYER["norms"], 2, kt)
        root(START2["norms"] + LAYERS * PER_LAYER["norms"], 2)

    @block.vector
    def _(dve):
        chain = Chain(dve_chain)
        Place.layer = Place.turn = None

        def split_half(n, h):
            dve.wait_ge(hi_ready, now(hi_ready, 2 * n + h + 1))
            a, b = h * PAN // 2, (h + 1) * PAN // 2
            dve.tensor_tensor(slot_lo(n, a, b), raw[:, (n % 2) * PAN + a:(n % 2) * PAN + b],
                              slot_hi(n, a, b).bitcast(F32), ALU.subtract).then_inc(lo_ready, 1)

        def split_panel(n):
            split_half(n, 0)
            split_half(n, 1)

        def begin(s):
            dve.wait_ge(tick, now(tick, STEP_TICK[s]))
            dve.wait_ge(freed, now(freed, s))

        def inverse(k, blk):
            rms = work[:, 1024:1024 + XW[blk]]
            dve.wait_ge(std_ready, now(std_ready, k + 1))
            dve.reciprocal(rms, rms).then_inc(dve_chain, 1)
            dve.wait_ge(dve_chain, chain.next())
            return rms

        def closing_norm(k, weight):
            inv = inverse(k, 2)
            for kt in range(KT):
                m = dve.scalar_tensor_tensor(x_of(kt), x_of(kt), weight[:, kt:kt + 1], inv, ALU.mult, ALU.mult)
            m.then_inc(x_done, 1)

        def modulate(k):
            inv = inverse(k, 1)
            for i in range(KT + 4):
                if i >= 4:
                    kt = i - 4
                    dve.wait_ge(xhi_ready, 8 * k + kt + 1)
                    dve.tensor_tensor(act_x(alo, 1, kt, 0, 512), gates[:, (kt % 4) * 512:(kt % 4) * 512 + 512],
                                      act_x(ahi, 1, kt, 0, 512).bitcast(F32), ALU.subtract).then_inc(x_split, 1)
                if i < KT:
                    if i >= 4:
                        dve.wait_ge(x_split, 8 * k + i - 3)
                    dve.tensor_tensor(gates[:, (i % 4) * 512:(i % 4) * 512 + 512], x_of(i, 0, 512), inv,
                                      ALU.mult).then_inc(tile_ready, 1)

        def modulation(l, cols):
            dve.wait_ge(mod_cols, l + 1)
            m = mod[:, l * 48:(l + 1) * 48].rearrange("p (t c) -> p t c", c=2)
            small = [sm1[:, l * NSMALL1 + SMALL1[x][0]:l * NSMALL1 + SMALL1[x][1]] for x in ("ada_b", "norm_w")]
            dve.tensor_tensor(m, cols.rearrange("p (t c) -> p t c", c=2), bcast(small[0], 2, 2),
                              ALU.add).then_inc(dve_chain, 1)
            dve.wait_ge(dve_chain, chain.next())
            dve.scalar_tensor_tensor(moda[:, l * 16:(l + 1) * 16].rearrange("p (t c) -> p t c", c=2), m[:, 8:16, :], 1.0,
                                     bcast(small[1], 2, 2), ALU.add, ALU.mult).then_inc(mod_ready, 1)

        def attention(blk, mixer, with_ctx, st):
            units, groups, pairs = attention_plan(blk, mixer, with_ctx)
            u0, g0, p0 = st.at["units"], st.at["groups"], st.at["pairs"]
            for i in range(len(units) + 8):
                for r, slot in enumerate(GATE_SLOTS if blk == 2 else ()):
                    n = st.at["panels"] + r
                    if i == slot + 2:
                        if r == 0:
                            dve.wait_ge(rs_ready, now(rs_ready, 2))
                        dve.wait_ge(tick, now(tick, PANEL_TICK[n]))
                        dve.tensor_tensor(merge_gate_place(r), tile4(banks[7][:, :], 2), bcast(rs[:, :], 1, 2),
                                          ALU.mult).then_inc(merge_scaled, 1)
                if i < len(units):
                    un, u = units[i], u0 + i
                    sbase = (u % 3) * 8
                    dve.wait_ge(scores, now(scores, u + 1))
                    bank = score_bank(u)
                    for c, w, segs, mask in un.masks:
                        if isinstance(mask, tuple):
                            nb = st.layer * NH + mask[1]
                            dve.wait_ge(biased, nb + 1)
                            mk = bias[:, (nb % 2) * 512 + mask[2] * T:(nb % 2) * 512 + (mask[2] + 1) * T]
                            dve.tensor_tensor(bank[:, c:c + w], bank[:, c:c + w], mk, ALU.add).then_inc(bias_used, 1)
                            dve.wait_ge(bias_used, 2 * nb + mask[2] + 1)
                        elif segs == 1:
                            dve.tensor_tensor(bank[:, c:c + w], bank[:, c:c + w], mask, ALU.add).then_inc(dve_chain, 1)
                            dve.wait_ge(dve_chain, chain.next())
                        else:
                            dst = tile4(bank[:, :], 2)[:, :, c:c + w]
                            dve.tensor_tensor(dst, dst, bcast(mask, 1, 2), ALU.add).then_inc(dve_chain, 1)
                            dve.wait_ge(dve_chain, chain.next())
                    ns = len(un.segs)
                    nm = stats[:, sbase:sbase + ns]
                    w = un.segs[0][1]
                    src = bank[:, 0:w] if ns == 1 else tile4(bank[:, :], 2)[:, :, 0:w]
                    m = dve.reduce_max(nm, src, AX.X, negate=True)
                    if un.segs[0][2] is not None:
                        m.then_inc(dve_chain, 1)
                        dve.wait_ge(dve_chain, chain.next())
                        a = SMALL1["sink"][0] + st.layer * NSMALL1 + un.segs[0][2]
                        m = dve.scalar_tensor_tensor(nm, sm1[:, a:a + ns], -1.0, nm, ALU.mult, ALU.min)
                    m.then_inc(negmax, 1)
                j = i - 1
                if 0 <= j < len(units):
                    un, u = units[j], u0 + j
                    sbase = (u % 3) * 8
                    ns = len(un.segs)
                    dve.wait_ge(exped, now(exped, u + 1))
                    total = stats[:, sbase + 2:sbase + 2 + ns]
                    if un.segs[0][2] is not None:
                        dve.tensor_tensor(total, total, stats[:, sbase + 6:sbase + 6 + ns], ALU.add).then_inc(dve_chain, 1)
                        dve.wait_ge(dve_chain, chain.next())
                    inv = stats[:, sbase + 4:sbase + 4 + ns]
                    dve.reciprocal(inv, total).then_inc(dve_chain, 1)
                    dve.wait_ge(dve_chain, chain.next())
                    if un.segs[0][3] is not None:
                        qt, col = un.segs[0][3]
                        dve.tensor_tensor(inv, inv, gT[:, qt * 24 + col:qt * 24 + col + 2], ALU.mult).then_inc(dve_chain, 1)
                        dve.wait_ge(dve_chain, chain.next())
                    for k, (c, w, _, _) in enumerate(un.segs):
                        m = dve.tensor_scalar(probs(u)[:, c:c + w], probs(u)[:, c:c + w], inv[:, k:k + 1], None, ALU.mult)
                    m.then_inc(normed, 1)
                for r, slot in enumerate(ADA_SLOTS if st.panels and blk == 1 else ()):
                    for h in range(2):
                        if i == slot + 1 + h:
                            split_half(st.at["panels"] + r + 2, h)
                for r, slot in enumerate(GATE_SLOTS if blk == 2 else ()):
                    for h in range(2):
                        if i == slot + 2 + h:
                            split_half(st.at["panels"] + r + 2, h)
                j = i - 5
                if 0 <= j < len(units) and last_unit_of(units, units[j].group) == j and groups[units[j].group].last:
                    g = units[j].group
                    pr = groups[g].pair
                    dve.wait_ge(pv, now(pv, g0 + g + 1))
                    if p0 + pr - 1 >= 1:
                        dve.wait_ge(usplit, now(usplit, p0 + pr - 1))
                    if blk == 1:
                        m = dve.tensor_tensor(gated(p0 + pr), out_bank(p0 + pr)[:, 0:T], gate_of(1, pairs[pr]), ALU.mult)
                    else:
                        m = dve.tensor_copy(gated(p0 + pr), out_bank(p0 + pr)[:, 0:T])
                    m.then_inc(omul, 1)
                j = i - 7
                if 0 <= j < len(units) and last_unit_of(units, units[j].group) == j and groups[units[j].group].last:
                    pr = groups[units[j].group].pair
                    dve.wait_ge(uhi, now(uhi, p0 + pr + 1))
                    dve.tensor_tensor(u_of(alo, blk, pairs[pr]), gated(p0 + pr), u_of(ahi, blk, pairs[pr]).bitcast(F32),
                                      ALU.subtract).then_inc(usplit, 1)

        def norm_squares(j):
            x = xT[:, :].rearrange("p (k t) -> p k t", k=KT)[:, 2 * j:2 * j + 2, 0:T]
            dve.tensor_tensor(tile4(work[:, j * 512:(j + 1) * 512], 2), x, x, ALU.mult).then_inc(sq_ready, 2)

        def norm_lo(k, weight, j):
            for kt in (2 * j, 2 * j + 1):
                dve.wait_ge(xhi_ready, now(xhi_ready, 8 * k_x(k) + kt + 1))
                dve.scalar_tensor_tensor(act_x(alo, 2, kt, 0, T), x_of(kt), weight[:, kt:kt + 1],
                                         act_x(ahi, 2, kt, 0, T).bitcast(F32), ALU.mult, ALU.subtract).then_inc(x_split, 1)

        def norm_scale(k):
            dve.wait_ge(std_ready, now(std_ready, k + 1))
            dve.reciprocal(rs[:, :], rs[:, :]).then_inc(rs_ready, 1)

        def rope(src, dst, heads, cos, sin, nsin, rows=P, dup=False):
            x = src.rearrange("p (h e f) -> p h e f", h=heads, e=2)
            t1 = work[0:rows, 0:heads * HD].rearrange("p (h e f) -> p h e f", h=heads, e=2)
            t2 = work[0:rows, 512:512 + heads * HD].rearrange("p (h e f) -> p h e f", h=heads, e=2)
            b1 = bcast(bcast(cos, 1, 2), 1, heads)
            dve.tensor_tensor(t1, x, b1, ALU.mult)
            dve.tensor_tensor(t2[:, :, 0, :], x[:, :, 1, :], bcast(nsin, 1, heads), ALU.mult)
            dve.tensor_tensor(t2[:, :, 1, :], x[:, :, 0, :], bcast(sin, 1, heads), ALU.mult).then_inc(dve_chain, 1)
            dve.wait_ge(dve_chain, chain.next())
            a, b = work[0:rows, 0:heads * HD], work[0:rows, 512:512 + heads * HD]
            if not dup:
                dve.tensor_tensor(dst, a, b, ALU.add).then_inc(dve_chain, 1)
                dve.wait_ge(dve_chain, chain.next())
            else:
                d = dst.rearrange("p (h e f) -> p h e f", h=heads, e=2)
                a, b = (v.rearrange("p (h f) -> p h f", h=heads) for v in (a, b))
                dve.tensor_tensor(d[:, :, 0, :], a, b, ALU.add).then_inc(dve_chain, 1)
                dve.wait_ge(dve_chain, chain.next())
                dve.tensor_tensor(d[:, :, 1, :], a, b, ALU.add).then_inc(dve_chain, 1)
                dve.wait_ge(dve_chain, chain.next())

        dve.memset(ahi[:, CP:CP + KT * P].bitcast(mybir.dt.uint32), 0).then_inc(c_split, 1)
        split_panel(0)
        dve.wait_ge(c_hi, 1)
        cpad = ahi[:, CP:CP + KT * P].rearrange("p (k m) -> p k m", k=KT)
        dve.tensor_tensor(cpad[:, :, 2:4], tile4(cmpw[:, 0:2 * KT], KT), cpad[:, :, 0:2].bitcast(F32),
                          ALU.subtract).then_inc(c_split, 1)
        split_panel(1)

        for l in range(LAYERS):
            wctx = l == 0
            nt = 4 if wctx else 2
            s1 = l * NSMALL1

            def small(name):
                a, b = SMALL1[name]
                return sm1[:, s1 + a:s1 + b]

            if wctx:
                st = ONE["ada", l]
                for j in range(ADA_PANELS):
                    split_panel(st.at["panels"] + j + 2)
                dve.wait_ge(consts_in, 48)
                modulation(0, banks[4][:, 0:48])
            modulate(ONE["norm", l].at["norms"])

            def heads_of(j):
                sec, col, heads, tiles = head_part(j, wctx)
                return tok[:, sec:sec + 2048].rearrange("p (t w) -> p t w", t=4)[:, 0:tiles, col:col + heads * HD]

            def head_norm(j):
                _, _, heads, tiles = head_part(j, wctx)
                x, h = heads_of(j), head_stats(j, wctx)
                sq = work[:, 0:tiles * heads * HD]
                dve.tensor_tensor(sq.rearrange("p (t w) -> p t w", t=tiles), x, x, ALU.mult).then_inc(dve_chain, 1)
                dve.wait_ge(dve_chain, chain.next())
                dve.reduce_sum(h, sq.rearrange("p (a f) -> p a f", f=HD), AX.X).then_inc(hs_sum, 1)
                dve.wait_ge(hs_std, 3 * l + j + 1)
                dve.reciprocal(h, h).then_inc(dve_chain, 1)
                dve.wait_ge(dve_chain, chain.next())
                x4 = x.rearrange("p t (h f) -> p t h f", h=heads)
                dve.tensor_tensor(x4, x4, bcast(tile4(h, tiles), 3, HD), ALU.mult).then_inc(dve_chain, 1)
                dve.wait_ge(dve_chain, chain.next())
                w = small("qn" if j < 2 else "kn")
                dve.tensor_tensor(x4, x4, bcast(bcast(w, 1, heads), 1, tiles), ALU.mult).then_inc(dve_chain, 1)
                dve.wait_ge(dve_chain, chain.next())

            def rotate(j):
                for tt in range(4 if j == 2 else 2):
                    tabs = [const(x)[:, tt * HALF:(tt + 1) * HALF] for x in ("cos1", "sin1", "nsin1")] if tt < 2 else None
                    if j < 2:
                        q = tok[:, Q1 + tt * 512 + j * PW:Q1 + tt * 512 + (j + 1) * PW]
                        rope(q, q, 4, *tabs)
                        continue
                    k = tok[:, K1 + tt * 512:K1 + tt * 512 + P]
                    kd = work[:, 1024 + tt * 256:1024 + (tt + 1) * 256]
                    if tt < 2:
                        rope(k, kd, 2, *tabs, dup=True)
                    else:
                        dve.tensor_copy(kd.rearrange("p (h e f) -> p h e f", h=2, e=2),
                                        bcast(k.rearrange("p (h f) -> p h f", h=2), 2, 2)).then_inc(dve_chain, 1)
                        dve.wait_ge(dve_chain, chain.next())
                if j == 2:
                    dve.sem_inc(roped, 1)

            def qkv(m):
                st = ONE["qkv" + m, l]
                for j in range(st.panels):
                    split_panel(st.at["panels"] + j + 2)
                    if m != "B":
                        dve.wait_ge(freed, st.at["steps"] + j + 1)
                    if m == "A":
                        head_norm(j)
                    if m != "B":
                        rotate(j)

            def gate(m):
                for j in range(2):
                    split_panel(ONE["gate" + m, l].at["panels"] + j + 2)

            def wout(m):
                st = ONE["wout" + m, l]
                for j in range(2):
                    for c in range(2):
                        s = st.at["steps"] + 2 * j + c
                        if c == 1:
                            split_panel(st.at["panels"] + j + 2)
                        begin(s)
                        for e in range(2):
                            kt = 4 * j + 2 * c + e
                            bank = step_banks(s)[e]
                            for part in range(2 if wctx else 1):
                                o = dve.scalar_tensor_tensor(x_of(kt, part * T, (part + 1) * T), bank[:, part * T:(part + 1) * T],
                                                             mod[:, l * 48 + 32 + kt * 2 + part:l * 48 + 33 + kt * 2 + part],
                                                             x_of(kt, part * T, (part + 1) * T), ALU.mult, ALU.add)
                        o.then_inc(freed, 1)

            for m in MIX1:
                if m == "A":
                    qkv("A")
                gate(m)
                attention(1, m, wctx, ONE["attn" + m, l])
                if m == "A":
                    qkv("B")
                    wout("A")
                if m == "B":
                    qkv("C")
                    wout("B")
                if m == "C":
                    if wctx:
                        modulation(1, banks[7][:, MOD_COLS:MOD_COLS + 48])
                    wout("C")
            dve.wait_ge(freed, ONE["woutC", l].at["steps"] + 4)
            dve.sem_inc(x_done, 1)

        closing_norm(START2["norms"] - 1, smg[:, 0:8])

        assert chain.n == DVE_START2, chain.n
        with dve.Fori(0, LAYERS) as layer:
            Place.layer = layer

            def small(name):
                a, b = SMALL2[name]
                return sm2[:, a:b]

            dve.tensor_copy(sm2[:, :], sm2all[:, bass.ds(layer * NSMALL2, NSMALL2)]).then_inc(small2_in, 1)
            dve.wait_ge(small2_in, now(small2_in, 1))

            def up(st, first_hidden, scales):
                n0, s0 = st.at["panels"], st.at["steps"]
                with dve.Fori(0, FT // 2) as turn:
                    Place.turn = turn
                    for j in range(2):
                        n, s, a = n0 + j, s0 + j, first_hidden + j
                        gu = work[:, (j % 2) * 512:(j % 2) * 512 + 512]
                        dve.wait_ge(rs_ready, now(rs_ready, scales))
                        dve.wait_ge(tick, now(tick, STEP_TICK[s]))
                        dve.tensor_tensor(tile4(gu, 2), tile4(step_banks(s)[0][:, :], 2), bcast(rs[:, :], 1, 2),
                                          ALU.mult).then_inc(freed, 1)
                        split_half(n + 2, 0)
                        dve.wait_ge(silu_ready, now(silu_ready, a + 1))
                        dve.tensor_tensor(gu[:, T:2 * T], gu[:, T:2 * T], gu[:, 0:T], ALU.mult).then_inc(hid_gated, 1)
                        split_half(n + 2, 1)
                        dve.wait_ge(hhi_ready, now(hhi_ready, a + 1))
                        f = [x[:, H2:H2 + FT * T].rearrange("p (f t) -> p f t", f=FT)[:, 2 * turn + j, :] for x in (ahi, alo)]
                        dve.tensor_tensor(f[1], gu[:, T:2 * T], f[0].bitcast(F32), ALU.subtract).then_inc(hid_split, 1)
                    Place.turn = None

            def residual(s, kt, factor, src):
                x = xT[:, :].rearrange("p (k t) -> p k t", k=KT)[:, kt:kt + 2, 0:T]
                return dve.scalar_tensor_tensor(x, tile4(src[:, :], 2), factor, x, ALU.mult, ALU.add)

            def down(st, k=None, weight=None):
                n = 0
                for j in range(4):
                    while (n + 1) * NB < DOWN_STEP_ENDS[j]:
                        split_panel(st.at["panels"] + n + 2)
                        n += 1
                    if j and k is not None:
                        norm_lo(k, weight, j - 1)
                    s = st.at["steps"] + j
                    begin(s)
                    residual(s, 2 * j, 0.5, step_banks(s)[0]).then_inc(freed, 1)
                    if k is not None:
                        dve.wait_ge(freed, now(freed, s + 1))
                        norm_squares(j)
                split_half(st.at["panels"] + n + 2, 0)
                if k is not None:
                    norm_lo(k, weight, 3)
                split_half(st.at["panels"] + n + 2, 1)
                dve.wait_ge(freed, now(freed, st.at["steps"] + 4))
                dve.sem_inc(x_done, 1)

            dve.wait_ge(x_done, now(x_done, X_DONE2))
            norm_squares(0)
            for j in range(4):
                if j < 3:
                    norm_squares(j + 1)
                norm_lo(TWO["norm1"].at["norms"], small("n1"), j)
            norm_scale(TWO["norm1"].at["norms"])
            up(TWO["up1"], 0, 1)
            down(TWO["down1"], TWO["norm2"].at["norms"], small("n2"))
            norm_scale(TWO["norm2"].at["norms"])

            def rotate(tt, what):
                tabs = [const(x)[:, tt * HALF:(tt + 1) * HALF] for x in ("cos2", "sin2", "nsin2")]
                if what == "nsa":
                    q = tok[:, Q2 + tt * 512:Q2 + (tt + 1) * 512]
                    rope(q, q, 8, *tabs)
                    rope(tok[:, KS2 + tt * 256:KS2 + (tt + 1) * 256], work[:, 1024 + tt * 512:1024 + (tt + 1) * 512], 4,
                         *tabs, dup=True)
                else:
                    a = M2 + tt * 1536 + what * 512
                    rope(tok[:, a:a + 512], tok[:, a:a + 512], 8, *tabs)

            st = TWO["cmp_kv"]
            split_panel(st.at["panels"] + 2)
            dve.wait_ge(freed, now(freed, st.at["steps"] + 1))
            for tt in range(TT):
                kd = work[:, 1024 + tt * 512:1024 + (tt + 1) * 512].rearrange("p (k e f) -> p k e f", k=4, e=2)
                k = tok[:, KC2 + tt * 256:KC2 + (tt + 1) * 256].rearrange("p (k f) -> p k f", k=4)
                dve.tensor_copy(kd, bcast(k, 2, 2))
            x2 = gates[:, 0:4 * 272].rearrange("p (k t) -> p k t", k=4)
            dve.memset(x2[:, :, T - 1:272], 0.0).then_inc(roped, 1)
            split_panel(TWO["nsa_g"].at["panels"] + 2)
            dve.wait_ge(turn_out, now(turn_out, st.at["turns"] + 2))
            pos = small("pos")
            for kg in range(4):
                base = gates[:, kg * 272:kg * 272 + 256]
                src = bass.AP(base.tensor, base.offset, [base.ap[0], [16, NCMP], [2, 16]])
                o = dve.tensor_tensor(work[:, kg * 256:(kg + 1) * 256].rearrange("p (n j) -> p n j", n=NCMP), src,
                                      bcast(pos[:, (kg // 2) * 16:(kg // 2 + 1) * 16], 1, NCMP), ALU.add)
            o.then_inc(cm_dve, 1)
            split_panel(TWO["nsa_q"].at["panels"] + 2)
            dve.wait_ge(cm_act, now(cm_act, 1))
            dve.tensor_tensor(alo[:, H2:H2 + 1024], work[:, 0:1024], ahi[:, H2:H2 + 1024].bitcast(F32),
                              ALU.subtract).then_inc(cm_dve, 1)
            dve.wait_ge(cm_dve, now(cm_dve, 2))
            split_panel(TWO["nsa_q"].at["panels"] + 3)
            for j in range(4):
                split_panel(TWO["nsa_kv"].at["panels"] + j + 2)
            m0, s0 = TWO["moba_qkv"].at["panels"], TWO["moba_qkv"].at["steps"]
            rotate(0, "nsa")
            split_panel(m0 + 2)
            rotate(1, "nsa")
            dve.sem_inc(roped, 1)
            split_panel(m0 + 3)
            dve.wait_ge(cm_act, now(cm_act, 2))
            rope(kct[0:32, 0:HD], kct[0:32, P:2 * P], 1, *[const(x)[0:32] for x in ("cosc", "sinc", "nsinc")], rows=32, dup=True)
            dve.sem_inc(cm_dve, 1)
            split_panel(m0 + 4)
            dve.wait_ge(freed, now(freed, s0 + 2))
            rotate(0, 0)
            rotate(1, 0)
            split_panel(m0 + 5)
            dve.wait_ge(cm_pe, now(cm_pe, 3))
            dve.tensor_tensor(cmpw[:, :].rearrange("p (q h c) -> p q h c", q=2, h=NH),
                              banks[7][:, 0:256].rearrange("p (q h c) -> p q h c", q=2, h=NH),
                              bcast(tile4(const("cmp_add"), 2), 2, NH), ALU.add).then_inc(dve_chain, 1)
            dve.wait_ge(dve_chain, chain.next())
            heads = cmpw[:, :].rearrange("p (a c) -> p a c", c=NCMP)
            dve.reduce_max(cstat[:, 0:16], heads, AX.X, negate=True).then_inc(dve_chain, 1)
            dve.wait_ge(dve_chain, chain.next())
            dve.tensor_tensor(heads, heads, bcast(cstat[:, 0:16], 2, NCMP), ALU.add).then_inc(cm_dve, 1)
            dve.wait_ge(freed, now(freed, s0 + 4))
            rotate(0, 1)
            split_panel(m0 + 6)
            dve.wait_ge(cm_act, now(cm_act, 4))
            keep = bcast(tile4(const("cmp_keep"), 2), 2, NH)
            w4 = cmpw[:, :].rearrange("p (q h c) -> p q h c", q=2, h=NH)
            dve.tensor_tensor(w4, w4, keep, ALU.mult).then_inc(dve_chain, 1)
            dve.wait_ge(dve_chain, chain.next())
            dve.reduce_sum(cstat[:, 0:16], heads, AX.X).then_inc(dve_chain, 1)
            dve.wait_ge(dve_chain, chain.next())
            dve.tensor_scalar(cstat[:, 0:16], cstat[:, 0:16], TINY, None, ALU.max).then_inc(dve_chain, 1)
            dve.wait_ge(dve_chain, chain.next())
            dve.reciprocal(cstat[:, 0:16], cstat[:, 0:16]).then_inc(dve_chain, 1)
            dve.wait_ge(dve_chain, chain.next())
            g0 = tile4(gT[:, :], 2).rearrange("p q (h b) -> p q h b", b=3)[:, :, :, 0]
            dve.tensor_tensor(tile4(cstat[:, 0:16], 2), tile4(cstat[:, 0:16], 2), g0, ALU.mult).then_inc(dve_chain, 1)
            dve.wait_ge(dve_chain, chain.next())
            dve.wait_ge(cm_pe, now(cm_pe, 4))
            dve.tensor_tensor(vblk.rearrange("p (h f) -> p h f", h=NH), bcast(banks[7][:, 256:256 + HD], 1, NH),
                              bcast(const("head_of"), 2, HD), ALU.mult)
            dve.tensor_tensor(heads, heads, bcast(cstat[:, 0:16], 2, NCMP), ALU.mult).then_inc(cm_dve, 1)
            rotate(1, 1)
            dve.sem_inc(roped, 1)
            split_panel(m0 + 7)
            attention(2, None, False, TWO["attn"])
            st = TWO["merge"]
            for j in range(4):
                s = st.at["steps"] + j
                begin(s)
                dve.wait_ge(merge_gate, now(merge_gate, 2 * j + 2))
                m1 = work[:, (j % 2) * 1024:(j % 2) * 1024 + 512]
                m2 = work[:, (j % 2) * 1024 + 512:(j % 2) * 1024 + 1024]
                for branch, m in enumerate((m1, m2)):
                    o = dve.tensor_tensor(tile4(m, 2), tile4(step_banks(s)[branch][:, :], 2), merge_gate_place(2 * j + branch),
                                          ALU.mult)
                o.then_inc(freed, 1)
                dve.wait_ge(freed, now(freed, s + 1))
                dve.tensor_tensor(m2, m2, m1, ALU.add).then_inc(merged, 1)
                split_half(st.at["panels"] + j + 2, 0)
                dve.wait_ge(mhi_ready, now(mhi_ready, st.at["merges"] + j + 1))
                dve.tensor_tensor(alo[:, H2 + 2048 + j * 512:H2 + 2048 + (j + 1) * 512], m2,
                                  ahi[:, H2 + 2048 + j * 512:H2 + 2048 + (j + 1) * 512].bitcast(F32),
                                  ALU.subtract).then_inc(m_split, 1)
                split_half(st.at["panels"] + j + 2, 1)
            st = TWO["out"]
            for j in range(4):
                s = st.at["steps"] + j
                begin(s)
                residual(s, 2 * j, 1.0, step_banks(s)[0]).then_inc(freed, 1)
                dve.wait_ge(freed, now(freed, s + 1))
                norm_squares(j)
                split_half(st.at["panels"] + j + 2, 0)
                norm_lo(TWO["norm3"].at["norms"], small("n3"), j)
                split_half(st.at["panels"] + j + 2, 1)
            dve.wait_ge(freed, now(freed, st.at["steps"] + 4))
            dve.sem_inc(x_done, 1)
            norm_scale(TWO["norm3"].at["norms"])
            up(TWO["up2"], FT, 3)
            down(TWO["down2"])
            assert chain.n == DVE_START2 + DVE_LAYER, chain.n
            Place.layer = None
        chain.n = DVE_START2 + LAYERS * DVE_LAYER
        closing_norm(START2["norms"] + LAYERS * PER_LAYER["norms"], smg[:, 8:16])

    @block.tensor
    def _(pe):
        Place.layer = Place.turn = None

        def mm3(dst, whi_, wlo_, xhi_, xlo_, start, stop):
            pe.matmul(dst, whi_, xhi_, start=start, stop=False, skip_group_check=True)
            pe.matmul(dst, whi_, xlo_, start=False, stop=False, skip_group_check=True)
            return pe.matmul(dst, wlo_, xhi_, start=False, stop=stop, skip_group_check=True)

        def need(n, half):
            pe.wait_ge(lo_ready, now(lo_ready, 2 * n + half + 1))

        def take(s):
            if s - 1 >= 1:
                pe.wait_ge(freed, now(freed, s - 1))

        def wblock(n, b, c0=0, c1=PW):
            return slot_hi(n, b * PW + c0, b * PW + c1), slot_lo(n, b * PW + c0, b * PW + c1)

        def feature_major(n, dst, m, rhs, blocks=range(NB), inputs=None):
            bl = list(blocks)
            for b in bl:
                need(n, b // 4)
                if inputs is not None:
                    pe.wait_ge(inputs[0], now(inputs[0], inputs[1] + b // inputs[2] + 1))
                wh, wl = wblock(n, b, m * P, (m + 1) * P)
                xh, xl = rhs(b)
                o = mm3(dst, wh, wl, xh, xl, b == bl[0], b == bl[-1])
            return o

        def token_major(n, dst, blk, tt, width=PW, inputs=None):
            for kt in range(KT):
                need(n, kt // 4)
                if inputs is not None:
                    pe.wait_ge(x_split, now(x_split, inputs + kt + 1))
                wh, wl = wblock(n, kt, 0, width)
                xh, xl = (act_x(x, blk, kt, tt * P, (tt + 1) * P) for x in (ahi, alo))
                o = mm3(dst, xh, xl, wh, wl, kt == 0, kt == KT - 1)
            return o

        def sum_square(k, blk, kt):
            w = XW[blk]
            if k and kt == 0:
                pe.wait_ge(std_ready, now(std_ready, k))
            pe.wait_ge(sq_ready, now(sq_ready, 8 * k + kt + 1))
            pe.matmul(banks[7][:, 0:w], ones, work[:, (kt % 2) * 512:(kt % 2) * 512 + w],
                      start=kt == 0, stop=kt == KT - 1).then_inc(sq_used, 1)

        def ada_panel(n, dst):
            cpad = ahi[:, CP:CP + KT * P].rearrange("p (k m) -> p k m", k=KT)
            for kt in range(KT):
                need(n, kt // 4)
                wh, wl = wblock(n, kt)
                pe.matmul(dst, cpad[:, kt, :], wh, start=kt == 0, stop=False, skip_group_check=True)
                o = pe.matmul(dst, cpad[:, kt, :], wl, start=False, stop=kt == KT - 1, skip_group_check=True)
            o.then_inc(tick, 1)

        def to_columns(rows, dst):
            for e in range(2):
                o = pe.matmul(dst[:, 2 * e:2 * e + 2], rows[:, e * P:(e + 1) * P], const("sel", slice(0, 4)),
                              start=True, stop=True, skip_group_check=True)
            return o

        def norm_sums(k, tiles):
            if 0 in tiles:
                pe.wait_ge(std_ready, now(std_ready, k))
            for kt in tiles:
                pe.wait_ge(sq_ready, now(sq_ready, 8 * k + kt + 1))
                pe.matmul(banks[7][:, 0:T], ones, work[:, kt * T:(kt + 1) * T],
                          start=kt == 0, stop=kt == KT - 1).then_inc(sq_used, 1)

        def turn(b, blocks):
            if b - 1 >= 1:
                pe.wait_ge(turn_out, now(turn_out, b - 1))
            for k, src in enumerate(blocks):
                o = pe.transpose(turn_bank(b)[:, k * P:(k + 1) * P], src, ident)
            o.then_inc(turned, 1)

        def attention(blk, mixer, with_ctx, st, after):
            units, groups, pairs = attention_plan(blk, mixer, with_ctx)
            u0, g0, p0 = st.at["units"], st.at["groups"], st.at["pairs"]
            pe.wait_ge(freed, now(freed, after))
            for i in range(len(units) + 5):
                if i < len(units):
                    un, u = units[i], u0 + i
                    if u - 2 >= 1:
                        pe.wait_ge(exped, now(exped, u - 2))
                    for k, (keys, c, w) in enumerate(un.keys):
                        o = pe.matmul(score_bank(u)[:, c:c + w], un.q, keys, start=True, stop=True, skip_group_check=True)
                    o.then_inc(scores, 1)
                for r, slot in enumerate(GATE_SLOTS if blk == 2 else ()):
                    for e in range(2):
                        if i == slot + e:
                            if r and e == 0:
                                pe.wait_ge(merge_scaled, now(merge_scaled, r))
                            o = feature_major(st.at["panels"] + r, banks[7][:, e * T:(e + 1) * T], e,
                                              lambda b: (act_x(ahi, 2, b, 0, T), act_x(alo, 2, b, 0, T)))
                            if e:
                                o.then_inc(tick, 1)
                for r, slot in enumerate(ADA_SLOTS if st.panels and blk == 1 else ()):
                    row = MIX1.index(mixer) * len(ADA_SLOTS) + r
                    if i == slot:
                        if row:
                            pe.wait_ge(row_out, row)
                        ada_panel(st.at["panels"] + r, banks[7][:, 0:PW])
                    if i == slot + 3:
                        pe.wait_ge(row_out, row + 1)
                        c = MOD_COLS + 4 * row
                        to_columns(cmpw[0:4, 0:PW], banks[7][:, c:c + 4]).then_inc(row_turned, 1)
                j = i - 3
                if 0 <= j < len(units):
                    un, u = units[j], u0 + j
                    pe.wait_ge(normed, now(normed, u + 1))
                    if u - 1 >= 1:
                        pe.wait_ge(probT_out, now(probT_out, u - 1))
                    for c, b in un.blocks:
                        o = pe.transpose(prob_bank(u)[:, b * P:(b + 1) * P], probs(u)[:, c:c + P], ident)
                    o.then_inc(probT, 1)
                j = i - 5
                if 0 <= j < len(units) and last_unit_of(units, units[j].group) == j:
                    g = units[j].group
                    gr = groups[g]
                    pe.wait_ge(probT_out, now(probT_out, u0 + j + 1))
                    if p0 + gr.pair - 1 >= 1:
                        pe.wait_ge(omul, now(omul, p0 + gr.pair - 1))
                    ob = out_bank(p0 + gr.pair)
                    if gr.cmp:
                        pr = pairs[gr.pair][0]
                        pe.matmul(ob[:, 0:T], vblk[:, pr * P:(pr + 1) * P], pcT, start=True, stop=False,
                                  skip_group_check=True)
                    for k, (half, v, b, q0, start) in enumerate(gr.adds):
                        o = pe.matmul(ob[half * HD:(half + 1) * HD, q0:T], v, probsT(g0 + g)[:, b, q0:T],
                                      start=start, stop=k == len(gr.adds) - 1, skip_group_check=True)
                    o.then_inc(pv, 1)
            if st.panels and blk == 1 and mixer == "C":
                pe.wait_ge(row_turned, ADA_PANELS)
                pe.sem_inc(mod_cols, 1)

        for l in range(LAYERS):
            wctx = l == 0
            nt = 4 if wctx else 2
            w = 2 * T if wctx else T
            k = ONE["norm", l].at["norms"]
            if wctx:
                st = ONE["ada", l]
                pe.wait_ge(c_split, 2)
                for j in range(ADA_PANELS + 1):
                    n, s = st.at["panels"] + j, st.at["steps"] + j
                    if j < ADA_PANELS:
                        take(s)
                        ada_panel(n, step_banks(s)[0][:, 0:PW])
                    if j == 1:
                        pe.wait_ge(consts_in, 48)
                    if 3 <= j < KT + 3:
                        sum_square(k, 1, j - 3)
                    if j > 0:
                        pe.wait_ge(freed, now(freed, s))
                        o = to_columns(tok[0:4, (j - 1) * PW:j * PW], banks[4][:, 4 * (j - 1):4 * j])
                o.then_inc(mod_cols, 1)
                pe.wait_ge(pads_zero, 2)
            else:
                pe.wait_ge(mod_ready, l + 1)
                for kt in range(KT):
                    sum_square(k, 1, kt)

            def qkv(m):
                st = ONE["qkv" + m, l]
                for j in range(st.panels):
                    n, s = st.at["panels"] + j, st.at["steps"] + j
                    take(s)
                    full = qkv_places(m, j)[0][0] != Q1 or wctx
                    dst = [step_banks(s)[tt // 2][:, (tt % 2) * PW:(tt % 2 + 1) * PW] for tt in range(4 if full else 2)]
                    if m == "A" and j == 0:
                        for kt in range(KT):
                            need(n, kt // 4)
                            pe.wait_ge(x_split, 8 * k + kt + 1)
                            wh, wl = wblock(n, kt)
                            for tt, d in enumerate(dst):
                                xh, xl = (act_x(x, 1, kt, tt * P, (tt + 1) * P) for x in (ahi, alo))
                                o = mm3(d, xh, xl, wh, wl, kt == 0 and tt % 2 == 0, kt == KT - 1)
                    else:
                        for tt, d in enumerate(dst):
                            o = token_major(n, d, 1, tt)
                    o.then_inc(tick, 1)

            def gate(m):
                st = ONE["gate" + m, l]
                for j in range(2):
                    n, s = st.at["panels"] + j, st.at["steps"] + j
                    take(s)
                    for c in range(2):
                        o = feature_major(n, step_banks(s)[c][:, 0:w], c,
                                          lambda b: (act_x(ahi, 1, b, 0, w), act_x(alo, 1, b, 0, w)))
                    o.then_inc(tick, 1)

            def wout(m):
                st = ONE["wout" + m, l]
                at = ONE["attn" + m, l]
                pe.wait_ge(usplit, now(usplit, at.at["pairs"] + at.pairs))
                for j in range(2):
                    n = st.at["panels"] + j
                    for c in range(2):
                        s = st.at["steps"] + 2 * j + c
                        take(s)
                        for e in range(2):
                            for kt in range(4):
                                a = kt * 512 + (2 * c + e) * P
                                need(n, (a + P - 1) // (PAN // 2))
                                ux = [x[:, U1 + kt * 512:U1 + kt * 512 + w] for x in (ahi, alo)]
                                o = mm3(step_banks(s)[e][:, 0:w], slot_hi(n, a, a + P), slot_lo(n, a, a + P), *ux,
                                        kt == 0, kt == 3)
                        o.then_inc(tick, 1)

            for m in MIX1:
                if m == "A":
                    qkv("A")
                gate(m)
                st = ONE["turn" + m, l]
                b = st.at["turns"]
                pe.wait_ge(roped, 2 * l + (1 if m == "A" else 2)) if m != "B" else None
                pe.wait_ge(freed, now(freed, ONE["qkv" + m, l].at["steps"] + ONE["qkv" + m, l].steps))
                if ONE["attn" + m, l].at["pairs"] >= 1:
                    pe.wait_ge(omul, now(omul, ONE["attn" + m, l].at["pairs"]))
                for tt in range(nt):
                    turn(b, [tok[:, Q1 + tt * 512 + i * P:Q1 + tt * 512 + (i + 1) * P] for i in range(4)])
                    b += 1
                if m == "B":
                    for tt in range(4):
                        turn(b, [tok[:, K1 + tt * 512 + i * P:K1 + tt * 512 + (i + 1) * P] for i in range(4)])
                        b += 1
                else:
                    for c in range(2):
                        turn(b, [work[:, 1024 + tt * 256 + g * P:1024 + tt * 256 + (g + 1) * P]
                                     for g in range(2) for tt in (2 * c, 2 * c + 1)])
                        b += 1
                pe.wait_ge(turn_out, now(turn_out, b))
                attention(1, m, wctx, ONE["attn" + m, l], ONE["gate" + m, l].at["steps"] + 2)
                if m == "A":
                    qkv("B")
                    wout("A")
                if m == "B":
                    qkv("C")
                    wout("B")
                if m == "C":
                    wout("C")

        for kt in range(KT):
            sum_square(START2["norms"] - 1, 2, kt)

        pe.wait_ge(pads_zero, 4)
        with pe.Fori(0, LAYERS) as layer:
            Place.layer = layer

            def small(name):
                a, b = SMALL2[name]
                return sm2[:, a:b]

            def up(st, k):
                n0, s0 = st.at["panels"], st.at["steps"]
                with pe.Fori(0, FT // 2) as turn_:
                    Place.turn = turn_
                    for j in range(2):
                        n, s = n0 + j, s0 + j
                        take(s)
                        for c in range(2):
                            o = feature_major(n, step_banks(s)[0][:, c * T:(c + 1) * T], c,
                                              lambda b: (act_x(ahi, 2, b, 0, T), act_x(alo, 2, b, 0, T)),
                                              inputs=(x_split, 8 * k_x(k), 1) if j == 0 and c == 0 else None)
                        o.then_inc(tick, 1)
                    Place.turn = None

            def down(st, first_hidden, k=None):
                for blkno in range(FT * D // PW):
                    n, b = st.at["panels"] + blkno // NB, blkno % NB
                    j, kt = blkno // FT, blkno % FT
                    s = st.at["steps"] + j
                    need(n, b // 4)
                    if kt == 0:
                        take(s)
                    if j == 0:
                        pe.wait_ge(hid_split, now(hid_split, first_hidden + kt + 1))
                    xh, xl = (x[:, H2 + kt * T:H2 + (kt + 1) * T] for x in (ahi, alo))
                    for c in range(2):
                        wh, wl = wblock(n, b, c * P, (c + 1) * P)
                        o = mm3(step_banks(s)[0][:, c * T:(c + 1) * T], wh, wl, xh, xl, kt == 0 and c == 0, kt == FT - 1)
                    if b == NB - 1 or kt == FT - 1:
                        o.then_inc(tick, 1)
                    if k is not None and j and kt == FT - 1:
                        norm_sums(k, (2 * j - 2, 2 * j - 1))
                if k is not None:
                    norm_sums(k, (6, 7))

            norm_sums(TWO["norm1"].at["norms"], range(KT))
            up(TWO["up1"], TWO["norm1"].at["norms"])
            down(TWO["down1"], 0, TWO["norm2"].at["norms"])
            def tok_panels(name, width=PW, which=None):
                st = TWO[name]
                for j in range(st.panels) if which is None else (which,):
                    n, s = st.at["panels"] + j, st.at["steps"] + j
                    take(s)
                    inputs = 8 * k_x(TWO["norm2"].at["norms"]) if name == "cmp_kv" else None
                    for tt in range(TT):
                        o = token_major(n, step_banks(s)[0][:, tt * PW:tt * PW + width], 2, tt, width,
                                        inputs if tt == 0 else None)
                    o.then_inc(tick, 1)

            tok_panels("cmp_kv")
            pe.wait_ge(rs_ready, now(rs_ready, 2))
            for tt in range(TT):
                o = pe.matmul(banks[7][:, T + 2 * tt:T + 2 * tt + 2], rs[:, tt * P:(tt + 1) * P], ident[:, 0:2],
                              start=True, stop=True, skip_group_check=True)
            o.then_inc(rcol_turned, 1)
            tok_panels("nsa_g", 24)
            b = TWO["cmp_kv"].at["turns"]
            pe.wait_ge(roped, now(roped, ROPED2 + 1))
            for tt in range(TT):
                turn(b, [work[:, 1024 + tt * 512 + i * P:1024 + tt * 512 + (i + 1) * P] for i in range(4)])
                b += 1
            tok_panels("nsa_q")
            st = TWO["nsa_kv"]
            for j in range(2):
                tok_panels("nsa_kv", which=2 * j)
                n, s = st.at["panels"] + 2 * j + 1, st.at["steps"] + 2 * j + 1
                if j == 0:
                    pe.wait_ge(cm_dve, now(cm_dve, 2))
                take(s)
                xs = [x[:, H2 + j * 512:H2 + (j + 1) * 512].rearrange("p (n j) -> p n j", j=16) for x in (ahi, alo)]
                for q in range(16):
                    need(n, q // 8)
                    o = mm3(step_banks(s)[0][:, 0:32], slot_hi(n, q * P, (q + 1) * P), slot_lo(n, q * P, (q + 1) * P),
                            xs[0][:, :, q], xs[1][:, :, q], q == 0, q == 15)
                o.then_inc(tick, 1)
            tok_panels("moba_qkv", which=0)
            pe.wait_ge(freed, now(freed, st.at["steps"] + 4))
            pe.matmul(banks[7][0:32, 0:HD], glu[:, 0:32], small("w2k"), start=True, stop=True).then_inc(cm_pe, 1)
            tok_panels("moba_qkv", which=1)
            pe.wait_ge(roped, now(roped, ROPED2 + 2))
            b = TWO["turn_nsa"].at["turns"]
            for tt in range(TT):
                turn(b, [tok[:, Q2 + tt * 512 + i * P:Q2 + tt * 512 + (i + 1) * P] for i in range(4)])
                b += 1
            tok_panels("moba_qkv", which=2)
            for tt in range(TT):
                turn(b, [work[:, 1024 + tt * 512 + i * P:1024 + tt * 512 + (i + 1) * P] for i in range(4)])
                b += 1
            pe.wait_ge(cm_dve, now(cm_dve, 3))
            pe.transpose(banks[7][:, 0:P], kct[:, P:2 * P], ident).then_inc(cm_pe, 1)
            tok_panels("moba_qkv", which=3)
            pe.wait_ge(turn_out, now(turn_out, b))
            pe.wait_ge(cm_act, now(cm_act, 3))
            qv = qT[:, :].rearrange("p (a t) -> p a t", a=4)
            for qt in range(TT):
                for p in range(NPAIR):
                    o = pe.matmul(banks[7][:, qt * P + p * 32:qt * P + (p + 1) * 32], qv[:, p, qt * P:(qt + 1) * P],
                                  kcp[:, (p // 2) * 32:(p // 2 + 1) * 32], start=True, stop=True, skip_group_check=True)
            o.then_inc(cm_pe, 1)
            tok_panels("moba_qkv", which=4)
            pe.wait_ge(cm_dve, now(cm_dve, 4))
            pe.matmul(banks[7][:, 256:256 + HD], glu[:, 32:32 + P], small("w2v"), start=True, stop=True,
                      skip_group_check=True).then_inc(cm_pe, 1)
            tok_panels("moba_qkv", which=5)
            pe.wait_ge(cm_dve, now(cm_dve, 5))
            for qt in range(TT):
                o = pe.transpose(banks[7][:, qt * P:(qt + 1) * P], cmpw[:, qt * P:(qt + 1) * P], ident)
            o.then_inc(cm_pe, 1)
            pe.wait_ge(roped, now(roped, ROPED2 + 3))
            b = TWO["turn_moba"].at["turns"]
            for c in range(2):
                for tt in range(TT):
                    a = M2 + tt * 1536 + c * 512
                    turn(b, [tok[:, a + i * P:a + (i + 1) * P] for i in range(4)])
                    b += 1
            pe.wait_ge(turn_out, now(turn_out, b))
            pe.wait_ge(cm_act, now(cm_act, 5))
            attention(2, None, False, TWO["attn"], TWO["moba_qkv"].at["steps"] + 6)
            st = TWO["merge"]
            at = TWO["attn"]
            pe.wait_ge(usplit, now(usplit, at.at["pairs"] + at.pairs))
            for j in range(4):
                n, s = st.at["panels"] + j, st.at["steps"] + j
                take(s)
                for branch in range(2):
                    for e in range(2):
                        o = feature_major(n, step_banks(s)[branch][:, e * T:(e + 1) * T], e,
                                          lambda b: tuple(x[:, H2 + b * T:H2 + (b + 1) * T] for x in (ahi, alo)),
                                          range(4 * branch, 4 * branch + 4))
                o.then_inc(tick, 1)
            st = TWO["out"]
            for j in range(4):
                n, s = st.at["panels"] + j, st.at["steps"] + j
                take(s)
                for e in range(2):
                    o = feature_major(n, step_banks(s)[0][:, e * T:(e + 1) * T], e,
                                      lambda b: tuple(x[:, H2 + 2048 + b * T:H2 + 2048 + (b + 1) * T] for x in (ahi, alo)),
                                      inputs=(m_split, TWO["merge"].at["merges"], 2) if j == 0 and e == 0 else None)
                o.then_inc(tick, 1)
                if j:
                    norm_sums(TWO["norm3"].at["norms"], (2 * j - 2, 2 * j - 1))
            norm_sums(TWO["norm3"].at["norms"], (6, 7))
            up(TWO["up2"], TWO["norm3"].at["norms"])
            down(TWO["down2"], FT)
            Place.layer = None
        for kt in range(KT):
            sum_square(START2["norms"] + LAYERS * PER_LAYER["norms"], 2, kt)


def columns(w, c0, width=PW):
    k = w.shape[0] // P
    return w[:, c0:c0 + width].reshape(k, P, width).transpose(1, 0, 2).reshape(P, k * width)


def weight_stream(a):
    out = np.zeros((PANELS + SPARE, P, PAN), np.float32)
    n = 0

    def put(*parts):
        nonlocal n
        c = 0
        for x in parts:
            out[n, :, c:c + x.shape[1]] = x
            c += x.shape[1]
        n += 1

    hb = NH * HD
    at = {"A": (0, hb, 0), "B": (768, 1280, 1), "C": (2304, 2816, 2)}
    for l in range(LAYERS):
        w_in, w_out = a["w_in"][l], a["w_out"][l]
        gate0 = w_in.shape[1] - 3 * hb

        def qkv(m):
            for j in range(QKV_PANELS[m]):
                put(columns(w_in, at[m][0] + j * PW))

        def gate(m):
            for j in range(2):
                put(columns(w_in, gate0 + at[m][2] * hb + j * PW))

        def wout(m):
            for j in range(2):
                put(columns(w_out[at[m][2] * hb:(at[m][2] + 1) * hb], j * 2 * PW, 2 * PW))

        def ada(layer, first, count):
            for j in range(first, first + count):
                put(columns(a["ada_w"][layer], j * PW))

        def ada_next(part):
            if l == 0:
                ada(1, part * ADA_PANELS // 3, ADA_PANELS // 3)

        if l == 0:
            ada(0, 0, ADA_PANELS)
        qkv("A")
        gate("A")
        ada_next(0)
        qkv("B")
        wout("A")
        gate("B")
        ada_next(1)
        qkv("C")
        wout("B")
        gate("C")
        ada_next(2)
        wout("C")
    for l in range(LAYERS):
        w_in = a["w_in_2"][l]

        def ffn(which):
            wg, wu, wd = (a[f"ffn{which}_{x}_2"][l] for x in ("wg", "wu", "wd"))
            for j in range(FT):
                put(np.concatenate([wg[:, j * P:(j + 1) * P].reshape(KT, P, P), wu[:, j * P:(j + 1) * P].reshape(KT, P, P)], 2)
                    .transpose(1, 0, 2).reshape(P, PAN))
            blocks = np.concatenate([columns(wd, m * PW) for m in range(D // PW)], 1)
            for j in range(DOWN_PANELS):
                put(blocks[:, j * PAN:(j + 1) * PAN])

        ffn(1)
        kv0 = hb + 3 * NH
        put(columns(w_in, kv0))
        g = np.zeros((P, KT, PW), np.float32)
        g[:, :, 0:3 * NH] = w_in[:, hb:kv0].reshape(KT, P, 3 * NH).transpose(1, 0, 2)
        put(g.reshape(P, PAN))
        for j in range(2):
            put(columns(w_in, j * PW))
        for j, x in enumerate(("cmpk_w1_2", "cmpv_w1_2")):
            put(columns(w_in, kv0 + PW + j * PW))
            put(a[x][l].reshape(16, P, P).transpose(1, 0, 2).reshape(P, PAN))
        moba0 = kv0 + 6 * P
        for j in range(6):
            put(columns(w_in, moba0 + j * PW))
        ga0 = moba0 + 3 * hb
        for j in range(4):
            put(columns(w_in, ga0 + j * PW))
            put(columns(w_in, ga0 + D + j * PW))
        for j in range(4):
            put(columns(a["w_branch_nsa_2"][l], j * PW), columns(a["w_branch_moba_2"][l], j * PW))
        for j in range(4):
            put(columns(a["w_out_2"][l], j * PW))
        ffn(2)
    assert n == PANELS
    return out


def by_feature(v):
    return v.reshape(-1, P).T


def constants():
    c = np.zeros((P, NCONST), np.float32)

    def put(name, v, rows=P):
        a, b = CONST[name]
        c[0:rows, a:b] = v

    i, j = np.arange(P)[:, None], np.arange(P)[None, :]
    put("ident", np.eye(P))
    put("ones", np.full((P, P), 1.0 / D))
    put("tri_le", np.where(j <= i, 0.0, NEG))
    put("tri_ge", np.where(j >= i, 0.0, NEG))
    q = np.arange(T)
    col = q % GRID_W
    first = np.clip(col - NB_COLS // 2, 0, GRID_W - NB_COLS)
    near = (col[None, :] >= first[:, None]) & (col[None, :] < first[:, None] + NB_COLS)
    put("near", np.where(near, 0.0, NEG).reshape(TT, P, T).transpose(1, 0, 2).reshape(P, TT * T))
    theta = np.float32(10000.0)
    t = np.arange(T)
    nf = HD // 4
    fr = (theta ** (-np.arange(nf, dtype=np.float32) / np.float32(nf))).astype(np.float32)
    ang1 = np.concatenate([(t // GRID_W).astype(np.float32)[:, None] * fr, (t % GRID_W).astype(np.float32)[:, None] * fr], 1)
    inv = (theta ** (-np.arange(0, HD, 2, dtype=np.float32) / np.float32(HD))).astype(np.float32)
    ang2 = t.astype(np.float32)[:, None] * inv
    for k, ang in (("1", ang1), ("2", ang2)):
        for name, v in (("cos", np.cos(ang)), ("sin", np.sin(ang)), ("nsin", -np.sin(ang))):
            put(name + k, v.astype(np.float32).reshape(TT, P, HALF).transpose(1, 0, 2).reshape(P, TT * HALF))
    end = np.arange(NCMP) * 16 + 31
    angc = np.tile(end.astype(np.float32)[:, None] * inv, (2, 1))
    put("cosc", np.cos(angc), 32)
    put("sinc", np.sin(angc), 32)
    put("nsinc", -np.sin(angc), 32)
    ok = (end[None, :] <= q[:, None]) & (np.arange(NCMP) < NCMP - 1)[None, :]
    put("cmp_add", np.where(ok, 0.0, NEG).reshape(TT, P, NCMP).transpose(1, 0, 2).reshape(P, TT * NCMP))
    put("cmp_keep", ok.astype(np.float32).reshape(TT, P, NCMP).transpose(1, 0, 2).reshape(P, TT * NCMP))
    put("head_of", (np.arange(P)[:, None] // NCMP == np.arange(NH)[None, :]).astype(np.float32))
    sel = np.zeros((P, 2), np.float32)
    sel[[0, 2], 0] = 1.0
    sel[[1, 3], 1] = 1.0
    put("sel", sel)
    put("eps", np.full((P, 1), EPS))
    return c


def bias_tiles(rpb):
    t = np.arange(T)
    row, col = t // GRID_W, t % GRID_W
    dr = row[None, :] - row[:, None] + NB_ROWS - 1
    dc = np.clip(col[None, :] - col[:, None] + NB_COLS - 1, 0, 2 * NB_COLS - 2)
    tiles = rpb.reshape(LAYERS * NH, 2 * NB_ROWS - 1, 2 * NB_COLS - 1)[:, dr, dc]
    return tiles.reshape(LAYERS * NH, TT, P, T).transpose(0, 2, 1, 3).reshape(LAYERS * NH, P, TT * T)


def small_tiles(a):
    s1 = np.zeros((P, LAYERS, NSMALL1), np.float32)
    s2 = np.zeros((P, LAYERS, NSMALL2), np.float32)
    for l in range(LAYERS):
        for name, v in (("norm_w", by_feature(a["norm_w"][l])), ("ada_b", by_feature(a["ada_b"][l])),
                        ("qn", a["q_norm_a"][l][None]), ("kn", a["k_norm_a"][l][None]), ("sink", a["sink_c"][l][None])):
            s1[:, l, slice(*SMALL1[name])] = v
        for name, v in (("n1", by_feature(a["ffn1_norm_2"][l])), ("n2", by_feature(a["mix_norm_2"][l])),
                        ("n3", by_feature(a["ffn2_norm_2"][l])), ("w2k", a["cmpk_w2_2"][l]), ("w2v", a["cmpv_w2_2"][l])):
            s2[:, l, slice(*SMALL2[name])] = v
        for k, x in enumerate(("cmpk_pos_2", "cmpv_pos_2")):
            p0 = SMALL2["pos"][0] + 16 * k
            s2[:, l, p0:p0 + 16] = a[x][l].reshape(16, P).T
    g = np.zeros((P, NSMALLG), np.float32)
    g[:, 0:8], g[:, 8:16] = by_feature(a["final_norm_w"]), by_feature(a["final_norm_2"])
    g[:, 16:] = np.stack([by_feature(a["c"][0]), by_feature(a["c_ctx"])], 2).reshape(P, 2 * KT)
    return s1.reshape(P, -1), s2.reshape(P, -1), g


def kernel(**inputs):
    import concourse.bacc as bacc
    from concourse.bass_utils import run_bass_kernel_spmd

    a = {k: np.asarray(v) for k, v in inputs.items()}
    both = np.concatenate([a["x"][0].T.reshape(KT, P, T), a["ctx"][0].T.reshape(KT, P, T)], 2)
    s1, s2, sg = small_tiles(a)
    arrays = {"xin": both.transpose(1, 0, 2).reshape(P, -1), "small1": s1, "small2": s2, "smallg": sg,
              "consts": constants(), "rpb": bias_tiles(a["rpb_b"]), "weights": weight_stream(a)}
    arrays = {k: np.ascontiguousarray(v, dtype=np.float32) for k, v in arrays.items()}
    nc = bacc.Bacc("TRN2", target_bir_lowering=False, num_devices=1)
    t = {k: nc.dram_tensor(k, v.shape, F32, kind="ExternalInput").ap() for k, v in arrays.items()}
    out = nc.dram_tensor("out", (D, T), F32, kind="ExternalOutput").ap()
    with ExitStack() as ctx:
        program(nc, ctx, t["xin"], t["smallg"], t["small1"], t["small2"], t["consts"], t["rpb"], t["weights"], out)
    r = run_bass_kernel_spmd(nc, [arrays], core_ids=[0])
    return np.ascontiguousarray(r.results[0]["out"].T).reshape(1, T, D)
```
